# Optimizing a Trainium2 kernel written in Bass

```python
import math
import jax, jax.numpy as jnp
from jax import lax
import numpy as np

D_MODEL = 1024
BATCH = 1
SEQ = 256
DEPTH = 2

CHUNK = 64
EPS = 1e-6
F32 = jnp.float32

SC_WIDTH = 512
SC_KERNEL = 3
SSM_D_INNER = 1024
SSM_HEAD_DIM = 64
SSM_HEADS = SSM_D_INNER // SSM_HEAD_DIM
SSM_GROUPS = 4
SSM_STATE = 128
SSM_CONV = 4
SSM_CONV_DIM = SSM_D_INNER + 2 * SSM_GROUPS * SSM_STATE
GM_WIDTH = 512
GM_GROUPS = 4
GM_BLOCK = 128
GM_GROUP_DIM = GM_WIDTH // GM_GROUPS
POOL_WIDTH = 512
POOL_WINDOWS = (2, 4, 8, 16)
POOL_GROUP = POOL_WIDTH // len(POOL_WINDOWS)
N_BRANCH = 4
IN_A = 3 * SC_WIDTH
IN_B = SSM_D_INNER + SSM_CONV_DIM + SSM_HEADS
IN_C = 2 * GM_WIDTH
IN_D = POOL_WIDTH
IN_TOTAL = IN_A + IN_B + IN_C + IN_D
D_FF = 2816
N_EXPERTS = 8
TOP_K = 2
D_FF_EXPERT = 3584
N_DENSE = (DEPTH + 1) // 2
N_MOE = DEPTH // 2

kernel_name = "hybrid_parallel_gated_mixers_moe"

def rmsnorm(x, g):
    xf = x.astype(F32)
    y = xf * lax.rsqrt(jnp.mean(xf * xf, -1, keepdims=True) + EPS)
    return (y * g.astype(F32)).astype(x.dtype)

def causal_dwconv(x, w):
    k = w.shape[0]
    L = x.shape[1]
    xp = jnp.pad(x, ((0, 0), (k - 1, 0), (0, 0)))
    return sum(xp[:, i:i + L] * w[i] for i in range(k))

def short_conv_mixer(h, b_gate, c_gate, conv_w):
    return b_gate * causal_dwconv(c_gate * h, conv_w)

def segsum_exp(a):
    cs = jnp.cumsum(a, -1)
    diff = cs[..., :, None] - cs[..., None, :]
    l = a.shape[-1]
    mask = jnp.tril(jnp.ones((l, l), bool))
    return jnp.exp(jnp.where(mask, diff, -jnp.inf))

def ssd_scan(x, dt, a, bmat, cmat):
    bsz, L, H, P = x.shape
    G, N = bmat.shape[-2:]
    K = H // G
    nc = L // CHUNK
    xdt = (x.astype(F32) * dt[..., None]).reshape(bsz, nc, CHUNK, G, K, P)
    da = jnp.moveaxis((dt * a).reshape(bsz, nc, CHUNK, G, K), 2, -1)
    bc = bmat.astype(F32).reshape(bsz, nc, CHUNK, G, N)
    cc = cmat.astype(F32).reshape(bsz, nc, CHUNK, G, N)
    da_cs = jnp.cumsum(da, -1)
    cb = jnp.einsum("bclgn,bcsgn->bcgls", cc, bc)
    scores = cb[:, :, :, None] * segsum_exp(da)
    y_diag = jnp.einsum("bcgkls,bcsgkp->bclgkp", scores, xdt)
    decay_to_end = jnp.exp(da_cs[..., -1:] - da_cs)
    states = jnp.einsum("bclgn,bcgkl,bclgkp->bcgkpn", bc, decay_to_end, xdt)
    chunk_decay = jnp.exp(da_cs[..., -1])

    def step(h, inp):
        s_c, d_c = inp
        return h * d_c[..., None, None] + s_c, h

    h0 = jnp.zeros((bsz, G, K, P, N), F32)
    _, h_in = lax.scan(step, h0, (jnp.moveaxis(states, 1, 0), jnp.moveaxis(chunk_decay, 1, 0)))
    h_in = jnp.moveaxis(h_in, 0, 1)
    y_off = jnp.einsum("bclgn,bcgkpn,bcgkl->bclgkp", cc, h_in, jnp.exp(da_cs))
    return (y_diag + y_off).reshape(bsz, L, H, P)

def mamba2_mixer(z, xbc, dt_raw, conv_w, conv_b, dt_bias, a_log, d_skip, norm_g):
    bsz, L, _ = z.shape
    xbc = jax.nn.silu(causal_dwconv(xbc, conv_w) + conv_b)
    xs, bm, cm = jnp.split(xbc, [SSM_D_INNER, SSM_D_INNER + SSM_GROUPS * SSM_STATE], -1)
    xs = xs.reshape(bsz, L, SSM_HEADS, SSM_HEAD_DIM)
    bm = bm.reshape(bsz, L, SSM_GROUPS, SSM_STATE)
    cm = cm.reshape(bsz, L, SSM_GROUPS, SSM_STATE)
    dt = jax.nn.softplus(dt_raw.astype(F32) + dt_bias.astype(F32))
    a = -jnp.exp(a_log.astype(F32))
    y = ssd_scan(xs, dt, a, bm, cm) + xs.astype(F32) * d_skip.astype(F32)[:, None]
    y = y.reshape(bsz, L, SSM_D_INNER) * jax.nn.silu(z.astype(F32))
    yg = y.reshape(bsz, L, SSM_GROUPS, -1)
    yg = yg * lax.rsqrt(jnp.mean(yg * yg, -1, keepdims=True) + EPS)
    return (yg.reshape(bsz, L, SSM_D_INNER) * norm_g.astype(F32)).astype(z.dtype)

def gmlp_mixer(uv, ln_g, ln_b, w_s, s_bias):
    uv = jax.nn.gelu(uv)
    u, v = jnp.split(uv, 2, -1)
    vf = v.astype(F32)
    mu = jnp.mean(vf, -1, keepdims=True)
    var = jnp.mean(jnp.square(vf - mu), -1, keepdims=True)
    vf = (vf - mu) * lax.rsqrt(var + EPS) * ln_g.astype(F32) + ln_b.astype(F32)
    bsz, L, _ = v.shape
    nb = L // GM_BLOCK
    vf = vf.reshape(bsz, nb, GM_BLOCK, GM_GROUPS, GM_GROUP_DIM)
    mask = jnp.tril(jnp.ones((GM_BLOCK, GM_BLOCK), bool))
    ws = jnp.where(mask, w_s.astype(F32), 0.0)
    s = jnp.einsum("gts,bnsgc->bntgc", ws, vf) + s_bias.astype(F32).T[None, None, :, :, None]
    return u * s.reshape(bsz, L, GM_WIDTH).astype(u.dtype)

def pool_mixer(p, w_map, scale):
    bsz, L, _ = p.shape
    pf = p.astype(F32)
    count_base = jnp.arange(1, L + 1, dtype=F32)[None, :, None]
    outs = []
    for gi, w in enumerate(POOL_WINDOWS):
        xg = pf[..., gi * POOL_GROUP:(gi + 1) * POOL_GROUP]
        cs = jnp.cumsum(xg, 1)
        lag = jnp.pad(cs[:, :-w], ((0, 0), (w, 0), (0, 0)))
        outs.append((cs - lag) / jnp.minimum(count_base, w) - xg)
    pooled = jnp.stack(outs, 2)
    y = jnp.einsum("blgc,gcd->blgd", pooled, w_map.astype(F32)).reshape(bsz, L, POOL_WIDTH)
    return (y * scale.astype(F32)).astype(p.dtype)

def swiglu(x, wg, wu, wd):
    return (jax.nn.silu(x @ wg) * (x @ wu)) @ wd

def moe_ffn(x, router_w, wg, wu, wd):
    bsz, L, D = x.shape
    xt = x.reshape(-1, D)
    logits = (xt @ router_w).astype(F32)
    top_vals, top_idx = lax.top_k(logits, TOP_K)
    gates = jax.nn.softmax(top_vals, -1)
    combine = jnp.sum(jax.nn.one_hot(top_idx, N_EXPERTS, dtype=F32) * gates[..., None], 1)
    out = jnp.zeros(xt.shape, F32)
    for e in range(N_EXPERTS):
        out = out + combine[:, e:e + 1] * swiglu(xt, wg[e], wu[e], wd[e]).astype(F32)
    return out.astype(x.dtype).reshape(bsz, L, D)

def setup_inputs(seed: int = 0) -> dict:
    key = jax.random.key(seed)
    ks = iter(jax.random.split(key, 48))
    D = D_MODEL

    def nrm(shape, scale):
        return jax.random.normal(next(ks), shape, F32) * scale

    def gain(shape):
        return 1.0 + nrm(shape, 0.05)

    x = nrm((BATCH, SEQ, D), 1.0)
    norm1_g = gain((DEPTH, D))
    w_in = nrm((DEPTH, D, IN_TOTAL), D ** -0.5)
    w_gate = nrm((DEPTH, D, N_BRANCH * D), D ** -0.5)
    sc_conv_w = nrm((DEPTH, SC_KERNEL, SC_WIDTH), SC_KERNEL ** -0.5)
    ssm_conv_w = nrm((DEPTH, SSM_CONV, SSM_CONV_DIM), SSM_CONV ** -0.5)
    ssm_conv_b = nrm((DEPTH, SSM_CONV_DIM), 0.01)
    dt0 = jnp.exp(jax.random.uniform(next(ks), (DEPTH, SSM_HEADS), F32, math.log(1e-3), math.log(1e-1)))
    ssm_dt_bias = dt0 + jnp.log(-jnp.expm1(-dt0))
    ssm_a_log = jnp.log(jax.random.uniform(next(ks), (DEPTH, SSM_HEADS), F32, 1.0, 16.0))
    ssm_d = gain((DEPTH, SSM_HEADS))
    ssm_norm_g = gain((DEPTH, SSM_D_INNER))
    gm_ln_g = gain((DEPTH, GM_WIDTH))
    gm_ln_b = nrm((DEPTH, GM_WIDTH), 0.01)
    gm_ws = nrm((DEPTH, GM_GROUPS, GM_BLOCK, GM_BLOCK), GM_BLOCK ** -0.5)
    gm_bias = gain((DEPTH, GM_GROUPS, GM_BLOCK))
    pool_map = nrm((DEPTH, len(POOL_WINDOWS), POOL_GROUP, POOL_GROUP), POOL_GROUP ** -0.5)
    pool_scale = gain((DEPTH, POOL_WIDTH))
    w_br_a = nrm((DEPTH, SC_WIDTH, D), SC_WIDTH ** -0.5)
    w_br_b = nrm((DEPTH, SSM_D_INNER, D), SSM_D_INNER ** -0.5)
    w_br_c = nrm((DEPTH, GM_WIDTH, D), GM_WIDTH ** -0.5)
    w_br_d = nrm((DEPTH, POOL_WIDTH, D), POOL_WIDTH ** -0.5)
    w_out = nrm((DEPTH, D, D), D ** -0.5)
    norm2_g = gain((DEPTH, D))
    ffn_wg = nrm((N_DENSE, D, D_FF), D ** -0.5)
    ffn_wu = nrm((N_DENSE, D, D_FF), D ** -0.5)
    ffn_wd = nrm((N_DENSE, D_FF, D), D_FF ** -0.5)
    router_w = nrm((N_MOE, D, N_EXPERTS), D ** -0.5)
    moe_wg = nrm((N_MOE, N_EXPERTS, D, D_FF_EXPERT), D ** -0.5)
    moe_wu = nrm((N_MOE, N_EXPERTS, D, D_FF_EXPERT), D ** -0.5)
    moe_wd = nrm((N_MOE, N_EXPERTS, D_FF_EXPERT, D), D_FF_EXPERT ** -0.5)
    final_g = gain((D,))
    return {"x": x, "norm1_g": norm1_g, "w_in": w_in, "w_gate": w_gate,
            "sc_conv_w": sc_conv_w, "ssm_conv_w": ssm_conv_w, "ssm_conv_b": ssm_conv_b,
            "ssm_dt_bias": ssm_dt_bias, "ssm_a_log": ssm_a_log, "ssm_d": ssm_d,
            "ssm_norm_g": ssm_norm_g, "gm_ln_g": gm_ln_g, "gm_ln_b": gm_ln_b,
            "gm_ws": gm_ws, "gm_bias": gm_bias, "pool_map": pool_map,
            "pool_scale": pool_scale, "w_br_a": w_br_a, "w_br_b": w_br_b,
            "w_br_c": w_br_c, "w_br_d": w_br_d, "w_out": w_out, "norm2_g": norm2_g,
            "ffn_wg": ffn_wg, "ffn_wu": ffn_wu, "ffn_wd": ffn_wd, "router_w": router_w,
            "moe_wg": moe_wg, "moe_wu": moe_wu, "moe_wd": moe_wd, "final_g": final_g}

def reference(x, norm1_g, w_in, w_gate, sc_conv_w, ssm_conv_w, ssm_conv_b, ssm_dt_bias,
              ssm_a_log, ssm_d, ssm_norm_g, gm_ln_g, gm_ln_b, gm_ws, gm_bias, pool_map,
              pool_scale, w_br_a, w_br_b, w_br_c, w_br_d, w_out, norm2_g, ffn_wg, ffn_wu,
              ffn_wd, router_w, moe_wg, moe_wu, moe_wd, final_g):
    bsz, L, D = x.shape
    for layer in range(DEPTH):
        h = rmsnorm(x, norm1_g[layer])
        proj = h @ w_in[layer]
        pa, pb, pc, pd = jnp.split(proj, [IN_A, IN_A + IN_B, IN_A + IN_B + IN_C], -1)
        a_h, a_b, a_c = jnp.split(pa, 3, -1)
        y_a = short_conv_mixer(a_h, a_b, a_c, sc_conv_w[layer])
        z, xbc, dt_raw = jnp.split(pb, [SSM_D_INNER, SSM_D_INNER + SSM_CONV_DIM], -1)
        y_b = mamba2_mixer(z, xbc, dt_raw, ssm_conv_w[layer], ssm_conv_b[layer],
                           ssm_dt_bias[layer], ssm_a_log[layer], ssm_d[layer], ssm_norm_g[layer])
        y_c = gmlp_mixer(pc, gm_ln_g[layer], gm_ln_b[layer], gm_ws[layer], gm_bias[layer])
        y_d = pool_mixer(pd, pool_map[layer], pool_scale[layer])
        gates = jax.nn.sigmoid((h @ w_gate[layer]).astype(F32)).reshape(bsz, L, N_BRANCH, D)
        merged = (gates[:, :, 0] * (y_a @ w_br_a[layer]).astype(F32)
                  + gates[:, :, 1] * (y_b @ w_br_b[layer]).astype(F32)
                  + gates[:, :, 2] * (y_c @ w_br_c[layer]).astype(F32)
                  + gates[:, :, 3] * (y_d @ w_br_d[layer]).astype(F32))
        x = x + merged.astype(x.dtype) @ w_out[layer]
        h2 = rmsnorm(x, norm2_g[layer])
        idx = layer // 2
        if layer % 2 == 0:
            f = swiglu(h2, ffn_wg[idx], ffn_wu[idx], ffn_wd[idx])
        else:
            f = moe_ffn(h2, router_w[idx], moe_wg[idx], moe_wu[idx], moe_wd[idx])
        x = x + f
    return rmsnorm(x, final_g)


_drawn_inputs = setup_inputs


def setup_inputs(seed=0):
    import zlib

    import numpy as np

    out = dict(_drawn_inputs(seed))
    spreads = {}
    factors = {'ssm_conv_b': 3.347, 'gm_ln_g': 3.22, 'gm_ln_b': 8.0}
    for name, (base, spread) in spreads.items():
        noise = np.random.default_rng([zlib.crc32(name.encode()), seed]).standard_normal(out[name].shape)
        drawn = base * np.exp(spread * noise) if base else spread * noise
        out[name] = __import__('jax').numpy.asarray(drawn.astype(out[name].dtype))
    for name, factor in factors.items():
        out[name] = (out[name] * factor).astype(out[name].dtype)
    return out
```

```python
from contextlib import ExitStack

import numpy as np
import concourse.bass as bass
from concourse import mybir

D = 1024
SEQ = 256
DEPTH = 2
P = 128
KT = D // P
TT = SEQ // P
UNIT = 2048
BLOCKS = UNIT // P
EPS = 1e-6
HEADS, HEAD_DIM, GROUPS = 16, 64, 4
SC_BLOCKS, XBC_BLOCKS, Z_BLOCKS = 4, 16, 8
D_FF, D_FFE, EXPERTS = 2816, 3584, 8
SC_K, SSM_K = 3, 4
FF_STEPS = D_FF // (2 * P)
CHUNK_F = 512
CHUNKS = D_FFE // CHUNK_F
ITEM_UNITS = 6 * CHUNKS
MAX_ITEMS = EXPERTS + (2 * SEQ) // (P + 1)
RING = 3
AHEAD = 2

A_H, A_B, A_C, PD, GU, GV, ZB, XBC = 0, 4, 8, 12, 16, 20, 24, 32
N_PROJ = 48
IN_UNITS = N_PROJ // 2
GATE_UNITS, BR_UNITS = 8, 5
OUT_UNITS = 4
MIX_UNITS = IN_UNITS + 2 * (GATE_UNITS + BR_UNITS) + OUT_UNITS
FF_UNITS = 3 * FF_STEPS
Y_A, Y_B, Y_C, Y_D = 0, 4, 12, 16
BRANCHES = ((Y_A, 4), (Y_B, 8), (Y_C, 4), (Y_D, 4))


def columns(*parts):
    at, out = 0, {}
    for name, n in parts:
        out[name] = (at, at + n)
        at += n
    return out, at


PAR, N_PAR = columns(
    ("norm1", KT), ("norm2", KT), ("sc_w", SC_K * SC_BLOCKS), ("ssm_w", SSM_K * XBC_BLOCKS),
    ("ssm_b", XBC_BLOCKS), ("dt_bias", HEADS), ("a_log", HEADS), ("d_skip", 8), ("norm_g", 8),
    ("ln_g", 4), ("ln_b", 4), ("pool_scale", 4), ("w_dt", KT * HEADS), ("ws", 4 * P),
    ("gm_bias", 4 * P), ("pool_map", 4 * P))
CON, N_CON = columns(
    ("ident", P), ("upto", P), ("ones", P), ("after", P), ("iota", P), ("inv_count", 64),
    ("experts", EXPERTS), ("items", MAX_ITEMS * EXPERTS), ("eps", 1), ("final", KT), ("router", KT * EXPERTS))


def trunk(nc, x_in, par_in, con_in, mix_w, ff_w, moe_w, out):
    f32, f32r, i32, u32 = mybir.dt.float32, mybir.dt.float32r, mybir.dt.int32, mybir.dt.uint32
    ACT, ALU, AX = mybir.ActivationFunctionType, mybir.AluOpType, mybir.AxisListType
    ds = bass.ds
    ctx = ExitStack()
    with ctx:
        def sb(name, shape, dt=f32):
            return ctx.enter_context(nc.sbuf_tensor(name, shape, dt))

        def sem(name):
            return ctx.enter_context(nc.semaphore(name))

        raw = sb("weight_raw", [P, RING, UNIT])
        hi = sb("weight_hi", [P, RING, UNIT], f32r)
        lo = sb("weight_lo", [P, RING, UNIT], f32r)
        x = sb("x", [P, KT, SEQ])
        h_hi = sb("h_hi", [P, KT, SEQ], f32r)
        h_lo = sb("h_lo", [P, KT, SEQ], f32r)
        proj = sb("proj", [P, N_PROJ, SEQ])
        y_hi = sb("y_hi", [P, 20, SEQ], f32r)
        y_lo = sb("y_lo", [P, 20, SEQ], f32r)
        par = sb("par", [P, N_PAR])
        con = sb("con", [P, N_CON])
        scr = sb("scr", [P, 1024])
        small = sb("small", [P, 14, 2, HEADS])
        ints = sb("ints", [P, 32], i32)
        PS = ctx.enter_context(nc.psum_tensor("psum", [P, 8, 512], f32))

        def bank(b, n=1):
            return PS[:, b:b + n, :].rearrange("p b n -> p (b n)")

        def tiles(ap, n=SEQ):
            return ap.rearrange("p (t n) -> p t n", n=n)

        def flat(ap):
            return ap.rearrange("p t n -> p (t n)")

        def P_(name, i=0, n=None):
            a, b = PAR[name]
            return par[:, a + i:(b if n is None else a + i + n)]

        def C_(name, i=0, n=None):
            a, b = CON[name]
            return con[:, a + i:(b if n is None else a + i + n)]

        sq, h = proj[:, 0:8, :], proj[:, 8:16, :]
        xdt = flat(proj[:, 0:8, :]).rearrange("p (t c) -> p t c", t=TT)
        cb = flat(proj[:, 8:14, :]).rearrange("p (g l) -> p g l", g=GROUPS)
        seg_in0, seg_in1 = tiles(flat(proj[:, 14:18, :])), tiles(flat(proj[:, 18:20, :]), P)
        dec0 = tiles(flat(proj[:, 20:24, :]))
        dec1 = tiles(scr[:, 0:512], P)
        gates, merged = proj[:, 0:16, :], proj[:, 16:24, :]
        prod, pair = proj[:, 24:28, :], proj[:, 28:30, :]
        vT = flat(proj[:, 8:12, :]).rearrange("p (t c) -> p t c", t=TT)
        y_b = proj[:, 24:32, :]
        std = scr[:, 0:SEQ]
        ff_g, ff_h = flat(proj[:, 16:18, :]), flat(proj[:, 18:20, :])
        hid_hi, hid_lo = y_hi[:, 0:2, :], y_lo[:, 0:2, :]
        tok_hi, tok_lo = (flat(t[:, 0:8, :]).rearrange("p (t c) -> p t c", t=TT) for t in (y_hi, y_lo))
        xg_hi, xg_lo = (tiles(flat(t[:, 8:12, :]), P) for t in (y_hi, y_lo))
        hT_hi, hT_lo = (tiles(flat(t[:, 12:14, :]), P) for t in (y_hi, y_lo))
        pick = tiles(flat(y_hi[:, 14:15, :]), P)
        pick_g, pickT = tiles(flat(proj[:, 20:21, :]), P), proj[:, 21, :]
        y_sb = flat(proj[:, 22:26, :])
        route = flat(proj[:, 26:32, :])

        raw_landed = [sem(f"raw_landed{i}") for i in range(RING)]
        hi_done, lo_done, unit_used = sem("hi_done"), sem("lo_done"), sem("unit_used")
        in_loaded, par_loaded, stored = sem("in_loaded"), sem("par_loaded"), sem("stored")
        dve_order, act_order = sem("dve_order"), sem("act_order")
        S = {n: sem(n) for n in (
            "sq_done", "norm_sum", "std_done", "h_done", "h_hi_done", "h_lo_done", "dt_raw",
            "win_done", "gelu_done", "mean_sum", "dev_sq", "var_sum", "v_std", "v_norm", "v_T", "v_T_sb",
            "ws_masked", "s_done", "pooled", "pool_out", "a_sc", "a_exp", "dt_w", "dt_ln", "conv_acc", "conv_done",
            "xs_T", "xdt_done", "cb_ps", "cb_done", "seg_in", "seg_done", "dec_exp", "score_done", "y_ps",
            "y_done", "yb_sq", "yb_sum", "yb_std", "yf_done", "yhi_done", "ylo_done", "gate_done", "br_ps",
            "merge_done", "merged_all", "m_hi", "m_lo", "out_added", "silu_done", "mult_done", "hid_done",
            "acc_zero", "ff_added", "router_ps", "gap_exp", "gap_in", "sel_done", "pos_ps", "items_done",
            "tok_ps", "tok_hi_done", "tok_lo_done", "pick_done", "gather_ps", "pickT_ps", "pickT_done",
            "xg_hi_done", "xg_lo_done", "hT_ps", "hT_hi_done", "hT_lo_done", "esilu_done", "eh_done",
            "y_zero", "y_copied", "scatter_ps", "item_added", "final_done")}

        MOE_U = MIX_UNITS + FF_UNITS + MIX_UNITS

        def base_of(layer):
            return layer * (MIX_UNITS + FF_UNITS)

        block = ctx.enter_context(nc.Block())

        @block.sync
        def _(sp):
            def load(src, first, j, i=0):
                u = first + j + RING * i
                sp.wait_ge(lo_done, u + 1)
                sp.dma_start(raw[:, (first + j) % RING, :], src).then_inc(raw_landed[(first + j) % RING], 16)

            sp.dma_start(x[:], x_in).then_inc(in_loaded, 16)
            sp.dma_start(con[:], con_in).then_inc(in_loaded, 16)
            for layer in range(DEPTH):
                if layer:
                    sp.wait_ge(S["ylo_done"], 4 * layer)
                    sp.wait_ge(S["h_hi_done"], 2 * layer)
                sp.dma_start(par[:], par_in[layer]).then_inc(par_loaded, 16)
                with sp.Fori(0, MIX_UNITS // RING) as i:
                    for j in range(RING):
                        load(mix_w[layer, ds(i * RING + j, 1), :, :].rearrange("a p n -> (a p) n"), base_of(layer), j, i)
                if layer == 0:
                    with sp.Fori(0, FF_UNITS // RING) as i:
                        for j in range(RING):
                            load(ff_w[ds(i * RING + j, 1), :, :].rearrange("a p n -> (a p) n"), MIX_UNITS, j, i)
            sp.wait_ge(S["items_done"], 1)
            n_items = sp.value_load(ints[0:1, 31:32], min_val=1, max_val=MAX_ITEMS)
            with sp.Fori(0, n_items) as item:
                expert = sp.value_load(ints[0:1, ds(item, 1)], min_val=0, max_val=EXPERTS - 1)
                with sp.Fori(0, ITEM_UNITS // RING) as i:
                    for j in range(RING):
                        load(moe_w[ds(expert * ITEM_UNITS + i * RING + j, 1), :, :].rearrange("a p n -> (a p) n"),
                             MOE_U, j, i + item * (ITEM_UNITS // RING))
            for j in range(AHEAD):
                load(moe_w[j, :, :], MOE_U, j, n_items * (ITEM_UNITS // RING))
            sp.wait_ge(S["final_done"], 1)
            sp.dma_start(out, h).then_inc(stored, 16)
            sp.wait_ge(stored, 16)

        @block.scalar
        def _(act):
            A = nc.scalar.activation
            act_n = [0]

            def link(ins):
                act_n[0] += 1
                ins.then_inc(act_order, 1)
                act.wait_ge(act_order, act_n[0])

            def split(first, j, i=0):
                slot = (first + j) % RING
                u = first + j + RING * i
                act.wait_ge(raw_landed[slot], 16 * ((first + j) // RING + i + 1))
                act.wait_ge(unit_used, u + 1)
                A(hi[:, slot, :], raw[:, slot, :], ACT.Copy).then_inc(hi_done, 1)

            def used(u):
                act.wait_ge(unit_used, RING + u + 1)

            def norm(n, parts=True):
                act.wait_ge(S["norm_sum"], n + 1)
                A(std, bank(7)[:, 0:SEQ], ACT.Sqrt, bias=C_("eps"), scale=1.0 / D).then_inc(S["std_done"], 1)
                if parts:
                    act.wait_ge(S["h_done"], n + 1)
                    A(flat(h_hi[:]), flat(h), ACT.Copy).then_inc(S["h_hi_done"], 1)

            act.sem_inc(S["win_done"], RING)
            act.wait_ge(in_loaded, 32)
            for layer in range(DEPTH):
                b = base_of(layer)
                if layer == 0:
                    split(0, 0)
                    split(0, 1)
                norm(2 * layer)
                with act.Fori(0, IN_UNITS // RING) as i:
                    for j in range(RING):
                        split(b, j + AHEAD, i)
                        act.wait_ge(unit_used, RING + b + RING * i + j + 1)
                        A(proj[:, ds(i * (2 * RING) + 2 * j, 2), :].rearrange("p t n -> p (t n)"), bank(j), ACT.Copy)\
                            .then_inc(S["win_done"], 1)
                act.wait_ge(S["yf_done"], 4 * layer + 1)
                A(flat(y_hi[:, Y_A:Y_A + 4, :]), flat(proj[:, A_B:A_B + 4, :]), ACT.Copy).then_inc(S["yhi_done"], 1)
                act.wait_ge(S["win_done"], RING + IN_UNITS * (layer + 1))
                A(flat(proj[:, GU:GU + 8, :]), flat(proj[:, GU:GU + 8, :]), ACT.Gelu_apprx_tanh).then_inc(S["gelu_done"], 1)
                act.wait_ge(S["var_sum"], layer + 1)
                A(std, bank(7)[:, 0:SEQ], ACT.Sqrt, bias=C_("eps"), scale=1.0 / 512).then_inc(S["v_std"], 1)
                act.wait_ge(S["v_T"], layer + 1)
                A(flat(proj[:, 8:12, :]), bank(0, 2), ACT.Copy).then_inc(S["v_T_sb"], 1)
                act.wait_ge(S["yf_done"], 4 * layer + 2)
                A(flat(y_hi[:, Y_C:Y_C + 4, :]), flat(proj[:, GU:GU + 4, :]), ACT.Copy).then_inc(S["yhi_done"], 1)
                act.wait_ge(S["yf_done"], 4 * layer + 3)
                A(flat(y_hi[:, Y_D:Y_D + 4, :]), flat(proj[:, PD:PD + 4, :]), ACT.Copy).then_inc(S["yhi_done"], 1)
                if layer:
                    act.wait_ge(par_loaded, 16 * (layer + 1))
                act.wait_ge(S["a_sc"], layer + 1)
                A(small[:, 0, 0, :], P_("a_log"), ACT.Exp).then_inc(S["a_exp"], 1)
                A(small[:, 3, :, :], small[:, 2, :, :], ACT.Exp).then_inc(S["a_exp"], 1)
                act.wait_ge(S["dt_w"], layer + 1)
                A(small[:, 5, :, :], small[:, 4, :, :], ACT.Ln).then_inc(S["dt_ln"], 1)
                for t in range(XBC_BLOCKS):
                    act.wait_ge(S["conv_acc"], XBC_BLOCKS * layer + t + 1)
                    A(proj[:, XBC + t, :], scr[:, (t % 4) * SEQ:(t % 4 + 1) * SEQ], ACT.Silu, bias=P_("ssm_b", t, 1)).then_inc(S["conv_done"], 1)
                A(flat(proj[:, ZB:ZB + 8, :]), flat(proj[:, ZB:ZB + 8, :]), ACT.Silu).then_inc(S["conv_done"], 1)
                for g in range(GROUPS):
                    act.wait_ge(S["seg_done"], GROUPS * layer + g + 1)
                    if layer or g:
                        act.wait_ge(S["y_ps"], GROUPS * layer + g)
                    A(flat(dec0), bank(0, 2), ACT.Exp)
                    A(flat(dec1), bank(2), ACT.Exp).then_inc(S["dec_exp"], 1)
                act.wait_ge(S["yb_sum"], layer + 1)
                A(scr[:, 0:1024], bank(0, 2), ACT.Sqrt, bias=C_("eps"), scale=1.0 / 256).then_inc(S["yb_std"], 1)
                act.wait_ge(S["yf_done"], 4 * layer + 4)
                A(flat(y_hi[:, Y_B:Y_B + 8, :]), flat(y_b), ACT.Copy).then_inc(S["yhi_done"], 1)
                u = IN_UNITS
                for half in range(2):
                    if half:
                        act.wait_ge(S["merge_done"], 8 * layer + 4)
                    for q in range(GATE_UNITS):
                        split(b, u + AHEAD)
                        used(b + u)
                        A(flat(gates[:, 2 * q:2 * q + 2, :]), bank(q % 4), ACT.Sigmoid).then_inc(S["gate_done"], 1)
                        u += 1
                    for q in range(BR_UNITS):
                        split(b, u + AHEAD)
                        u += 1
                act.wait_ge(S["merged_all"], layer + 1)
                A(flat(h_hi[:]), flat(merged), ACT.Copy).then_inc(S["m_hi"], 1)
                for q in range(OUT_UNITS):
                    if layer == 0 or q < OUT_UNITS - AHEAD:
                        split(b, u + AHEAD)
                    u += 1
                norm(2 * layer + 1)
                if layer == 0:
                    f0 = MIX_UNITS
                    split(f0, AHEAD)
                    used(f0)
                    A(ff_g, bank(4), ACT.Silu).then_inc(S["silu_done"], 1)
                    split(f0, 1 + AHEAD)
                    with act.Fori(0, FF_STEPS - 1) as i:
                        split(f0, 2 + AHEAD, i)
                        act.wait_ge(unit_used, RING + f0 + 2 + RING * i + 1)
                        act.wait_ge(S["mult_done"], i + 1)
                        A(ff_g, bank(4), ACT.Silu).then_inc(S["silu_done"], 1)
                        split(f0, 3 + AHEAD, i)
                        split(f0, 4 + AHEAD, i)
                    split(f0, FF_UNITS - 1 + AHEAD)

            act.wait_ge(S["gap_in"], 1)
            A(small[:, 6, :, 0:1], small[:, 5, :, 0:1], ACT.Exp).then_inc(S["gap_exp"], 1)
            for t in range(TT):
                act.wait_ge(S["tok_ps"], t + 1)
                A(tok_hi[:, t, :], bank(2 * t, 2), ACT.Copy).then_inc(S["tok_hi_done"], 1)
            act.wait_ge(S["items_done"], 1)
            n_items = act.value_load(ints[0:1, 31:32], min_val=1, max_val=MAX_ITEMS)
            for j in range(AHEAD):
                split(MOE_U, j)
            with act.Fori(0, n_items) as item:
                it = item * (ITEM_UNITS // RING)
                act.wait_ge(S["pickT_ps"], item + 1)
                A(pickT, bank(6)[:, 0:SEQ], ACT.Copy).then_inc(S["pickT_done"], 1)
                act.wait_ge(S["gather_ps"], item + 1)
                A(flat(xg_hi), bank(0, 2), ACT.Copy).then_inc(S["xg_hi_done"], 1)
                split(MOE_U, 0 + AHEAD, it)
                split(MOE_U, 1 + AHEAD, it)
                act.wait_ge(unit_used, RING + MOE_U + 2 + item * ITEM_UNITS)
                A(ff_g, bank(4), ACT.Silu).then_inc(S["esilu_done"], 1)
                split(MOE_U, 2 + AHEAD, it)
                split(MOE_U, 3 + AHEAD, it)
                with act.Fori(0, CHUNKS - 1) as c:
                    split(MOE_U, 4 + AHEAD, it + 2 * c)
                    act.wait_ge(S["hT_ps"], item * CHUNKS + c + 1)
                    A(flat(hT_hi), bank(6), ACT.Copy).then_inc(S["hT_hi_done"], 1)
                    split(MOE_U, 5 + AHEAD, it + 2 * c)
                    act.wait_ge(unit_used, RING + MOE_U + 6 + item * ITEM_UNITS + 6 * c)
                    A(ff_g, bank(4), ACT.Silu).then_inc(S["esilu_done"], 1)
                    for j in range(6, 10):
                        split(MOE_U, j + AHEAD, it + 2 * c)
                act.wait_ge(S["hT_ps"], item * CHUNKS + CHUNKS)
                A(flat(hT_hi), bank(6), ACT.Copy).then_inc(S["hT_hi_done"], 1)
                split(MOE_U, ITEM_UNITS - 2 + AHEAD, it)
                split(MOE_U, ITEM_UNITS - 1 + AHEAD, it)
                act.wait_ge(unit_used, RING + MOE_U + ITEM_UNITS + item * ITEM_UNITS)
                A(y_sb, bank(0, 2), ACT.Copy).then_inc(S["y_copied"], 1)
            norm(2 * DEPTH, False)

        @block.vector
        def _(dve):
            V = nc.vector
            dve_n = [0]

            def link(ins):
                dve_n[0] += 1
                ins.then_inc(dve_order, 1)
                dve.wait_ge(dve_order, dve_n[0])

            def split(first, j, i=0):
                slot = (first + j) % RING
                dve.wait_ge(hi_done, first + j + RING * i + 1)
                V.tensor_tensor(lo[:, slot, :], raw[:, slot, :], hi[:, slot, :].bitcast(f32), ALU.subtract).then_inc(lo_done, 1)

            def rest(out_, whole, hi_part, signal):
                V.tensor_tensor(out_, whole, hi_part.bitcast(f32), ALU.subtract).then_inc(signal, 1)

            def norm(n, gain, parts=True):
                V.tensor_tensor(flat(sq), flat(x[:]), flat(x[:]), ALU.mult).then_inc(S["sq_done"], 1)
                dve.wait_ge(S["std_done"], n + 1)
                link(V.reciprocal(std, std))
                for k in range(KT):
                    last = V.scalar_tensor_tensor(h[:, k, :], x[:, k, :], gain[:, k:k + 1], std, ALU.mult, ALU.mult)
                if not parts:
                    last.then_inc(S["final_done"], 1)
                    return
                last.then_inc(S["h_done"], 1)
                dve.wait_ge(S["h_hi_done"], n + 1)
                rest(flat(h_lo[:]), flat(h), flat(h_hi[:]), S["h_lo_done"])

            dve.sem_inc(lo_done, RING)
            dve.wait_ge(in_loaded, 32)
            for layer in range(DEPTH):
                b = base_of(layer)
                dve.wait_ge(par_loaded, 16 * (layer + 1))
                if layer == 0:
                    split(0, 0)
                    split(0, 1)
                norm(2 * layer, P_("norm1"))
                with dve.Fori(0, IN_UNITS // RING) as i:
                    for j in range(RING):
                        split(b, j + AHEAD, i)

                dve.wait_ge(S["win_done"], RING + IN_UNITS * (layer + 1))
                a_h, a_b, a_c = (proj[:, n:n + 4, :] for n in (A_H, A_B, A_C))
                link(V.tensor_tensor(flat(a_h), flat(a_h), flat(a_c), ALU.mult))
                for t in range(SC_BLOCKS):
                    last = V.tensor_scalar(a_c[:, t, :], a_h[:, t, :], P_("sc_w", 2 * SC_BLOCKS + t, 1), None, ALU.mult)
                link(last)
                for tap in (1, 0):
                    s = SC_K - 1 - tap
                    for t in range(SC_BLOCKS):
                        last = V.scalar_tensor_tensor(a_c[:, t, s:], a_h[:, t, :SEQ - s], P_("sc_w", tap * SC_BLOCKS + t, 1),
                                                      a_c[:, t, s:], ALU.mult, ALU.add)
                    link(last)
                V.tensor_tensor(flat(a_b), flat(a_b), flat(a_c), ALU.mult).then_inc(S["yf_done"], 1)
                dve.wait_ge(S["yhi_done"], 4 * layer + 1)
                rest(flat(y_lo[:, Y_A:Y_A + 4, :]), flat(a_b), flat(y_hi[:, Y_A:Y_A + 4, :]), S["ylo_done"])

                u_, v_ = proj[:, GU:GU + 4, :], proj[:, GV:GV + 4, :]
                for g in range(4):
                    last = V.tensor_tensor(P_("ws", g * P, P), P_("ws", g * P, P), C_("upto"), ALU.mult)
                last.then_inc(S["ws_masked"], 1)
                dve.wait_ge(S["gelu_done"], layer + 1)
                dve.wait_ge(S["mean_sum"], layer + 1)
                mean = scr[:, SEQ:2 * SEQ]
                link(V.tensor_scalar(mean, bank(7)[:, 0:SEQ], 1.0 / 512, None, ALU.mult))
                for t in range(4):
                    last = V.tensor_tensor(v_[:, t, :], v_[:, t, :], mean, ALU.subtract)
                link(last)
                V.tensor_tensor(flat(proj[:, 0:4, :]), flat(v_), flat(v_), ALU.mult).then_inc(S["dev_sq"], 1)
                dve.wait_ge(S["v_std"], layer + 1)
                link(V.reciprocal(std, std))
                for t in range(4):
                    last = V.tensor_tensor(v_[:, t, :], v_[:, t, :], std, ALU.mult)
                link(last)
                for t in range(4):
                    last = V.tensor_scalar(v_[:, t, :], v_[:, t, :], P_("ln_g", t, 1), P_("ln_b", t, 1), ALU.mult, ALU.add)
                last.then_inc(S["v_norm"], 1)
                dve.wait_ge(S["s_done"], layer + 1)
                for t in range(TT):
                    last = V.tensor_tensor(v_[:, :, t * P:(t + 1) * P], tiles(bank(2, 2))[:, :, t * P:(t + 1) * P],
                                           tiles(P_("gm_bias"), P), ALU.add)
                link(last)
                V.tensor_tensor(flat(u_), flat(u_), flat(v_), ALU.mult).then_inc(S["yf_done"], 1)
                dve.wait_ge(S["yhi_done"], 4 * layer + 2)
                rest(flat(y_lo[:, Y_C:Y_C + 4, :]), flat(u_), flat(y_hi[:, Y_C:Y_C + 4, :]), S["ylo_done"])

                pd, s_a, s_b = proj[:, PD:PD + 4, :], proj[:, 0:4, :], proj[:, 4:8, :]
                src, dst = pd, s_a
                for step in range(4):
                    w = 1 << step
                    V.tensor_tensor(dst[:, step:, w:], src[:, step:, w:], src[:, step:, :SEQ - w], ALU.add)
                    link(V.tensor_copy(dst[:, step:, 0:w], src[:, step:, 0:w]))
                    V.scalar_tensor_tensor(proj[:, 8 + step, 16:], dst[:, step, 16:], 1.0 / (2 * w), pd[:, step, 16:], ALU.mult, ALU.subtract)
                    link(V.tensor_tensor(proj[:, 8 + step, 0:16], dst[:, step, 0:16], C_("inv_count", 16 * step, 16), ALU.mult))
                    V.tensor_tensor(proj[:, 8 + step, 0:16], proj[:, 8 + step, 0:16], pd[:, step, 0:16], ALU.subtract)\
                        .then_inc(S["pooled"], 1)
                    src, dst = (s_a, s_b) if step % 2 == 0 else (s_b, s_a)
                dve.wait_ge(S["pool_out"], layer + 1)
                for t in range(4):
                    last = V.tensor_scalar(pd[:, t, :], tiles(bank(0, 2))[:, t, :], P_("pool_scale", t, 1), None, ALU.mult)
                last.then_inc(S["yf_done"], 1)
                dve.wait_ge(S["yhi_done"], 4 * layer + 3)
                rest(flat(y_lo[:, Y_D:Y_D + 4, :]), flat(pd), flat(y_hi[:, Y_D:Y_D + 4, :]), S["ylo_done"])

                dve.wait_ge(S["dt_raw"], layer + 1)
                raw_dt = bank(6)[:, 0:TT * HEADS].rearrange("p (t n) -> p t n", t=TT)
                for t in range(TT):
                    last = V.tensor_tensor(small[:, 1, t, :], raw_dt[:, t, :], P_("dt_bias"), ALU.add)
                link(last)
                link(V.tensor_scalar(small[:, 2], small[:, 1], -1.0, None, ALU.mult))
                V.tensor_tensor(small[:, 2], small[:, 2], small[:, 1], ALU.min).then_inc(S["a_sc"], 1)
                dve.wait_ge(S["a_exp"], 2 * layer + 2)
                V.tensor_scalar(small[:, 4], small[:, 3], 1.0, None, ALU.add).then_inc(S["dt_w"], 1)
                dve.wait_ge(S["dt_w"], layer + 1)
                link(V.scalar_tensor_tensor(small[:, 8], small[:, 4], -1.0, small[:, 3], ALU.add, ALU.subtract))
                link(V.reciprocal(small[:, 9], small[:, 4]))
                link(V.tensor_tensor(small[:, 8], small[:, 8], small[:, 9], ALU.mult))
                dve.wait_ge(S["dt_ln"], layer + 1)
                link(V.tensor_tensor(small[:, 5], small[:, 5], small[:, 8], ALU.subtract))
                link(V.scalar_tensor_tensor(small[:, 6], small[:, 1], 0.0, small[:, 5], ALU.max, ALU.add))
                for t in range(TT):
                    last = V.scalar_tensor_tensor(small[:, 7, t, :], small[:, 6, t, :], -1.0, small[:, 0, 0, :], ALU.mult, ALU.mult)
                link(last)
                for t in range(XBC_BLOCKS):
                    acc = scr[:, (t % 4) * SEQ:(t % 4 + 1) * SEQ]
                    raw_t = proj[:, XBC + t, :]
                    if t >= 4:
                        dve.wait_ge(S["conv_done"], (XBC_BLOCKS + 1) * layer + t - 3)
                    link(V.tensor_scalar(acc, raw_t, P_("ssm_w", 3 * XBC_BLOCKS + t, 1), None, ALU.mult))
                    for tap in (2, 1, 0):
                        s = SSM_K - 1 - tap
                        last = V.scalar_tensor_tensor(acc[:, s:], raw_t[:, :SEQ - s], P_("ssm_w", tap * XBC_BLOCKS + t, 1),
                                                      acc[:, s:], ALU.mult, ALU.add)
                        if tap:
                            link(last)
                    last.then_inc(S["conv_acc"], 1)
                for t in range(TT):
                    dve.wait_ge(S["xs_T"], TT * layer + t + 1)
                    V.tensor_tensor(xdt[:, t, :].rearrange("p (h n) -> p h n", h=HEADS),
                                    bank(2 * t, 2).rearrange("p (h n) -> p h n", h=HEADS),
                                    small[:, 6, t, :].rearrange("p (h n) -> p h n", n=1).broadcast_to([P, HEADS, HEAD_DIM]),
                                    ALU.mult).then_inc(S["xdt_done"], 1)
                for g in range(GROUPS):
                    dve.wait_ge(S["cb_ps"], GROUPS * layer + g + 1)
                    ps = bank(4 + g % 2)
                    V.tensor_tensor(cb[:, g, 0:P], ps[:, 0:P], C_("upto"), ALU.mult)
                    V.tensor_copy(cb[:, g, P:2 * P], ps[:, P:2 * P])
                    V.tensor_tensor(cb[:, g, 2 * P:], ps[:, 2 * P:3 * P], C_("upto"), ALU.mult).then_inc(S["cb_done"], 1)
                dve.wait_ge(S["cb_done"], GROUPS * (layer + 1))
                up_and_ones = C_("upto", 0, 2 * P)
                for g in range(GROUPS):
                    if layer or g:
                        dve.wait_ge(S["seg_done"], GROUPS * layer + g)
                    for n in range(4):
                        head = 4 * g + n
                        V.tensor_scalar(seg_in0[:, n, :], up_and_ones, small[:, 7, 0, head:head + 1], None, ALU.mult)
                        last = V.tensor_scalar(seg_in1[:, n, :], C_("upto"), small[:, 7, 1, head:head + 1], None, ALU.mult)
                    last.then_inc(S["seg_in"], 1)
                    dve.wait_ge(S["dec_exp"], GROUPS * layer + g + 1)
                    for n in range(4):
                        V.tensor_tensor(dec0[:, n, :], dec0[:, n, :], cb[:, g, 0:SEQ], ALU.mult)
                        last = V.tensor_tensor(dec1[:, n, :], dec1[:, n, :], cb[:, g, SEQ:], ALU.mult)
                    last.then_inc(S["score_done"], 1)
                    dve.wait_ge(S["y_ps"], GROUPS * layer + g + 1)
                    if g == 0:
                        dve.wait_ge(S["conv_done"], (XBC_BLOCKS + 1) * (layer + 1))
                    for t in range(2):
                        c = 2 * g + t
                        last = V.scalar_tensor_tensor(proj[:, XBC + c, :], proj[:, XBC + c, :], P_("d_skip", c, 1),
                                                      tiles(bank(3))[:, t, :], ALU.mult, ALU.add)
                    last.then_inc(S["y_done"], 1)
                dve.wait_ge(S["y_done"], GROUPS * (layer + 1))
                link(V.tensor_tensor(flat(y_b), flat(y_b), flat(proj[:, XBC:XBC + 8, :]), ALU.mult))
                V.tensor_tensor(flat(proj[:, XBC + 8:XBC + 16, :]), flat(y_b), flat(y_b), ALU.mult).then_inc(S["yb_sq"], 1)
                dve.wait_ge(S["yb_std"], layer + 1)
                link(V.reciprocal(scr[:, 0:1024], scr[:, 0:1024]))
                for c in range(8):
                    last = V.scalar_tensor_tensor(y_b[:, c, :], y_b[:, c, :], P_("norm_g", c, 1),
                                                  scr[:, (c // 2) * SEQ:(c // 2 + 1) * SEQ], ALU.mult, ALU.mult)
                last.then_inc(S["yf_done"], 1)
                dve.wait_ge(S["yhi_done"], 4 * layer + 4)
                rest(flat(y_lo[:, Y_B:Y_B + 8, :]), flat(y_b), flat(y_hi[:, Y_B:Y_B + 8, :]), S["ylo_done"])

                u = IN_UNITS
                for half in range(2):
                    for q in range(GATE_UNITS):
                        split(b, u + AHEAD)
                        u += 1
                    tile = 0
                    for q in range(BR_UNITS):
                        split(b, u + AHEAD)
                        u += 1
                        while tile < 4 and 20 * (tile + 1) <= BLOCKS * (q + 1):
                            if tile < 3:
                                dve.wait_ge(S["br_ps"], 3 * (2 * layer + half) + tile + 1)
                            else:
                                dve.wait_ge(unit_used, RING + b + u)
                            dve.wait_ge(S["gate_done"], 16 * layer + GATE_UNITS * (half + 1))
                            link(V.tensor_tensor(flat(prod), flat(gates[:, 4 * tile:4 * tile + 4, :]), bank(4 + 2 * (tile % 2), 2), ALU.mult))
                            link(V.tensor_tensor(flat(pair), flat(prod[:, 0:2, :]), flat(prod[:, 2:4, :]), ALU.add))
                            V.tensor_tensor(merged[:, 4 * half + tile, :], pair[:, 0, :], pair[:, 1, :], ALU.add).then_inc(S["merge_done"], 1)
                            tile += 1
                dve.wait_ge(S["merge_done"], 8 * (layer + 1))
                V.engine_nop().then_inc(S["merged_all"], 1)
                dve.wait_ge(S["m_hi"], layer + 1)
                rest(flat(h_lo[:]), flat(merged), flat(h_hi[:]), S["m_lo"])
                for q in range(OUT_UNITS):
                    if layer == 0 or q < OUT_UNITS - AHEAD:
                        split(b, u + AHEAD)
                    dve.wait_ge(unit_used, RING + b + u + 1)
                    link(V.tensor_tensor(flat(x[:, 2 * q:2 * q + 2, :]), flat(x[:, 2 * q:2 * q + 2, :]), bank(q), ALU.add))
                    u += 1
                norm(2 * layer + 1, P_("norm2"))
                if layer == 0:
                    f0 = MIX_UNITS
                    V.memset(bank(0, 4), 0.0).then_inc(S["acc_zero"], 1)

                    def hidden(i):
                        V.tensor_tensor(ff_h, ff_g, bank(5), ALU.mult).then_inc(S["mult_done"], 1)
                        dve.wait_ge(S["mult_done"], i + 1)
                        V.tensor_copy(flat(hid_hi), ff_h).then_inc(S["hid_done"], 1)
                        dve.wait_ge(S["hid_done"], 2 * i + 1)
                        rest(flat(hid_lo), ff_h, flat(hid_hi), S["hid_done"])

                    split(f0, AHEAD)
                    split(f0, 1 + AHEAD)
                    dve.wait_ge(S["silu_done"], 1)
                    dve.wait_ge(unit_used, RING + f0 + 2)
                    hidden(0)
                    with dve.Fori(0, FF_STEPS - 1) as i:
                        for j in range(RING):
                            split(f0, 2 + j + AHEAD, i)
                        dve.wait_ge(S["silu_done"], i + 2)
                        dve.wait_ge(unit_used, RING + f0 + 2 + RING * i + 3)
                        hidden(i + 1)
                    split(f0, FF_UNITS - 1 + AHEAD)
                    dve.wait_ge(unit_used, RING + f0 + FF_UNITS)
                    link(V.tensor_tensor(flat(x[:]), flat(x[:]), bank(0, 4), ALU.add))

            NT = EXPERTS
            at = [0]

            def table(*shape):
                n = int(np.prod(shape))
                ap = route[:, at[0]:at[0] + n]
                at[0] += n
                return ap.rearrange("p (a b) -> p a b", a=shape[0]) if len(shape) == 2 else ap

            logit, top, comb, chosen, slot = (table(TT, NT) for _ in range(5))
            place_f, g1, g2 = table(TT, NT), table(TT, 1), table(TT, 1)
            first_e, other_e = table(TT, NT), table(TT, NT)
            count, blocks_e, cum = table(NT), table(NT), table(NT)
            expert_f, second = table(MAX_ITEMS), table(MAX_ITEMS)
            grid, one_hot, pickv = table(MAX_ITEMS, NT), table(MAX_ITEMS, NT), table(MAX_ITEMS, NT)
            item_slot, item_gate = table(TT, MAX_ITEMS), table(TT, MAX_ITEMS)
            assert at[0] <= 1536
            place = ints[:, 0:16].bitcast(u32).rearrange("p (t n) -> p t n", t=TT)
            dve.wait_ge(S["router_ps"], 1)
            link(V.tensor_copy(logit, bank(6)[:, 0:TT * NT].rearrange("p (t n) -> p t n", t=TT)))
            for t in range(TT):
                last = V.max(top[:, t, :], logit[:, t, :])
            link(last)
            V.tensor_tensor(small[:, 5, :, 0:1], top[:, :, 1:2], top[:, :, 0:1], ALU.subtract).then_inc(S["gap_in"], 1)
            for t in range(TT):
                last = V.max_index(place[:, t, :], top[:, t, :], logit[:, t, :])
            link(last)
            link(V.tensor_copy(place_f, place))
            dve.wait_ge(S["gap_exp"], 1)
            link(V.tensor_scalar(g2, small[:, 6, :, 0:1], 1.0, None, ALU.add))
            link(V.reciprocal(g1, g2))
            link(V.tensor_tensor(g2, g1, small[:, 6, :, 0:1], ALU.mult))
            for t in range(TT):
                V.tensor_scalar(first_e[:, t, :], C_("experts"), place_f[:, t, 0:1], None, ALU.is_equal)
                last = V.tensor_scalar(other_e[:, t, :], C_("experts"), place_f[:, t, 1:2], None, ALU.is_equal)
            link(last)
            V.tensor_tensor(chosen, first_e, other_e, ALU.add).then_inc(S["sel_done"], 1)
            for t in range(TT):
                last = V.tensor_scalar(comb[:, t, :], first_e[:, t, :], g1[:, t, :], None, ALU.mult)
            link(last)
            for t in range(TT):
                last = V.scalar_tensor_tensor(comb[:, t, :], other_e[:, t, :], g2[:, t, :], comb[:, t, :], ALU.mult, ALU.add)
            link(last)
            dve.wait_ge(S["pos_ps"], 1)
            link(V.tensor_copy(count, bank(6)[:, 2 * NT:3 * NT]))
            link(V.tensor_tensor(slot, bank(6)[:, 0:2 * NT].rearrange("p (t n) -> p t n", t=TT), chosen, ALU.mult))
            link(V.tensor_scalar(slot, slot, -1.0, None, ALU.add))
            link(V.tensor_scalar(cum, count, float(P) + 0.5, None, ALU.is_gt))
            link(V.scalar_tensor_tensor(blocks_e, count, 0.5, cum, ALU.is_gt, ALU.add))
            link(V.tensor_tensor_scan(cum, C_("ones", 0, NT), blocks_e, 0.0, ALU.mult, ALU.add))
            items = C_("items").rearrange("p (a b) -> p a b", a=MAX_ITEMS)
            link(V.tensor_tensor(grid, cum.rearrange("p (a b) -> p a b", a=1).broadcast_to([P, MAX_ITEMS, NT]), items, ALU.is_le))
            link(V.tensor_reduce(expert_f, grid, AX.X, ALU.add))
            link(V.memset(second, 0.0))
            link(V.tensor_tensor(second[:, 1:], expert_f[:, 1:], expert_f[:, :MAX_ITEMS - 1], ALU.is_equal))
            experts = C_("experts")
            for i in range(MAX_ITEMS):
                last = V.tensor_scalar(one_hot[:, i, :], experts, expert_f[:, i:i + 1], None, ALU.is_equal)
            link(last)
            for t in range(TT):
                for dst, of in ((item_slot, slot), (item_gate, comb)):
                    link(V.tensor_tensor(pickv, one_hot, of[:, t:t + 1, :].broadcast_to([P, MAX_ITEMS, NT]), ALU.mult))
                    link(V.tensor_reduce(dst[:, t, :], pickv, AX.X, ALU.add))
                link(V.scalar_tensor_tensor(item_slot[:, t, :], second, -float(P), item_slot[:, t, :], ALU.mult, ALU.add))
            V.tensor_copy(ints[:, 0:MAX_ITEMS], expert_f)
            V.tensor_copy(ints[:, 31:32], cum[:, NT - 1:NT]).then_inc(S["items_done"], 1)
            for t in range(TT):
                dve.wait_ge(S["tok_hi_done"], t + 1)
                rest(tok_lo[:, t, :], bank(2 * t, 2), tok_hi[:, t, :], S["tok_lo_done"])
            dve.wait_ge(S["items_done"], 1)
            dve.sem_inc(S["item_added"], 1)
            n_items = dve.value_load(ints[0:1, 31:32], min_val=1, max_val=MAX_ITEMS)
            for j in range(AHEAD):
                split(MOE_U, j)
            with dve.Fori(0, n_items) as item:
                it = item * (ITEM_UNITS // RING)
                for t in range(TT):
                    V.tensor_scalar(pick[:, t, :], C_("iota"), item_slot[:, t, ds(item, 1)], None, ALU.is_equal)
                    last = V.tensor_scalar(pick_g[:, t, :], C_("iota"), item_slot[:, t, ds(item, 1)],
                                           item_gate[:, t, ds(item, 1)], ALU.is_equal, ALU.mult)
                last.then_inc(S["pick_done"], 1)
                dve.wait_ge(S["gather_ps"], item + 1)
                V.tensor_copy(flat(xg_lo), bank(2, 2)).then_inc(S["xg_lo_done"], 1)
                dve.wait_ge(S["xg_hi_done"], item + 1)
                V.memset(bank(0, 2), 0.0).then_inc(S["y_zero"], 1)
                for j in range(4):
                    split(MOE_U, j + AHEAD, it)
                dve.wait_ge(S["esilu_done"], item * CHUNKS + 1)
                dve.wait_ge(unit_used, RING + MOE_U + 4 + item * ITEM_UNITS)
                V.tensor_tensor(ff_h, ff_g, bank(5), ALU.mult).then_inc(S["eh_done"], 1)
                with dve.Fori(0, CHUNKS - 1) as c:
                    split(MOE_U, 4 + AHEAD, it + 2 * c)
                    dve.wait_ge(S["hT_hi_done"], item * CHUNKS + c + 1)
                    rest(flat(hT_lo), bank(6), flat(hT_hi), S["hT_lo_done"])
                    for j in range(5, 8):
                        split(MOE_U, j + AHEAD, it + 2 * c)
                    dve.wait_ge(S["esilu_done"], item * CHUNKS + c + 2)
                    dve.wait_ge(unit_used, RING + MOE_U + 8 + item * ITEM_UNITS + 6 * c)
                    V.tensor_tensor(ff_h, ff_g, bank(5), ALU.mult).then_inc(S["eh_done"], 1)
                    for j in range(8, 10):
                        split(MOE_U, j + AHEAD, it + 2 * c)
                dve.wait_ge(S["hT_hi_done"], item * CHUNKS + CHUNKS)
                rest(flat(hT_lo), bank(6), flat(hT_hi), S["hT_lo_done"])
                split(MOE_U, ITEM_UNITS - 2 + AHEAD, it)
                split(MOE_U, ITEM_UNITS - 1 + AHEAD, it)
                dve.wait_ge(S["scatter_ps"], item + 1)
                dve.wait_ge(S["item_added"], item + 1)
                V.tensor_tensor(flat(x[:]), flat(x[:]), bank(2, 4), ALU.add).then_inc(S["item_added"], 1)
            dve.wait_ge(S["item_added"], n_items + 1)
            norm(2 * DEPTH, C_("final"), False)

        @block.tensor
        def _(pe):
            def mm(o, a, b_, start, stop, **k):
                return nc.tensor.matmul(o, a, b_, start=start, stop=stop, skip_group_check=True, **k)

            def product(o, slot, blk, a_hi, a_lo, start, stop):
                w = slice(blk * P, (blk + 1) * P)
                mm(o, hi[:, slot, w], a_hi, start, False)
                mm(o, hi[:, slot, w], a_lo, False, False)
                return mm(o, lo[:, slot, w], a_hi, False, stop)

            def tile_pair(b_out, first, j):
                for t in range(2):
                    for k in range(KT):
                        last = product(bank(b_out)[:, t * SEQ:(t + 1) * SEQ], (first + j) % RING, KT * t + k,
                                       h_hi[:, k, :], h_lo[:, k, :], k == 0, k == KT - 1)
                last.then_inc(unit_used, 1)

            def split_is(u):
                pe.wait_ge(lo_done, RING + u + 1)

            def norm(n):
                pe.wait_ge(S["sq_done"], n + 1)
                for k in range(KT):
                    last = mm(bank(7)[:, 0:SEQ], C_("ones"), sq[:, k, :], k == 0, k == KT - 1)
                last.then_inc(S["norm_sum"], 1)

            pe.sem_inc(unit_used, RING)
            pe.wait_ge(in_loaded, 32)
            for layer in range(DEPTH):
                b = base_of(layer)
                norm(2 * layer)
                pe.wait_ge(S["h_done"], 2 * layer + 1)
                pe.wait_ge(par_loaded, 16 * (layer + 1))
                w_dt = P_("w_dt").rearrange("p (k n) -> p k n", k=KT)
                for t in range(TT):
                    for k in range(KT):
                        last = mm(bank(6)[:, t * HEADS:(t + 1) * HEADS], h[:, k, t * P:(t + 1) * P], w_dt[:, k, :], k == 0, k == KT - 1)
                last.then_inc(S["dt_raw"], 1)
                pe.wait_ge(S["h_lo_done"], 2 * layer + 1)
                with pe.Fori(0, IN_UNITS // RING) as i:
                    for j in range(RING):
                        split_is(b + RING * i + j)
                        pe.wait_ge(S["win_done"], IN_UNITS * layer + RING * i + j + 1)
                        tile_pair(j, b, j)
                v_ = proj[:, GV:GV + 4, :]
                pe.wait_ge(S["gelu_done"], layer + 1)
                for k in range(4):
                    last = mm(bank(7)[:, 0:SEQ], C_("ones"), v_[:, k, :], k == 0, k == 3)
                last.then_inc(S["mean_sum"], 1)
                pe.wait_ge(S["dev_sq"], layer + 1)
                for k in range(4):
                    last = mm(bank(7)[:, 0:SEQ], C_("ones"), proj[:, k, :], k == 0, k == 3)
                last.then_inc(S["var_sum"], 1)
                pe.wait_ge(S["v_norm"], layer + 1)
                for t in range(TT):
                    for g in range(4):
                        last = nc.tensor.transpose(bank(t)[:, g * P:(g + 1) * P], v_[:, g, t * P:(t + 1) * P], C_("ident"))
                last.then_inc(S["v_T"], 1)
                pe.wait_ge(S["v_T_sb"], layer + 1)
                pe.wait_ge(S["ws_masked"], layer + 1)
                for g in range(4):
                    for t in range(TT):
                        at = (g % 2) * SEQ + t * P
                        last = mm(bank(2 + g // 2)[:, at:at + P], vT[:, t, g * P:(g + 1) * P], P_("ws", g * P, P), True, True)
                last.then_inc(S["s_done"], 1)
                pe.wait_ge(S["pooled"], 4 * (layer + 1))
                for g in range(4):
                    last = mm(bank(g // 2)[:, (g % 2) * SEQ:(g % 2 + 1) * SEQ], P_("pool_map", g * P, P), proj[:, 8 + g, :], True, True)
                last.then_inc(S["pool_out"], 1)
                pe.wait_ge(S["yf_done"], 4 * layer + 3)
                pe.wait_ge(S["conv_done"], (XBC_BLOCKS + 1) * layer + 8)
                for t in range(TT):
                    for c in range(8):
                        last = nc.tensor.transpose(bank(2 * t + c // 4)[:, (c % 4) * P:(c % 4 + 1) * P],
                                                   proj[:, XBC + c, t * P:(t + 1) * P], C_("ident"))
                    last.then_inc(S["xs_T"], 1)
                pe.wait_ge(S["conv_done"], (XBC_BLOCKS + 1) * layer + XBC_BLOCKS)
                for g in range(GROUPS):
                    if g >= 2:
                        pe.wait_ge(S["cb_done"], GROUPS * layer + g - 1)
                    b_t, c_t = proj[:, XBC + 8 + g, :], proj[:, XBC + 12 + g, :]
                    mm(bank(4 + g % 2)[:, 0:SEQ], b_t[:, 0:P], c_t, True, True)
                    mm(bank(4 + g % 2)[:, SEQ:SEQ + P], b_t[:, P:], c_t[:, P:], True, True).then_inc(S["cb_ps"], 1)
                pe.wait_ge(S["xdt_done"], TT * (layer + 1))
                for g in range(GROUPS):
                    pe.wait_ge(S["seg_in"], GROUPS * layer + g + 1)
                    for n in range(2):
                        mm(bank(n), C_("after"), flat(seg_in0[:, 2 * n:2 * n + 2, :]), True, False)
                        mm(tiles(bank(n))[:, :, P:], C_("ones"), seg_in1[:, 2 * n:2 * n + 2, :], False, True)
                    mm(bank(2), C_("after"), flat(seg_in1), True, True).then_inc(S["seg_done"], 1)
                    pe.wait_ge(S["score_done"], GROUPS * layer + g + 1)
                    if layer or g:
                        pe.wait_ge(S["y_done"], GROUPS * layer + g)
                    for n in range(4):
                        head = 4 * g + n
                        o = bank(3)[HEAD_DIM * (n % 2):HEAD_DIM * (n % 2 + 1), (n // 2) * SEQ:(n // 2 + 1) * SEQ]
                        heads = slice(head * HEAD_DIM, (head + 1) * HEAD_DIM)
                        mm(o, xdt[:, 0, heads], dec0[:, n, :], True, False)
                        last = mm(o[:, P:], xdt[:, 1, heads], dec1[:, n, :], False, True)
                    last.then_inc(S["y_ps"], 1)
                pe.wait_ge(S["yb_sq"], layer + 1)
                for g in range(GROUPS):
                    for t in range(2):
                        last = mm(bank(g // 2)[:, (g % 2) * SEQ:(g % 2 + 1) * SEQ], C_("ones"), proj[:, XBC + 8 + 2 * g + t, :], t == 0, t == 1)
                last.then_inc(S["yb_sum"], 1)
                u = IN_UNITS
                pe.wait_ge(S["yb_std"], layer + 1)
                for half in range(2):
                    for q in range(GATE_UNITS):
                        split_is(b + u)
                        n = 16 * layer + GATE_UNITS * half + q
                        if n >= 4:
                            pe.wait_ge(S["gate_done"], n - 3)
                        tile_pair(q % 4, b, u)
                        u += 1
                    if half == 0:
                        pe.wait_ge(S["ylo_done"], 4 * (layer + 1))
                    blk = 0
                    for tile in range(4):
                        n = 8 * layer + 4 * half + tile
                        if n >= 2:
                            pe.wait_ge(S["merge_done"], n - 1)
                        for br, (y0, depth) in enumerate(BRANCHES):
                            o = bank(4 + 2 * (tile % 2) + br // 2)[:, (br % 2) * SEQ:(br % 2 + 1) * SEQ]
                            for k in range(depth):
                                if blk % BLOCKS == 0:
                                    split_is(b + u)
                                last = product(o, (b + u) % RING, blk % BLOCKS, y_hi[:, y0 + k, :], y_lo[:, y0 + k, :], k == 0, k == depth - 1)
                                blk += 1
                                if blk % BLOCKS == 0:
                                    last.then_inc(unit_used, 1)
                                    u += 1
                        if tile < 3:
                            last.then_inc(S["br_ps"], 1)
                pe.wait_ge(S["m_lo"], layer + 1)
                for q in range(OUT_UNITS):
                    split_is(b + u)
                    tile_pair(q, b, u)
                    u += 1
                norm(2 * layer + 1)
                pe.wait_ge(S["h_lo_done"], 2 * layer + 2)
                if layer == 0:
                    f0 = MIX_UNITS

                    def down(j, i=0):
                        for f in range(2):
                            for m in range(KT):
                                last = product(bank(m // 2)[:, (m % 2) * SEQ:(m % 2 + 1) * SEQ], (f0 + j) % RING, f * KT + m,
                                               hid_hi[:, f, :], hid_lo[:, f, :], False, False)
                        last.then_inc(unit_used, 1)

                    split_is(f0)
                    tile_pair(4, f0, 0)
                    split_is(f0 + 1)
                    tile_pair(5, f0, 1)
                    pe.wait_ge(S["acc_zero"], 1)
                    with pe.Fori(0, FF_STEPS - 1) as i:
                        split_is(f0 + 2 + RING * i)
                        pe.wait_ge(S["silu_done"], i + 1)
                        tile_pair(4, f0, 2)
                        split_is(f0 + 3 + RING * i)
                        pe.wait_ge(S["hid_done"], 2 * i + 2)
                        down(3)
                        split_is(f0 + 4 + RING * i)
                        tile_pair(5, f0, 4)
                    split_is(f0 + FF_UNITS - 1)
                    pe.wait_ge(S["hid_done"], 2 * FF_STEPS)
                    down(FF_UNITS - 1)

            r_w = C_("router").rearrange("p (k n) -> p k n", k=KT)
            for t in range(TT):
                for k in range(KT):
                    last = mm(bank(6)[:, t * EXPERTS:(t + 1) * EXPERTS], h[:, k, t * P:(t + 1) * P], r_w[:, k, :], k == 0, k == KT - 1)
            last.then_inc(S["router_ps"], 1)
            for t in range(TT):
                for k in range(KT):
                    last = nc.tensor.transpose(bank(2 * t + k // 4)[:, (k % 4) * P:(k % 4 + 1) * P], h[:, k, t * P:(t + 1) * P], C_("ident"))
                last.then_inc(S["tok_ps"], 1)
            pe.wait_ge(S["sel_done"], 1)
            chosen = route[:, 3 * TT * EXPERTS:4 * TT * EXPERTS].rearrange("p (t n) -> p t n", t=TT)
            mm(bank(6)[:, 0:EXPERTS], C_("upto"), chosen[:, 0, :], True, True)
            mm(bank(6)[:, EXPERTS:2 * EXPERTS], C_("upto"), chosen[:, 1, :], True, False)
            mm(bank(6)[:, EXPERTS:2 * EXPERTS], C_("ones"), chosen[:, 0, :], False, True)
            mm(bank(6)[:, 2 * EXPERTS:3 * EXPERTS], C_("ones"), chosen[:, 0, :], True, False)
            mm(bank(6)[:, 2 * EXPERTS:3 * EXPERTS], C_("ones"), chosen[:, 1, :], False, True).then_inc(S["pos_ps"], 1)
            pe.wait_ge(S["tok_lo_done"], TT)
            pe.wait_ge(S["items_done"], 1)
            n_items = pe.value_load(ints[0:1, 31:32], min_val=1, max_val=MAX_ITEMS)
            with pe.Fori(0, n_items) as item:
                def up(o, j, c=0):
                    slot, half = (MOE_U + j) % RING, j % 2
                    split_is(MOE_U + j + ITEM_UNITS * item + 6 * c)
                    for k in range(4):
                        w = slice(k * CHUNK_F, (k + 1) * CHUNK_F)
                        kk = 4 * half + k
                        mm(o, xg_hi[:, kk, :], hi[:, slot, w], kk == 0, False)
                        mm(o, xg_hi[:, kk, :], lo[:, slot, w], False, False)
                        last = mm(o, xg_lo[:, kk, :], hi[:, slot, w], False, kk == KT - 1)
                    last.then_inc(unit_used, 1)

                def transposes(c):
                    pe.wait_ge(S["eh_done"], item * CHUNKS + c + 1)
                    for f in range(4):
                        last = nc.tensor.transpose(bank(6)[:, f * P:(f + 1) * P], ff_h[:, f * P:(f + 1) * P], C_("ident"))
                    last.then_inc(S["hT_ps"], 1)

                def down(j, c):
                    slot, half = (MOE_U + j) % RING, j % 2
                    split_is(MOE_U + j + ITEM_UNITS * item + 6 * c)
                    for f in range(2):
                        for n in range(2):
                            w = slice(f * D + n * 512, f * D + (n + 1) * 512)
                            mm(bank(n), hT_hi[:, 2 * half + f, :], hi[:, slot, w], False, False)
                            mm(bank(n), hT_hi[:, 2 * half + f, :], lo[:, slot, w], False, False)
                            last = mm(bank(n), hT_lo[:, 2 * half + f, :], hi[:, slot, w], False, False)
                    last.then_inc(unit_used, 1)

                pe.wait_ge(S["pick_done"], item + 1)
                pe.wait_ge(S["item_added"], item + 1)
                for t in range(TT):
                    last = nc.tensor.transpose(bank(6)[:, t * P:(t + 1) * P], pick_g[:, t, :], C_("ident"))
                last.then_inc(S["pickT_ps"], 1)
                for part, tok in enumerate((tok_hi, tok_lo)):
                    for k in range(KT):
                        o = bank(2 * part + k // 4)[:, (k % 4) * P:(k % 4 + 1) * P]
                        mm(o, tok[:, 0, k * P:(k + 1) * P], pick[:, 0, :], True, False)
                        last = mm(o, tok[:, 1, k * P:(k + 1) * P], pick[:, 1, :], False, True)
                last.then_inc(S["gather_ps"], 1)
                pe.wait_ge(S["xg_hi_done"], item + 1)
                pe.wait_ge(S["xg_lo_done"], item + 1)
                up(bank(4), 0)
                up(bank(4), 1)
                up(bank(5), 2)
                pe.wait_ge(S["pickT_done"], item + 1)
                pe.wait_ge(S["y_zero"], item + 1)
                up(bank(5), 3)
                with pe.Fori(0, CHUNKS - 1) as c:
                    pe.wait_ge(S["esilu_done"], item * CHUNKS + c + 1)
                    up(bank(4), 4, c)
                    transposes(c)
                    up(bank(4), 5, c)
                    up(bank(5), 6, c)
                    up(bank(5), 7, c)
                    pe.wait_ge(S["hT_lo_done"], item * CHUNKS + c + 1)
                    down(8, c)
                    down(9, c)
                transposes(CHUNKS - 1)
                pe.wait_ge(S["hT_lo_done"], item * CHUNKS + CHUNKS)
                down(ITEM_UNITS - 2, 0)
                down(ITEM_UNITS - 1, 0)
                pe.wait_ge(S["y_copied"], item + 1)
                for m in range(KT):
                    last = mm(bank(2 + m // 2)[:, (m % 2) * SEQ:(m % 2 + 1) * SEQ], y_sb[:, m * P:(m + 1) * P], pickT, True, True)
                last.then_inc(S["scatter_ps"], 1)
            norm(2 * DEPTH)


def blocks_of(w):
    k, n = w.shape
    return w.reshape(k // P, P, n // P, P).transpose(0, 2, 1, 3)


def units_of(blocks):
    a = np.asarray(blocks).reshape(-1, BLOCKS, P, P)
    return a.transpose(0, 2, 1, 3).reshape(-1, P, UNIT)


def by_output(w):
    return blocks_of(w).transpose(1, 0, 2, 3).reshape(-1, P, P)


def per_channel(v):
    return v.reshape(-1, P).T


def mixer_units(q, layer):
    w = q["w_in"][layer]
    n_a, n_b, z = 3 * 512, 1024 + 2048 + HEADS, 1024
    b0 = n_a
    c0 = n_a + n_b
    d0 = c0 + 1024
    order = [w[:, 0:n_a], w[:, d0:d0 + 512], w[:, c0:c0 + 1024], w[:, b0:b0 + z], w[:, b0 + z:b0 + z + 2048]]
    parts = [by_output(np.concatenate(order, 1))]
    gate = blocks_of(q["w_gate"][layer])
    br = [blocks_of(q[n][layer]) for n in ("w_br_a", "w_br_b", "w_br_c", "w_br_d")]
    for half in range(2):
        outs = range(4 * half, 4 * half + 4)
        parts.append(np.concatenate([gate[:, n * 8 + j] for j in outs for n in range(4)]))
        parts.append(np.concatenate([w_[:, j] for j in outs for w_ in br]))
    parts.append(by_output(q["w_out"][layer]))
    return np.concatenate([units_of(p) for p in parts])


def dense_units(q):
    g, u = (by_output(q[n][0]).reshape(-1, BLOCKS, P, P) for n in ("ffn_wg", "ffn_wu"))
    d = blocks_of(q["ffn_wd"][0]).reshape(-1, BLOCKS, P, P)
    seq = [g[0], u[0]]
    for f in range(FF_STEPS - 1):
        seq += [g[f + 1], d[f], u[f + 1]]
    return units_of(np.concatenate(seq + [d[-1]]))


def expert_units(q):
    def up(w):
        return w.reshape(EXPERTS, 2, 4, P, CHUNKS, CHUNK_F).transpose(0, 4, 1, 3, 2, 5).reshape(EXPERTS, CHUNKS, 2, P, UNIT)

    g, u = up(q["moe_wg"][0]), up(q["moe_wu"][0])
    d = q["moe_wd"][0].reshape(EXPERTS, CHUNKS, 2, 2, P, D).transpose(0, 1, 2, 4, 3, 5).reshape(EXPERTS, CHUNKS, 2, P, UNIT)
    out = np.empty((EXPERTS, ITEM_UNITS, P, UNIT), np.float32)
    out[:, 0:2], out[:, 2:4] = g[:, 0], u[:, 0]
    for c in range(CHUNKS - 1):
        at = 4 + 6 * c
        out[:, at:at + 2], out[:, at + 2:at + 4], out[:, at + 4:at + 6] = g[:, c + 1], u[:, c + 1], d[:, c]
    out[:, ITEM_UNITS - 2:] = d[:, CHUNKS - 1]
    return out.reshape(-1, P, UNIT)


def params(q, layer):
    def rows(v):
        return np.broadcast_to(v.reshape(1, -1), (P, v.size))

    w_dt = q["w_in"][layer][:, 3 * 512 + 3072:3 * 512 + 3072 + HEADS].reshape(KT, P, HEADS).transpose(1, 0, 2).reshape(P, -1)
    parts = [per_channel(q["norm1_g"][layer]), per_channel(q["norm2_g"][layer]), per_channel(q["sc_conv_w"][layer]),
             per_channel(q["ssm_conv_w"][layer]), per_channel(q["ssm_conv_b"][layer]), rows(q["ssm_dt_bias"][layer]),
             rows(q["ssm_a_log"][layer]), per_channel(np.repeat(q["ssm_d"][layer], HEAD_DIM)), per_channel(q["ssm_norm_g"][layer]),
             per_channel(q["gm_ln_g"][layer]), per_channel(q["gm_ln_b"][layer]), per_channel(q["pool_scale"][layer]), w_dt,
             q["gm_ws"][layer].transpose(2, 0, 1).reshape(P, -1), rows(q["gm_bias"][layer]),
             q["pool_map"][layer].transpose(1, 0, 2).reshape(P, -1)]
    return np.concatenate(parts, 1)


def constants(q):
    r = np.arange(P)
    f = lambda a: np.asarray(a, np.float32)
    inv = np.stack([1.0 / np.minimum(np.arange(1, 17), w) for w in (2, 4, 8, 16)])
    wide = lambda a: np.broadcast_to(f(a).reshape(1, -1), (P, np.size(a)))
    parts = [f(np.eye(P)), f(r[:, None] <= r[None, :]), f(np.ones((P, P))), f(r[:, None] > r[None, :]), wide(r), wide(inv),
             wide(np.arange(EXPERTS)), wide(np.repeat(np.arange(MAX_ITEMS), EXPERTS)), wide([EPS]), per_channel(q["final_g"]),
             q["router_w"][0].reshape(KT, P, EXPERTS).transpose(1, 0, 2).reshape(P, -1)]
    return np.concatenate(parts, 1)


def kernel(**inputs):
    import concourse.bacc as bacc
    from concourse.bass_utils import run_bass_kernel_spmd

    q = {k: np.asarray(v) for k, v in inputs.items()}
    arrays = {
        "x_in": q["x"][0].T.reshape(KT, P, SEQ).transpose(1, 0, 2),
        "par_in": np.stack([params(q, layer) for layer in range(DEPTH)]),
        "con_in": constants(q),
        "mix_w": np.stack([mixer_units(q, layer) for layer in range(DEPTH)]),
        "ff_w": dense_units(q),
        "moe_w": expert_units(q),
    }
    arrays = {k: np.ascontiguousarray(v) for k, v in arrays.items()}
    nc = bacc.Bacc("TRN2", target_bir_lowering=False, num_devices=1)
    aps = [nc.dram_tensor(k, a.shape, mybir.dt.from_np(a.dtype), kind="ExternalInput").ap() for k, a in arrays.items()]
    out = nc.dram_tensor("out", (P, KT, SEQ), mybir.dt.float32, kind="ExternalOutput").ap()
    trunk(nc, *aps, out)
    r = run_bass_kernel_spmd(nc, [arrays], core_ids=[0])
    return r.results[0]["out"].transpose(1, 0, 2).reshape(D, SEQ).T.reshape(1, SEQ, D)
```

```python
from contextlib import ExitStack

import numpy as np
import concourse.bass as bass
from concourse import mybir

D = 1024
SEQ = 256
DEPTH = 2
P = 128
KT = D // P
TT = SEQ // P
UNIT = 2048
BLOCKS = UNIT // P
EPS = 1e-6
HEADS, HEAD_DIM, GROUPS = 16, 64, 4
SC_BLOCKS, XBC_BLOCKS, Z_BLOCKS = 4, 16, 8
D_FF, D_FFE, EXPERTS = 2816, 3584, 8
SC_K, SSM_K = 3, 4
FF_STEPS = D_FF // (2 * P)
CHUNK_F = 512
CHUNKS = D_FFE // CHUNK_F
ITEM_UNITS = 6 * CHUNKS
MAX_ITEMS = EXPERTS + (2 * SEQ) // (P + 1)
MIN_ITEMS = 2 * SEQ // P
RING = 3
AHEAD = 2

XBC, GU, GV, PD, A_H, A_B, A_C, ZB = 0, 16, 20, 24, 28, 32, 36, 40
N_PROJ = 48
IN_UNITS = N_PROJ // 2
EARLY = ("a", "c", "d")
EARLY_BLOCKS = len(EARLY) * (KT + 4)
EARLY_UNITS = KT * EARLY_BLOCKS // BLOCKS
B_UNITS = KT * KT // BLOCKS
OUT_UNITS = KT * KT // BLOCKS
U_EARLY = IN_UNITS
U_GB = U_EARLY + EARLY_UNITS
U_PB = U_GB + B_UNITS
U_OUT = U_PB + B_UNITS
MIX_UNITS = U_OUT + OUT_UNITS
FF_UNITS = 3 * FF_STEPS
RAW_E = 6
PLAN = (
    ("dt_in", 1), ("dt_log", 1), ("conv0", 2), ("dt_out", 0), ("conv1", 2), ("conv2", 2), ("conv3", 2),
    ("xs_T", 1), ("xdt", 1), ("gelu", 1), ("mean", 1), ("var", 1), ("v_T", 1), ("spatial", 2), ("pool", 2),
    ("pool_out", 2), ("short", 2), ("z", 1), ("cb0", 1), ("cb1", 1),
    ("seg_in0", 1), ("seg0", 1), ("score0", 1), ("y0", 0), ("seg_in1", 1), ("seg1", 1), ("score1", 1), ("y1", 0),
    ("seg_in2", 1), ("seg2", 1), ("score2", 1), ("y2", 0), ("seg_in3", 1), ("seg3", 1), ("score3", 1), ("y3", 0),
    ("y_sq", 1), ("y_sum", 2), ("y_norm", 0))


def early_event(layer, e):
    ends = [EARLY_BLOCKS * (n // 2) + (len(EARLY) * KT if n % 2 == 0 else EARLY_BLOCKS) for n in range(2 * KT)]
    own = [n for n in ends if n % BLOCKS]
    return ends[e], (own.index(ends[e]) + 1 + len(own) * layer if ends[e] % BLOCKS else None)


def columns(*parts):
    at, out = 0, {}
    for name, n in parts:
        out[name] = (at, at + n)
        at += n
    return out, at


PAR, N_PAR = columns(
    ("norm1", KT), ("norm2", KT), ("sc_w", SC_K * SC_BLOCKS), ("ssm_w", SSM_K * XBC_BLOCKS),
    ("ssm_b", XBC_BLOCKS), ("dt_bias", HEADS), ("a_log", HEADS), ("d_skip", 8), ("norm_g", 8),
    ("ln_g", 4), ("ln_b", 4), ("pool_scale", 4), ("w_dt", KT * HEADS), ("ws", 4 * P),
    ("gm_bias", 4 * P), ("pool_map", 4 * P))
CON, N_CON = columns(
    ("ident", P), ("upto", P), ("ones", P), ("after", P), ("iota", P), ("inv_count", 64),
    ("experts", EXPERTS), ("items", MAX_ITEMS * EXPERTS), ("eps", 1), ("final", KT), ("router", KT * EXPERTS))


def trunk(nc, x_in, par_in, con_in, mix_w, ff_w, moe_w, out):
    f32, f32r, i32, u32 = mybir.dt.float32, mybir.dt.float32r, mybir.dt.int32, mybir.dt.uint32
    ACT, ALU, AX = mybir.ActivationFunctionType, mybir.AluOpType, mybir.AxisListType
    ds = bass.ds
    ctx = ExitStack()
    with ctx:
        def sb(name, shape, dt=f32):
            return ctx.enter_context(nc.sbuf_tensor(name, shape, dt))

        def sem(name):
            return ctx.enter_context(nc.semaphore(name))

        raw = sb("weight_raw", [P, RING, UNIT])
        hi = sb("weight_hi", [P, RING, UNIT], f32r)
        lo = sb("weight_lo", [P, RING, UNIT], f32r)
        x = sb("x", [P, KT, SEQ])
        h_hi = sb("h_hi", [P, KT, SEQ], f32r)
        h_lo = sb("h_lo", [P, KT, SEQ], f32r)
        proj = sb("proj", [P, N_PROJ, SEQ])
        y_hi = sb("y_hi", [P, 12, SEQ], f32r)
        y_lo = sb("y_lo", [P, 12, SEQ], f32r)
        with nc.sbuf_tensor("tmp", [P, 16, SEQ], f32) as tmp:
            pass
        yb_hi = sb("yb_hi", [P, 8, SEQ], f32r)
        yb_lo = sb("yb_lo", [P, 8, SEQ], f32r)
        par = sb("par", [P, N_PAR])
        con = sb("con", [P, N_CON])
        scr = sb("scr", [P, 1024])
        small = sb("small", [P, 14, 2, HEADS])
        ints = sb("ints", [P, 32], i32)
        PS = ctx.enter_context(nc.psum_tensor("psum", [P, 8, 512], f32))

        def bank(b, n=1):
            return PS[:, b:b + n, :].rearrange("p b n -> p (b n)")

        def tiles(ap, n=SEQ):
            return ap.rearrange("p (t n) -> p t n", n=n)

        def flat(ap):
            return ap.rearrange("p t n -> p (t n)")

        def P_(name, i=0, n=None):
            a, b = PAR[name]
            return par[:, a + i:(b if n is None else a + i + n)]

        def C_(name, i=0, n=None):
            a, b = CON[name]
            return con[:, a + i:(b if n is None else a + i + n)]

        sq, h = proj[:, 24:32, :], proj[:, 32:40, :]
        xdt = flat(tmp[:, 0:8, :]).rearrange("p (t c) -> p t c", t=TT)
        cb = flat(proj[:, 24:30, :]).rearrange("p (g l) -> p g l", g=GROUPS)
        seg_in0, seg_in1 = tiles(flat(proj[:, 30:34, :])), tiles(flat(proj[:, 34:36, :]), P)
        dec0 = tiles(flat(proj[:, 36:40, :]))
        dec1 = tiles(scr[:, 0:512], P)
        merged, gate_b, y_b = proj[:, 16:24, :], proj[:, 24:32, :], proj[:, ZB:ZB + 8, :]
        y_sq = proj[:, 8:16, :]
        vT = flat(tmp[:, 8:12, :]).rearrange("p (t c) -> p t c", t=TT)
        v_sq, pooled = tmp[:, 12:16, :], tmp[:, 8:12, :]
        v_std, v_mean = tmp[:, 8, :], tmp[:, 9, :]
        std = scr[:, 0:SEQ]

        def gate_of(tile):
            at = 8 + 3 * (tile % 2)
            return tmp[:, at:at + 3, :]

        ff_g, ff_h = flat(proj[:, 40:42, :]), flat(proj[:, 42:44, :])
        pick_g, pickT = tiles(flat(proj[:, 44:45, :]), P), proj[:, 45, :]
        y_sb = scr[:, 0:D]
        hid_hi, hid_lo = y_hi[:, 0:2, :], y_lo[:, 0:2, :]
        tok_hi, tok_lo = (flat(t[:]).rearrange("p (t c) -> p t c", t=TT) for t in (yb_hi, yb_lo))
        xg_hi, xg_lo = (tiles(flat(t[:, 0:4, :]), P) for t in (y_hi, y_lo))
        hT_hi, hT_lo = (tiles(flat(t[:, 4:6, :]), P) for t in (y_hi, y_lo))
        pick = tiles(flat(y_hi[:, 6:7, :]), P)
        route = flat(proj[:, 26:32, :])

        def raw_e(v):
            n = v % RAW_E
            return raw[:, n, :] if n < RING else flat(proj[:, 8 * (n - RING):8 * (n - RING) + 8, :])

        raw_landed = [sem(f"raw_landed{i}") for i in range(RING)]
        raw_e_landed = [sem(f"raw_e_landed{i}") for i in range(RAW_E)]
        hi_done, lo_done, unit_used = sem("hi_done"), sem("lo_done"), sem("unit_used")
        in_loaded, par_loaded, stored = sem("in_loaded"), sem("par_loaded"), sem("stored")
        dve_order, act_order = sem("dve_order"), sem("act_order")
        S = {n: sem(n) for n in (
            "sq_done", "norm_sum", "std_done", "h_done", "h_hi_done", "h_lo_done", "dt_raw",
            "win_done", "gelu_done", "mean_sum", "dev_sq", "var_sum", "v_std", "v_norm", "v_T", "v_T_sb",
            "ws_masked", "s_done", "pooled", "pool_out", "a_sc", "a_exp", "dt_w", "dt_ln", "conv_acc", "conv_done",
            "z_done", "xs_T", "xdt_done", "cb_ps", "cb_done", "seg_in", "seg_done", "dec_exp", "score_done", "y_ps",
            "y_done", "yb_sq", "yb_sum", "yb_std", "ya_f", "ya_hi", "ya_lo", "yc_f", "yc_hi", "yc_lo", "yd_f", "yd_hi",
            "yd_lo", "yb_f", "yb_hi", "yb_lo", "early_ps", "gate_done", "early_added", "gate_b_done", "merge_done",
            "m_hi", "m_lo", "silu_done", "mult_done", "hid_done",
            "acc_zero", "router_ps", "gap_exp", "gap_in", "sel_done", "pos_ps", "items_done",
            "tok_ps", "tok_hi_done", "tok_lo_done", "pick_done", "pick_g_done", "gather_ps", "pickT_ps", "pickT_done",
            "xg_hi_done", "xg_lo_done", "hT_ps", "hT_hi_done", "hT_lo_done", "esilu_done", "eh_done",
            "y_zero", "y_copied", "scatter_ps", "item_added", "final_done")}
        PAIRS = KT // 2

        MOE_U = MIX_UNITS + FF_UNITS + MIX_UNITS

        def base_of(layer):
            return layer * (MIX_UNITS + FF_UNITS)

        def item_at(item):
            return 4 + item * ITEM_UNITS

        def last_split(layer, u):
            return layer == DEPTH - 1 and u + AHEAD >= MIX_UNITS

        block = ctx.enter_context(nc.Block())

        @block.sync
        def _(sp):
            def load(src, first, j, i=0):
                u = first + j + RING * i
                sp.wait_ge(lo_done, u + 1)
                sp.dma_start(raw[:, (first + j) % RING, :], src).then_inc(raw_landed[(first + j) % RING], 16)

            sp.dma_start(x[:], x_in).then_inc(in_loaded, 16)
            sp.dma_start(con[:], con_in).then_inc(in_loaded, 16)
            for layer in range(DEPTH):
                if layer:
                    sp.wait_ge(S["yb_lo"], 2 * layer)
                    sp.wait_ge(S["h_done"], 2 * PAIRS * layer)
                sp.dma_start(par[:], par_in[layer]).then_inc(par_loaded, 16)
                with sp.Fori(0, MIX_UNITS // RING) as i:
                    for j in range(RING):
                        load(mix_w[layer, ds(i * RING + j, 1), :, :].rearrange("a p n -> (a p) n"), base_of(layer), j, i)
                if layer == 0:
                    with sp.Fori(0, FF_UNITS // RING) as i:
                        for j in range(RING):
                            load(ff_w[ds(i * RING + j, 1), :, :].rearrange("a p n -> (a p) n"), MIX_UNITS, j, i)

            def load_e(unit, v, after):
                sp.wait_ge(lo_done, RING + MOE_U + after + 1)
                sp.dma_start(raw_e(v), moe_w[ds(unit, 1), :, :].rearrange("a p n -> (a p) n")).then_inc(raw_e_landed[v % RAW_E], 16)

            sp.wait_ge(S["items_done"], 1)
            last_item = sp.value_load(ints[0:1, 31:32], min_val=MIN_ITEMS - 1, max_val=MAX_ITEMS - 1)
            expert = sp.value_load(ints[0:1, 0:1], min_val=0, max_val=EXPERTS - 1)
            for v in range(4):
                load_e(expert * ITEM_UNITS + v, v, -1)
            for v in (4, 5):
                load_e(expert * ITEM_UNITS + v, v, -1)
            with sp.Fori(0, last_item) as item:
                expert = sp.value_load(ints[0:1, ds(item, 1)], min_val=0, max_val=EXPERTS - 1)
                following = sp.value_load(ints[0:1, ds(item + 1, 1)], min_val=0, max_val=EXPERTS - 1)
                with sp.Fori(0, 5) as i:
                    for j in range(6):
                        load_e(expert * ITEM_UNITS + 6 + 6 * i + j, 6 + j, item * ITEM_UNITS + 6 * i + j)
                for j in range(4):
                    load_e(expert * ITEM_UNITS + 36 + j, 36 + j, item * ITEM_UNITS + 30 + j)
                for j in range(4):
                    load_e(following * ITEM_UNITS + j, 40 + j, item * ITEM_UNITS + 34 + j)
                for j in range(2):
                    load_e(expert * ITEM_UNITS + 40 + j, 44 + j, item * ITEM_UNITS + 38 + j)
                for j in range(2):
                    load_e(following * ITEM_UNITS + 4 + j, 46 + j, item * ITEM_UNITS + 40 + j)
            expert = sp.value_load(ints[0:1, ds(last_item, 1)], min_val=0, max_val=EXPERTS - 1)
            for j in range(36):
                load_e(expert * ITEM_UNITS + 6 + j, 6 + j, last_item * ITEM_UNITS + j)
            sp.wait_ge(S["final_done"], 1)
            sp.dma_start(out, h).then_inc(stored, 16)
            sp.wait_ge(stored, 16)

        @block.scalar
        def _(act):
            A = nc.scalar.activation
            def split(first, j, i=0):
                slot = (first + j) % RING
                u = first + j + RING * i
                act.wait_ge(raw_landed[slot], 16 * ((first + j) // RING + i + 1))
                act.wait_ge(unit_used, u + 1)
                A(hi[:, slot, :], raw[:, slot, :], ACT.Copy).then_inc(hi_done, 1)

            def used(u):
                act.wait_ge(unit_used, RING + u + 1)

            def norm(n, parts=True):
                act.wait_ge(S["norm_sum"], n + 1)
                A(std, bank(4)[:, 0:SEQ], ACT.Sqrt, bias=C_("eps"), scale=1.0 / D).then_inc(S["std_done"], 1)
                if parts:
                    for q in range(PAIRS):
                        act.wait_ge(S["h_done"], PAIRS * n + q + 1)
                        A(flat(h_hi[:, 2 * q:2 * q + 2, :]), flat(h[:, 2 * q:2 * q + 2, :]), ACT.Copy).then_inc(S["h_hi_done"], 1)

            def mixer_unit(layer, u):
                b = base_of(layer)
                if not last_split(layer, u):
                    split(b, u + AHEAD)
                if u < IN_UNITS:
                    used(b + u)
                    A(flat(proj[:, 2 * u:2 * u + 2, :]), bank(u % 4), ACT.Copy).then_inc(S["win_done"], 1)
                elif u < U_GB:
                    for tile in range(KT):
                        end, count = early_event(layer, 2 * tile)
                        if (end - 1) // BLOCKS == u - U_EARLY:
                            if count:
                                act.wait_ge(S["early_ps"], count)
                            else:
                                used(b + u)
                            if tile >= 2:
                                act.wait_ge(S["early_added"], KT * layer + tile - 1)
                            A(flat(gate_of(tile)), bank(0, 2)[:, 0:3 * SEQ], ACT.Sigmoid).then_inc(S["gate_done"], 1)
                elif u < U_PB:
                    q = u - U_GB
                    used(b + u)
                    if q == 0:
                        act.wait_ge(S["y_ps"], GROUPS * (layer + 1))
                    A(flat(gate_b[:, 2 * q:2 * q + 2, :]), bank(q), ACT.Sigmoid).then_inc(S["gate_b_done"], 1)
                elif u < U_OUT:
                    q = u - U_PB
                    act.wait_ge(S["merge_done"], PAIRS * layer + q + 1)
                    A(flat(h_hi[:, 2 * q:2 * q + 2, :]), flat(merged[:, 2 * q:2 * q + 2, :]), ACT.Copy).then_inc(S["m_hi"], 1)

            def stage(name, layer):
                kind, g = name.rstrip("0123"), int(name[-1]) if name[-1].isdigit() else 0
                if kind == "dt_in":
                    act.wait_ge(par_loaded, 16 * (layer + 1))
                    act.wait_ge(S["a_sc"], layer + 1)
                    A(small[:, 0, 0, :], P_("a_log"), ACT.Exp).then_inc(S["a_exp"], 1)
                    A(small[:, 3, :, :], small[:, 2, :, :], ACT.Exp).then_inc(S["a_exp"], 1)
                elif kind == "dt_log":
                    act.wait_ge(S["dt_w"], layer + 1)
                    A(small[:, 5, :, :], small[:, 4, :, :], ACT.Ln).then_inc(S["dt_ln"], 1)
                elif kind == "conv":
                    for t in range(4 * g, 4 * g + 4):
                        act.wait_ge(S["conv_acc"], XBC_BLOCKS * layer + t + 1)
                        A(proj[:, XBC + t, :], scr[:, (t % 4) * SEQ:(t % 4 + 1) * SEQ], ACT.Silu, bias=P_("ssm_b", t, 1)).then_inc(S["conv_done"], 1)
                elif kind == "gelu":
                    act.wait_ge(S["win_done"], IN_UNITS * layer + 12)
                    A(flat(proj[:, GV:GV + 4, :]), flat(proj[:, GV:GV + 4, :]), ACT.Gelu_apprx_tanh).then_inc(S["gelu_done"], 1)
                    A(flat(proj[:, GU:GU + 4, :]), flat(proj[:, GU:GU + 4, :]), ACT.Gelu_apprx_tanh).then_inc(S["gelu_done"], 1)
                elif kind == "var":
                    act.wait_ge(S["var_sum"], layer + 1)
                    A(v_std, bank(7)[:, 0:SEQ], ACT.Sqrt, bias=C_("eps"), scale=1.0 / 512).then_inc(S["v_std"], 1)
                elif kind == "v_T":
                    act.wait_ge(S["v_T"], layer + 1)
                    A(flat(tmp[:, 8:12, :]), bank(4, 2), ACT.Copy).then_inc(S["v_T_sb"], 1)
                elif kind == "spatial":
                    act.wait_ge(S["yc_f"], layer + 1)
                    A(flat(y_hi[:, 4:8, :]), flat(proj[:, GU:GU + 4, :]), ACT.Copy).then_inc(S["yc_hi"], 1)
                elif kind == "pool_out":
                    act.wait_ge(S["yd_f"], layer + 1)
                    A(flat(y_hi[:, 8:12, :]), flat(proj[:, PD:PD + 4, :]), ACT.Copy).then_inc(S["yd_hi"], 1)
                elif kind == "short":
                    act.wait_ge(S["ya_f"], layer + 1)
                    A(flat(y_hi[:, 0:4, :]), flat(proj[:, A_B:A_B + 4, :]), ACT.Copy).then_inc(S["ya_hi"], 1)
                elif kind == "z":
                    act.wait_ge(S["win_done"], IN_UNITS * (layer + 1))
                    A(flat(y_b), flat(y_b), ACT.Silu).then_inc(S["z_done"], 1)
                elif kind == "seg":
                    act.wait_ge(S["seg_done"], GROUPS * layer + g + 1)
                    if layer or g:
                        act.wait_ge(S["y_ps"], GROUPS * layer + g)
                    A(flat(dec0), bank(4, 2), ACT.Exp)
                    A(flat(dec1), bank(6), ACT.Exp).then_inc(S["dec_exp"], 1)
                elif kind == "y_sum":
                    act.wait_ge(S["yb_sum"], layer + 1)
                    A(scr[:, 0:1024], bank(4, 2), ACT.Sqrt, bias=C_("eps"), scale=1.0 / 256).then_inc(S["yb_std"], 1)
                elif kind == "y_norm":
                    for half in range(2):
                        act.wait_ge(S["yb_f"], 2 * layer + half + 1)
                        if half == 0:
                            act.wait_ge(S["early_added"], KT * (layer + 1))
                        A(flat(yb_hi[:, 4 * half:4 * half + 4, :]), flat(y_b[:, 4 * half:4 * half + 4, :]), ACT.Copy).then_inc(S["yb_hi"], 1)

            act.wait_ge(in_loaded, 32)
            for layer in range(DEPTH):
                if layer == 0:
                    split(0, 0)
                    split(0, 1)
                norm(2 * layer)
                u = 0
                for name, n in PLAN:
                    stage(name, layer)
                    for _ in range(n):
                        mixer_unit(layer, u)
                        u += 1
                for u in range(u, MIX_UNITS):
                    mixer_unit(layer, u)
                norm(2 * layer + 1)
                if layer == 0:
                    f0 = MIX_UNITS
                    split(f0, AHEAD)
                    used(f0)
                    A(ff_g, bank(4), ACT.Silu).then_inc(S["silu_done"], 1)
                    split(f0, 1 + AHEAD)
                    with act.Fori(0, FF_STEPS - 1) as i:
                        split(f0, 2 + AHEAD, i)
                        act.wait_ge(unit_used, RING + f0 + 2 + RING * i + 1)
                        act.wait_ge(S["mult_done"], i + 1)
                        A(ff_g, bank(4), ACT.Silu).then_inc(S["silu_done"], 1)
                        split(f0, 3 + AHEAD, i)
                        split(f0, 4 + AHEAD, i)
                    split(f0, FF_UNITS - 1 + AHEAD)

            act.wait_ge(S["gap_in"], 1)
            A(small[:, 6, :, 0:1], small[:, 5, :, 0:1], ACT.Exp).then_inc(S["gap_exp"], 1)
            for t in range(TT):
                act.wait_ge(S["tok_ps"], t + 1)
                A(tok_hi[:, t, :], bank(2 * t, 2), ACT.Copy).then_inc(S["tok_hi_done"], 1)
            act.wait_ge(S["items_done"], 1)
            last_item = act.value_load(ints[0:1, 31:32], min_val=MIN_ITEMS - 1, max_val=MAX_ITEMS - 1)

            def split_e(v, item=0):
                act.wait_ge(raw_e_landed[v % RAW_E], 16 * (v // RAW_E + item * (ITEM_UNITS // RAW_E) + 1))
                act.wait_ge(unit_used, MOE_U + v + item * ITEM_UNITS + 1)
                A(hi[:, v % RING, :], raw_e(v), ACT.Copy).then_inc(hi_done, 1)

            def gathered(item):
                act.wait_ge(S["gather_ps"], 2 * item + 1)
                A(flat(xg_hi), bank(2, 2), ACT.Copy).then_inc(S["xg_hi_done"], 1)

            def body(item, final):
                v = 4
                for c in range(CHUNKS):
                    ahead = not (final and c == CHUNKS - 1)
                    if ahead:
                        split_e(v + AHEAD, item)
                        v += 1
                    act.wait_ge(S["hT_ps"], item * CHUNKS + c + 1)
                    A(flat(hT_hi), bank(6), ACT.Copy).then_inc(S["hT_hi_done"], 1)
                    if ahead:
                        split_e(v + AHEAD, item)
                        act.wait_ge(unit_used, RING + MOE_U + v + item * ITEM_UNITS + 1)
                        A(ff_g, bank(4), ACT.Silu).then_inc(S["esilu_done"], 1)
                        v += 1
                        for _ in range(2):
                            split_e(v + AHEAD, item)
                            v += 1
                        if c == CHUNKS - 2 and not final:
                            gathered(item + 1)
                    if c == 3:
                        act.wait_ge(S["pickT_ps"], item + 1)
                        A(pickT, bank(7)[:, 0:SEQ], ACT.Copy).then_inc(S["pickT_done"], 1)
                    for _ in range(2):
                        if not (final and v + AHEAD >= 4 + ITEM_UNITS - 4):
                            split_e(v + AHEAD, item)
                        v += 1
                act.wait_ge(unit_used, RING + MOE_U + v + item * ITEM_UNITS)
                act.wait_ge(S["item_added"], 2 * item + 3)
                A(y_sb, bank(0, 2), ACT.Copy).then_inc(S["y_copied"], 1)

            act.sem_inc(S["y_copied"], 1)
            for v in range(AHEAD):
                split_e(v)
            gathered(0)
            split_e(0 + AHEAD)
            split_e(1 + AHEAD)
            act.wait_ge(unit_used, RING + MOE_U + 2)
            A(ff_g, bank(4), ACT.Silu).then_inc(S["esilu_done"], 1)
            split_e(2 + AHEAD)
            split_e(3 + AHEAD)
            with act.Fori(0, last_item) as item:
                body(item, False)
            body(last_item, True)
            norm(2 * DEPTH, False)

        @block.vector
        def _(dve):
            V = nc.vector
            dve_n = [0]

            def link(ins):
                dve_n[0] += 1
                ins.then_inc(dve_order, 1)
                dve.wait_ge(dve_order, dve_n[0])

            def split(first, j, i=0):
                slot = (first + j) % RING
                dve.wait_ge(hi_done, first + j + RING * i + 1)
                V.tensor_tensor(lo[:, slot, :], raw[:, slot, :], hi[:, slot, :].bitcast(f32), ALU.subtract).then_inc(lo_done, 1)

            def rest(out_, whole, hi_part, signal):
                V.tensor_tensor(out_, whole, hi_part.bitcast(f32), ALU.subtract).then_inc(signal, 1)

            def squares(q):
                V.tensor_tensor(flat(sq[:, 2 * q:2 * q + 2, :]), flat(x[:, 2 * q:2 * q + 2, :]), flat(x[:, 2 * q:2 * q + 2, :]), ALU.mult)\
                    .then_inc(S["sq_done"], 1)

            def norm(n, gain):
                dve.wait_ge(S["std_done"], n + 1)
                link(V.reciprocal(std, std))

                def lows(q):
                    dve.wait_ge(S["h_hi_done"], PAIRS * n + q + 1)
                    rest(flat(h_lo[:, 2 * q:2 * q + 2, :]), flat(h[:, 2 * q:2 * q + 2, :]), flat(h_hi[:, 2 * q:2 * q + 2, :]), S["h_lo_done"])

                for q in range(PAIRS):
                    for k in (2 * q, 2 * q + 1):
                        last = V.scalar_tensor_tensor(h[:, k, :], x[:, k, :], gain[:, k:k + 1], std, ALU.mult, ALU.mult)
                    if n == 2 * DEPTH:
                        continue
                    last.then_inc(S["h_done"], 1)
                    if q:
                        lows(q - 1)
                if n == 2 * DEPTH:
                    last.then_inc(S["final_done"], 1)
                else:
                    lows(PAIRS - 1)

            def merged_low(layer, q):
                dve.wait_ge(S["m_hi"], PAIRS * layer + q + 1)
                rest(flat(h_lo[:, 2 * q:2 * q + 2, :]), flat(merged[:, 2 * q:2 * q + 2, :]), flat(h_hi[:, 2 * q:2 * q + 2, :]), S["m_lo"])

            def mixer_unit(layer, u):
                b = base_of(layer)
                if not last_split(layer, u):
                    split(b, u + AHEAD)
                if U_EARLY <= u < U_GB:
                    for tile in range(KT):
                        end, count = early_event(layer, 2 * tile + 1)
                        if (end - 1) // BLOCKS == u - U_EARLY:
                            if count:
                                dve.wait_ge(S["early_ps"], count)
                            else:
                                dve.wait_ge(unit_used, RING + b + u + 1)
                            dve.wait_ge(S["gate_done"], KT * layer + tile + 1)
                            g = gate_of(tile)
                            link(V.tensor_tensor(flat(g), flat(g), bank(2, 2)[:, 0:3 * SEQ], ALU.mult))
                            link(V.tensor_tensor(g[:, 0, :], g[:, 0, :], g[:, 1, :], ALU.add))
                            V.tensor_tensor(merged[:, tile, :], g[:, 0, :], g[:, 2, :], ALU.add).then_inc(S["early_added"], 1)
                elif U_PB <= u < U_OUT:
                    q = u - U_PB
                    two = slice(2 * q, 2 * q + 2)
                    dve.wait_ge(unit_used, RING + b + u + 1)
                    dve.wait_ge(S["gate_b_done"], PAIRS * layer + q + 1)
                    dve.wait_ge(S["early_added"], KT * (layer + 1))
                    link(V.tensor_tensor(flat(gate_b[:, two, :]), flat(gate_b[:, two, :]), bank(4 + q), ALU.mult))
                    V.tensor_tensor(flat(merged[:, two, :]), flat(merged[:, two, :]), flat(gate_b[:, two, :]), ALU.add).then_inc(S["merge_done"], 1)
                    if q:
                        merged_low(layer, q - 1)
                    if q == PAIRS - 1:
                        merged_low(layer, q)
                elif u >= U_OUT:
                    q = u - U_OUT
                    dve.wait_ge(unit_used, RING + b + u + 1)
                    added(q)

            def added(q):
                link(V.tensor_tensor(flat(x[:, 2 * q:2 * q + 2, :]), flat(x[:, 2 * q:2 * q + 2, :]), bank(q), ALU.add))
                squares(q)

            def stage(name, layer):
                kind, g = name.rstrip("0123"), int(name[-1]) if name[-1].isdigit() else 0
                if kind == "dt_in":
                    dve.wait_ge(par_loaded, 16 * (layer + 1))
                    dve.wait_ge(S["dt_raw"], layer + 1)
                    raw_dt = bank(6)[:, 0:TT * HEADS].rearrange("p (t n) -> p t n", t=TT)
                    for t in range(TT):
                        last = V.tensor_tensor(small[:, 1, t, :], raw_dt[:, t, :], P_("dt_bias"), ALU.add)
                    link(last)
                    link(V.tensor_scalar(small[:, 2], small[:, 1], -1.0, None, ALU.mult))
                    V.tensor_tensor(small[:, 2], small[:, 2], small[:, 1], ALU.min).then_inc(S["a_sc"], 1)
                    for n in range(4):
                        last = V.tensor_tensor(P_("ws", n * P, P), P_("ws", n * P, P), C_("upto"), ALU.mult)
                    last.then_inc(S["ws_masked"], 1)
                elif kind == "dt_log":
                    dve.wait_ge(S["a_exp"], 2 * layer + 2)
                    V.tensor_scalar(small[:, 4], small[:, 3], 1.0, None, ALU.add).then_inc(S["dt_w"], 1)
                    dve.wait_ge(S["dt_w"], layer + 1)
                    link(V.scalar_tensor_tensor(small[:, 8], small[:, 4], -1.0, small[:, 3], ALU.add, ALU.subtract))
                    link(V.reciprocal(small[:, 9], small[:, 4]))
                    link(V.tensor_tensor(small[:, 8], small[:, 8], small[:, 9], ALU.mult))
                elif kind == "dt_out":
                    dve.wait_ge(S["dt_ln"], layer + 1)
                    link(V.tensor_tensor(small[:, 5], small[:, 5], small[:, 8], ALU.subtract))
                    link(V.scalar_tensor_tensor(small[:, 6], small[:, 1], 0.0, small[:, 5], ALU.max, ALU.add))
                    for t in range(TT):
                        last = V.scalar_tensor_tensor(small[:, 7, t, :], small[:, 6, t, :], -1.0, small[:, 0, 0, :], ALU.mult, ALU.mult)
                    link(last)
                elif kind == "conv":
                    dve.wait_ge(S["win_done"], IN_UNITS * layer + 2 * g + 2)
                    if g:
                        dve.wait_ge(S["conv_done"], XBC_BLOCKS * layer + 4 * g)
                    accs, raws = tiles(scr[:]), proj[:, XBC + 4 * g:XBC + 4 * g + 4, :]
                    for t in range(4):
                        last = V.tensor_scalar(accs[:, t, :], raws[:, t, :], P_("ssm_w", 3 * XBC_BLOCKS + 4 * g + t, 1), None, ALU.mult)
                    link(last)
                    for tap in (2, 1, 0):
                        s = SSM_K - 1 - tap
                        for t in range(4):
                            last = V.scalar_tensor_tensor(accs[:, t, s:], raws[:, t, :SEQ - s], P_("ssm_w", tap * XBC_BLOCKS + 4 * g + t, 1),
                                                          accs[:, t, s:], ALU.mult, ALU.add)
                            if tap == 0:
                                last.then_inc(S["conv_acc"], 1)
                        if tap:
                            link(last)
                elif kind == "xdt":
                    for t in range(TT):
                        dve.wait_ge(S["xs_T"], TT * layer + t + 1)
                        V.tensor_tensor(xdt[:, t, :].rearrange("p (h n) -> p h n", h=HEADS),
                                        bank(6 - 2 * t, 2).rearrange("p (h n) -> p h n", h=HEADS),
                                        small[:, 6, t, :].rearrange("p (h n) -> p h n", n=1).broadcast_to([P, HEADS, HEAD_DIM]),
                                        ALU.mult).then_inc(S["xdt_done"], 1)
                elif kind == "mean":
                    dve.wait_ge(S["mean_sum"], layer + 1)
                    link(V.tensor_scalar(v_mean, bank(7)[:, 0:SEQ], 1.0 / 512, None, ALU.mult))
                    for t in range(4):
                        last = V.tensor_tensor(v_[:, t, :], v_[:, t, :], v_mean, ALU.subtract)
                    link(last)
                    V.tensor_tensor(flat(v_sq), flat(v_), flat(v_), ALU.mult).then_inc(S["dev_sq"], 1)
                elif kind == "var":
                    dve.wait_ge(S["v_std"], layer + 1)
                    link(V.reciprocal(v_std, v_std))
                    for t in range(4):
                        last = V.scalar_tensor_tensor(v_[:, t, :], v_[:, t, :], P_("ln_g", t, 1), v_std, ALU.mult, ALU.mult)
                    link(last)
                    for t in range(4):
                        last = V.tensor_scalar(v_[:, t, :], v_[:, t, :], P_("ln_b", t, 1), None, ALU.add)
                    last.then_inc(S["v_norm"], 1)
                elif kind == "spatial":
                    dve.wait_ge(S["s_done"], layer + 1)
                    for t in range(TT):
                        last = V.tensor_tensor(v_[:, :, t * P:(t + 1) * P], tiles(bank(6, 2))[:, :, t * P:(t + 1) * P],
                                               tiles(P_("gm_bias"), P), ALU.add)
                    link(last)
                    dve.wait_ge(S["gelu_done"], 2 * layer + 2)
                    V.tensor_tensor(flat(u_), flat(u_), flat(v_), ALU.mult).then_inc(S["yc_f"], 1)
                    dve.wait_ge(S["yc_hi"], layer + 1)
                    rest(flat(y_lo[:, 4:8, :]), flat(u_), flat(y_hi[:, 4:8, :]), S["yc_lo"])
                elif kind == "pool":
                    dve.wait_ge(S["win_done"], IN_UNITS * layer + PD // 2 + 2)
                    s_a, s_b = tmp[:, 12:16, :], v_
                    src, dst = pd, s_a
                    for step in range(4):
                        w = 1 << step
                        V.tensor_tensor(dst[:, step:, w:], src[:, step:, w:], src[:, step:, :SEQ - w], ALU.add)
                        link(V.tensor_copy(dst[:, step:, 0:w], src[:, step:, 0:w]))
                        V.scalar_tensor_tensor(pooled[:, step, 16:], dst[:, step, 16:], 1.0 / (2 * w), pd[:, step, 16:], ALU.mult, ALU.subtract)
                        link(V.tensor_tensor(pooled[:, step, 0:16], dst[:, step, 0:16], C_("inv_count", 16 * step, 16), ALU.mult))
                        V.tensor_tensor(pooled[:, step, 0:16], pooled[:, step, 0:16], pd[:, step, 0:16], ALU.subtract)\
                            .then_inc(S["pooled"], 1)
                        src, dst = (s_a, s_b) if step % 2 == 0 else (s_b, s_a)
                elif kind == "pool_out":
                    dve.wait_ge(S["pool_out"], layer + 1)
                    for t in range(4):
                        last = V.tensor_scalar(pd[:, t, :], tiles(bank(4, 2))[:, t, :], P_("pool_scale", t, 1), None, ALU.mult)
                    last.then_inc(S["yd_f"], 1)
                    dve.wait_ge(S["yd_hi"], layer + 1)
                    rest(flat(y_lo[:, 8:12, :]), flat(pd), flat(y_hi[:, 8:12, :]), S["yd_lo"])
                elif kind == "short":
                    dve.wait_ge(S["win_done"], IN_UNITS * layer + A_C // 2 + 2)
                    a_h, a_b, a_c = (proj[:, n:n + 4, :] for n in (A_H, A_B, A_C))
                    link(V.tensor_tensor(flat(a_h), flat(a_h), flat(a_c), ALU.mult))
                    for t in range(SC_BLOCKS):
                        last = V.tensor_scalar(a_c[:, t, :], a_h[:, t, :], P_("sc_w", 2 * SC_BLOCKS + t, 1), None, ALU.mult)
                    link(last)
                    for tap in (1, 0):
                        s = SC_K - 1 - tap
                        for t in range(SC_BLOCKS):
                            last = V.scalar_tensor_tensor(a_c[:, t, s:], a_h[:, t, :SEQ - s], P_("sc_w", tap * SC_BLOCKS + t, 1),
                                                          a_c[:, t, s:], ALU.mult, ALU.add)
                        link(last)
                    V.tensor_tensor(flat(a_b), flat(a_b), flat(a_c), ALU.mult).then_inc(S["ya_f"], 1)
                    dve.wait_ge(S["ya_hi"], layer + 1)
                    rest(flat(y_lo[:, 0:4, :]), flat(a_b), flat(y_hi[:, 0:4, :]), S["ya_lo"])
                elif kind == "cb":
                    for n in (2 * g, 2 * g + 1):
                        dve.wait_ge(S["cb_ps"], GROUPS * layer + n + 1)
                        ps = bank(6 + n % 2)
                        V.tensor_tensor(cb[:, n, 0:P], ps[:, 0:P], C_("upto"), ALU.mult)
                        V.tensor_copy(cb[:, n, P:2 * P], ps[:, P:2 * P])
                        V.tensor_tensor(cb[:, n, 2 * P:], ps[:, 2 * P:3 * P], C_("upto"), ALU.mult).then_inc(S["cb_done"], 1)
                elif kind == "seg_in":
                    up_and_ones = C_("upto", 0, 2 * P)
                    for n in range(4):
                        head = 4 * g + n
                        V.tensor_scalar(seg_in0[:, n, :], up_and_ones, small[:, 7, 0, head:head + 1], None, ALU.mult)
                        last = V.tensor_scalar(seg_in1[:, n, :], C_("upto"), small[:, 7, 1, head:head + 1], None, ALU.mult)
                    last.then_inc(S["seg_in"], 1)
                elif kind == "score":
                    dve.wait_ge(S["dec_exp"], GROUPS * layer + g + 1)
                    dve.wait_ge(S["cb_done"], GROUPS * (layer + 1))
                    for n in range(4):
                        V.tensor_tensor(dec0[:, n, :], dec0[:, n, :], cb[:, g, 0:SEQ], ALU.mult)
                        last = V.tensor_tensor(dec1[:, n, :], dec1[:, n, :], cb[:, g, SEQ:], ALU.mult)
                    last.then_inc(S["score_done"], 1)
                elif kind == "y":
                    dve.wait_ge(S["y_ps"], GROUPS * layer + g + 1)
                    for t in range(2):
                        c = 2 * g + t
                        last = V.scalar_tensor_tensor(proj[:, XBC + c, :], proj[:, XBC + c, :], P_("d_skip", c, 1),
                                                      tiles(bank(7))[:, t, :], ALU.mult, ALU.add)
                    last.then_inc(S["y_done"], 1)
                elif kind == "y_sq":
                    dve.wait_ge(S["z_done"], layer + 1)
                    dve.wait_ge(S["y_done"], GROUPS * (layer + 1))
                    link(V.tensor_tensor(flat(y_b), flat(y_b), flat(proj[:, XBC:XBC + 8, :]), ALU.mult))
                    V.tensor_tensor(flat(y_sq), flat(y_b), flat(y_b), ALU.mult).then_inc(S["yb_sq"], 1)
                elif kind == "y_norm":
                    dve.wait_ge(S["yb_std"], layer + 1)
                    link(V.reciprocal(scr[:, 0:1024], scr[:, 0:1024]))
                    for c in range(8):
                        last = V.scalar_tensor_tensor(y_b[:, c, :], y_b[:, c, :], P_("norm_g", c, 1),
                                                      scr[:, (c // 2) * SEQ:(c // 2 + 1) * SEQ], ALU.mult, ALU.mult)
                        if c % 4 == 3:
                            last.then_inc(S["yb_f"], 1)
                    for half in range(2):
                        four = slice(4 * half, 4 * half + 4)
                        dve.wait_ge(S["yb_hi"], 2 * layer + half + 1)
                        rest(flat(yb_lo[:, four, :]), flat(y_b[:, four, :]), flat(yb_hi[:, four, :]), S["yb_lo"])

            u_, v_, pd = (proj[:, n:n + 4, :] for n in (GU, GV, PD))
            dve.sem_inc(lo_done, RING)
            dve.wait_ge(in_loaded, 32)
            for layer in range(DEPTH):
                dve.wait_ge(par_loaded, 16 * (layer + 1))
                if layer == 0:
                    split(0, 0)
                    split(0, 1)
                    for q in range(PAIRS):
                        squares(q)
                norm(2 * layer, P_("norm1"))
                u = 0
                for name, n in PLAN:
                    stage(name, layer)
                    for _ in range(n):
                        mixer_unit(layer, u)
                        u += 1
                for u in range(u, MIX_UNITS):
                    mixer_unit(layer, u)
                norm(2 * layer + 1, P_("norm2"))
                if layer == 0:
                    f0 = MIX_UNITS
                    V.memset(bank(0, 4), 0.0).then_inc(S["acc_zero"], 1)

                    def hidden(i):
                        V.tensor_tensor(ff_h, ff_g, bank(5), ALU.mult).then_inc(S["mult_done"], 1)
                        dve.wait_ge(S["mult_done"], i + 1)
                        V.tensor_copy(flat(hid_hi), ff_h).then_inc(S["hid_done"], 1)
                        dve.wait_ge(S["hid_done"], 2 * i + 1)
                        rest(flat(hid_lo), ff_h, flat(hid_hi), S["hid_done"])

                    split(f0, AHEAD)
                    split(f0, 1 + AHEAD)
                    dve.wait_ge(S["silu_done"], 1)
                    dve.wait_ge(unit_used, RING + f0 + 2)
                    hidden(0)
                    with dve.Fori(0, FF_STEPS - 1) as i:
                        for j in range(RING):
                            split(f0, 2 + j + AHEAD, i)
                        dve.wait_ge(S["silu_done"], i + 2)
                        dve.wait_ge(unit_used, RING + f0 + 2 + RING * i + 3)
                        hidden(i + 1)
                    split(f0, FF_UNITS - 1 + AHEAD)
                    dve.wait_ge(unit_used, RING + f0 + FF_UNITS)
                    for q in range(PAIRS):
                        added(q)

            NT = EXPERTS
            at = [0]

            def table(*shape):
                n = int(np.prod(shape))
                ap = route[:, at[0]:at[0] + n]
                at[0] += n
                return ap.rearrange("p (a b) -> p a b", a=shape[0]) if len(shape) == 2 else ap

            logit, top, comb, chosen, slot = (table(TT, NT) for _ in range(5))
            place_f, g1, g2 = table(TT, NT), table(TT, 1), table(TT, 1)
            first_e, other_e = table(TT, NT), table(TT, NT)
            count, blocks_e, cum = table(NT), table(NT), table(NT)
            expert_f, second = table(MAX_ITEMS), table(MAX_ITEMS)
            grid, one_hot, pickv = table(MAX_ITEMS, NT), table(MAX_ITEMS, NT), table(MAX_ITEMS, NT)
            item_slot, item_gate = table(TT, MAX_ITEMS), table(TT, MAX_ITEMS)
            assert at[0] <= 1536
            place = ints[:, 0:16].bitcast(u32).rearrange("p (t n) -> p t n", t=TT)
            dve.wait_ge(S["router_ps"], 1)
            link(V.tensor_copy(logit, bank(6)[:, 0:TT * NT].rearrange("p (t n) -> p t n", t=TT)))
            for t in range(TT):
                last = V.max(top[:, t, :], logit[:, t, :])
            link(last)
            V.tensor_tensor(small[:, 5, :, 0:1], top[:, :, 1:2], top[:, :, 0:1], ALU.subtract).then_inc(S["gap_in"], 1)
            for t in range(TT):
                last = V.max_index(place[:, t, :], top[:, t, :], logit[:, t, :])
            link(last)
            link(V.tensor_copy(place_f, place))
            dve.wait_ge(S["gap_exp"], 1)
            link(V.tensor_scalar(g2, small[:, 6, :, 0:1], 1.0, None, ALU.add))
            link(V.reciprocal(g1, g2))
            link(V.tensor_tensor(g2, g1, small[:, 6, :, 0:1], ALU.mult))
            for t in range(TT):
                V.tensor_scalar(first_e[:, t, :], C_("experts"), place_f[:, t, 0:1], None, ALU.is_equal)
                last = V.tensor_scalar(other_e[:, t, :], C_("experts"), place_f[:, t, 1:2], None, ALU.is_equal)
            link(last)
            V.tensor_tensor(chosen, first_e, other_e, ALU.add).then_inc(S["sel_done"], 1)
            for t in range(TT):
                last = V.tensor_scalar(comb[:, t, :], first_e[:, t, :], g1[:, t, :], None, ALU.mult)
            link(last)
            for t in range(TT):
                last = V.scalar_tensor_tensor(comb[:, t, :], other_e[:, t, :], g2[:, t, :], comb[:, t, :], ALU.mult, ALU.add)
            link(last)
            dve.wait_ge(S["pos_ps"], 1)
            link(V.tensor_copy(count, bank(6)[:, 2 * NT:3 * NT]))
            link(V.tensor_tensor(slot, bank(6)[:, 0:2 * NT].rearrange("p (t n) -> p t n", t=TT), chosen, ALU.mult))
            link(V.tensor_scalar(slot, slot, -1.0, None, ALU.add))
            link(V.tensor_scalar(cum, count, float(P) + 0.5, None, ALU.is_gt))
            link(V.scalar_tensor_tensor(blocks_e, count, 0.5, cum, ALU.is_gt, ALU.add))
            link(V.tensor_tensor_scan(cum, C_("ones", 0, NT), blocks_e, 0.0, ALU.mult, ALU.add))
            items = C_("items").rearrange("p (a b) -> p a b", a=MAX_ITEMS)
            link(V.tensor_tensor(grid, cum.rearrange("p (a b) -> p a b", a=1).broadcast_to([P, MAX_ITEMS, NT]), items, ALU.is_le))
            link(V.tensor_reduce(expert_f, grid, AX.X, ALU.add))
            link(V.memset(second, 0.0))
            link(V.tensor_tensor(second[:, 1:], expert_f[:, 1:], expert_f[:, :MAX_ITEMS - 1], ALU.is_equal))
            experts = C_("experts")
            for i in range(MAX_ITEMS):
                last = V.tensor_scalar(one_hot[:, i, :], experts, expert_f[:, i:i + 1], None, ALU.is_equal)
            link(last)
            for t in range(TT):
                for dst, of in ((item_slot, slot), (item_gate, comb)):
                    link(V.tensor_tensor(pickv, one_hot, of[:, t:t + 1, :].broadcast_to([P, MAX_ITEMS, NT]), ALU.mult))
                    link(V.tensor_reduce(dst[:, t, :], pickv, AX.X, ALU.add))
                link(V.scalar_tensor_tensor(item_slot[:, t, :], second, -float(P), item_slot[:, t, :], ALU.mult, ALU.add))
            V.tensor_copy(ints[:, 0:MAX_ITEMS], expert_f)
            V.tensor_scalar(ints[:, 31:32], cum[:, NT - 1:NT], -1.0, None, ALU.add).then_inc(S["items_done"], 1)
            for t in range(TT):
                dve.wait_ge(S["tok_hi_done"], t + 1)
                rest(tok_lo[:, t, :], bank(2 * t, 2), tok_hi[:, t, :], S["tok_lo_done"])
            dve.wait_ge(S["items_done"], 1)
            dve.sem_inc(S["item_added"], 1)
            last_item = dve.value_load(ints[0:1, 31:32], min_val=MIN_ITEMS - 1, max_val=MAX_ITEMS - 1)

            def split_e(v, item=0):
                dve.wait_ge(hi_done, MOE_U + v + item * ITEM_UNITS + 1)
                V.tensor_tensor(lo[:, v % RING, :], raw_e(v), hi[:, v % RING, :].bitcast(f32), ALU.subtract).then_inc(lo_done, 1)

            def picks(item):
                for t in range(TT):
                    last = V.tensor_scalar(pick[:, t, :], C_("iota"), item_slot[:, t, ds(item, 1)], None, ALU.is_equal)
                last.then_inc(S["pick_done"], 1)

            def gathered(item):
                dve.wait_ge(S["gather_ps"], 2 * item + 2)
                V.tensor_copy(flat(xg_lo[:, 4:8, :]), bank(4))
                V.tensor_copy(flat(xg_lo[:, 0:4, :]), bank(7)).then_inc(S["xg_lo_done"], 1)

            def add_half(item, n):
                dve.wait_ge(S["scatter_ps"], 2 * item + n + 1)
                four = slice(4 * n, 4 * n + 4)
                V.tensor_tensor(flat(x[:, four, :]), flat(x[:, four, :]), bank(2, 2), ALU.add).then_inc(S["item_added"], 1)

            def gated(item, c):
                dve.wait_ge(S["esilu_done"], item * CHUNKS + c + 1)
                V.tensor_tensor(ff_h, ff_g, bank(5), ALU.mult).then_inc(S["eh_done"], 1)

            def body(item, final):
                v = 4
                for c in range(CHUNKS):
                    ahead = not (final and c == CHUNKS - 1)
                    if ahead:
                        split_e(v + AHEAD, item)
                        v += 1
                    if c == 0:
                        dve.wait_ge(S["y_copied"], item + 1)
                        V.memset(bank(0, 2), 0.0).then_inc(S["y_zero"], 1)
                    dve.wait_ge(S["hT_hi_done"], item * CHUNKS + c + 1)
                    rest(flat(hT_lo), bank(6), flat(hT_hi), S["hT_lo_done"])
                    if ahead:
                        for _ in range(3):
                            split_e(v + AHEAD, item)
                            v += 1
                        dve.wait_ge(unit_used, RING + MOE_U + v + item * ITEM_UNITS)
                        gated(item, c + 1)
                        if c == CHUNKS - 2 and not final:
                            gathered(item + 1)
                    if c in (1, 2):
                        add_half(item, c - 1)
                    if c == 2:
                        for t in range(TT):
                            last = V.tensor_scalar(pick_g[:, t, :], C_("iota"), item_slot[:, t, ds(item, 1)],
                                                   item_gate[:, t, ds(item, 1)], ALU.is_equal, ALU.mult)
                        last.then_inc(S["pick_g_done"], 1)
                    if c == 4 and not final:
                        picks(item + 1)
                    for _ in range(2):
                        if not (final and v + AHEAD >= 4 + ITEM_UNITS - 4):
                            split_e(v + AHEAD, item)
                        v += 1

            V.memset(y_sb, 0.0)
            V.memset(pickT, 0.0)
            picks(0)
            for v in range(AHEAD):
                split_e(v)
            gathered(0)
            for v in range(AHEAD, AHEAD + 4):
                split_e(v)
            dve.wait_ge(unit_used, RING + MOE_U + 4)
            gated(0, 0)
            with dve.Fori(0, last_item) as item:
                body(item, False)
            body(last_item, True)
            for n in range(2):
                dve.wait_ge(S["item_added"], 2 * last_item + 3 + n)
                add_half(last_item + 1, n)
                dve.wait_ge(S["item_added"], 2 * last_item + 4 + n)
                squares(2 * n)
                squares(2 * n + 1)
            norm(2 * DEPTH, C_("final"))

        @block.tensor
        def _(pe):
            def mm(o, a, b_, start, stop, **k):
                return nc.tensor.matmul(o, a, b_, start=start, stop=stop, skip_group_check=True, **k)

            def product(o, slot, blk, a_hi, a_lo, start, stop):
                w = slice(blk * P, (blk + 1) * P)
                mm(o, hi[:, slot, w], a_hi, start, False)
                mm(o, hi[:, slot, w], a_lo, False, False)
                return mm(o, lo[:, slot, w], a_hi, False, stop)

            def tile_pair(b_out, first, j, ready=None):
                for t in range(2):
                    for k in range(KT):
                        if ready and t == 0 and k % 2 == 0:
                            pe.wait_ge(ready[0], ready[1] + k // 2 + 1)
                        last = product(bank(b_out)[:, t * SEQ:(t + 1) * SEQ], (first + j) % RING, KT * t + k,
                                       h_hi[:, k, :], h_lo[:, k, :], k == 0, k == KT - 1)
                last.then_inc(unit_used, 1)

            def split_is(u):
                pe.wait_ge(lo_done, RING + u + 1)

            def norm_part(n, q):
                pe.wait_ge(S["sq_done"], PAIRS * n + q + 1)
                for k in (2 * q, 2 * q + 1):
                    last = mm(bank(4)[:, 0:SEQ], C_("ones"), sq[:, k, :], k == 0, k == KT - 1)
                if q == PAIRS - 1:
                    last.then_inc(S["norm_sum"], 1)

            def early_unit(layer, u):
                b = base_of(layer)
                ends = {}
                for e in range(2 * KT):
                    end, count = early_event(layer, e)
                    ends[end] = count
                for blk in range(BLOCKS * (u - U_EARLY), BLOCKS * (u - U_EARLY + 1)):
                    tile, n = blk // EARLY_BLOCKS, blk % EARLY_BLOCKS
                    if n < len(EARLY) * KT:
                        if n == 0 and tile == 0:
                            pe.wait_ge(S["win_done"], IN_UNITS * (layer + 1))
                        elif n == 0:
                            pe.wait_ge(S["gate_done"], KT * layer + tile)
                        br, k, depth = n // KT, n % KT, KT
                        out_bank, a_hi, a_lo = br // 2, h_hi[:, k, :], h_lo[:, k, :]
                    else:
                        n -= len(EARLY) * KT
                        if n == 0 and tile == 0:
                            for ready in ("ya_lo", "yc_lo", "yd_lo"):
                                pe.wait_ge(S[ready], layer + 1)
                        elif n == 0:
                            pe.wait_ge(S["early_added"], KT * layer + tile)
                        br, k, depth = n // 4, n % 4, 4
                        out_bank, a_hi, a_lo = 2 + br // 2, y_hi[:, n, :], y_lo[:, n, :]
                    last = product(bank(out_bank)[:, (br % 2) * SEQ:(br % 2 + 1) * SEQ], (b + u) % RING, blk % BLOCKS,
                                   a_hi, a_lo, k == 0, k == depth - 1)
                    if (blk + 1) % BLOCKS == 0:
                        last.then_inc(unit_used, 1)
                    elif blk + 1 in ends:
                        last.then_inc(S["early_ps"], 1)

            def mixer_unit(layer, u):
                b = base_of(layer)
                split_is(b + u)
                if u < IN_UNITS:
                    n = IN_UNITS * layer + u
                    if n >= 4:
                        pe.wait_ge(S["win_done"], n - 3)
                    tile_pair(u % 4, b, u, (S["h_lo_done"], 2 * PAIRS * layer) if u == 0 else None)
                elif u < U_GB:
                    early_unit(layer, u)
                elif u < U_PB:
                    if u == U_GB:
                        pe.wait_ge(S["gate_done"], KT * (layer + 1))
                        pe.wait_ge(S["early_added"], KT * (layer + 1))
                    tile_pair(u - U_GB, b, u)
                elif u < U_OUT:
                    q = u - U_PB
                    if q == 0:
                        pe.wait_ge(S["yb_lo"], 2 * (layer + 1))
                    for t in range(2):
                        for k in range(KT):
                            last = product(bank(4 + q)[:, t * SEQ:(t + 1) * SEQ], (b + u) % RING, KT * t + k,
                                           yb_hi[:, k, :], yb_lo[:, k, :], k == 0, k == KT - 1)
                    last.then_inc(unit_used, 1)
                else:
                    q = u - U_OUT
                    tile_pair(q, b, u, (S["m_lo"], PAIRS * layer) if q == 0 else None)
                    if q >= 2:
                        norm_part(2 * layer + 1, q - 2)
                    if q == OUT_UNITS - 1:
                        norm_part(2 * layer + 1, 2)
                        norm_part(2 * layer + 1, 3)

            def stage(name, layer):
                kind, g = name.rstrip("0123"), int(name[-1]) if name[-1].isdigit() else 0
                if kind == "dt_in":
                    pe.wait_ge(S["h_done"], 2 * PAIRS * layer + PAIRS)
                    pe.wait_ge(par_loaded, 16 * (layer + 1))
                    w_dt = P_("w_dt").rearrange("p (k n) -> p k n", k=KT)
                    for t in range(TT):
                        for k in range(KT):
                            last = mm(bank(6)[:, t * HEADS:(t + 1) * HEADS], h[:, k, t * P:(t + 1) * P], w_dt[:, k, :], k == 0, k == KT - 1)
                    last.then_inc(S["dt_raw"], 1)
                elif kind == "xs_T":
                    pe.wait_ge(S["conv_done"], XBC_BLOCKS * layer + 8)
                    pe.wait_ge(S["a_sc"], layer + 1)
                    for t in range(TT):
                        for c in range(8):
                            last = nc.tensor.transpose(bank(6 - 2 * t + c // 4)[:, (c % 4) * P:(c % 4 + 1) * P],
                                                       proj[:, XBC + c, t * P:(t + 1) * P], C_("ident"))
                        last.then_inc(S["xs_T"], 1)
                elif kind == "mean":
                    pe.wait_ge(S["gelu_done"], 2 * layer + 1)
                    pe.wait_ge(S["xdt_done"], TT * (layer + 1))
                    for k in range(4):
                        last = mm(bank(7)[:, 0:SEQ], C_("ones"), v_[:, k, :], k == 0, k == 3)
                    last.then_inc(S["mean_sum"], 1)
                elif kind == "var":
                    pe.wait_ge(S["dev_sq"], layer + 1)
                    for k in range(4):
                        last = mm(bank(7)[:, 0:SEQ], C_("ones"), v_sq[:, k, :], k == 0, k == 3)
                    last.then_inc(S["var_sum"], 1)
                elif kind == "v_T":
                    pe.wait_ge(S["v_norm"], layer + 1)
                    for t in range(TT):
                        for n in range(4):
                            last = nc.tensor.transpose(bank(4 + t)[:, n * P:(n + 1) * P], v_[:, n, t * P:(t + 1) * P], C_("ident"))
                    last.then_inc(S["v_T"], 1)
                elif kind == "spatial":
                    pe.wait_ge(S["v_T_sb"], layer + 1)
                    pe.wait_ge(S["ws_masked"], layer + 1)
                    for n in range(4):
                        for t in range(TT):
                            at = (n % 2) * SEQ + t * P
                            last = mm(bank(6 + n // 2)[:, at:at + P], vT[:, t, n * P:(n + 1) * P], P_("ws", n * P, P), True, True)
                    last.then_inc(S["s_done"], 1)
                elif kind == "pool_out":
                    pe.wait_ge(S["pooled"], 4 * (layer + 1))
                    for n in range(4):
                        last = mm(bank(4 + n // 2)[:, (n % 2) * SEQ:(n % 2 + 1) * SEQ], P_("pool_map", n * P, P), pooled[:, n, :], True, True)
                    last.then_inc(S["pool_out"], 1)
                elif kind == "cb":
                    pe.wait_ge(S["conv_done"], XBC_BLOCKS * (layer + 1))
                    if g == 0:
                        pe.wait_ge(S["yc_f"], layer + 1)
                    else:
                        pe.wait_ge(S["cb_done"], GROUPS * layer + 2)
                    for n in (2 * g, 2 * g + 1):
                        b_t, c_t = proj[:, XBC + 8 + n, :], proj[:, XBC + 12 + n, :]
                        mm(bank(6 + n % 2)[:, 0:SEQ], b_t[:, 0:P], c_t, True, True)
                        mm(bank(6 + n % 2)[:, SEQ:SEQ + P], b_t[:, P:], c_t[:, P:], True, True).then_inc(S["cb_ps"], 1)
                elif kind == "seg":
                    pe.wait_ge(S["seg_in"], GROUPS * layer + g + 1)
                    pe.wait_ge(S["yd_f"], layer + 1)
                    pe.wait_ge(S["cb_done"], GROUPS * (layer + 1))
                    for n in range(2):
                        mm(bank(4 + n), C_("after"), flat(seg_in0[:, 2 * n:2 * n + 2, :]), True, False)
                        mm(tiles(bank(4 + n))[:, :, P:], C_("ones"), seg_in1[:, 2 * n:2 * n + 2, :], False, True)
                    mm(bank(6), C_("after"), flat(seg_in1), True, True).then_inc(S["seg_done"], 1)
                elif kind == "y":
                    pe.wait_ge(S["score_done"], GROUPS * layer + g + 1)
                    if layer or g:
                        pe.wait_ge(S["y_done"], GROUPS * layer + g)
                    for n in range(4):
                        head = 4 * g + n
                        o = bank(7)[HEAD_DIM * (n % 2):HEAD_DIM * (n % 2 + 1), (n // 2) * SEQ:(n // 2 + 1) * SEQ]
                        heads = slice(head * HEAD_DIM, (head + 1) * HEAD_DIM)
                        mm(o, xdt[:, 0, heads], dec0[:, n, :], True, False)
                        last = mm(o[:, P:], xdt[:, 1, heads], dec1[:, n, :], False, True)
                    last.then_inc(S["y_ps"], 1)
                elif kind == "y_sum":
                    pe.wait_ge(S["yb_sq"], layer + 1)
                    for n in range(GROUPS):
                        for t in range(2):
                            last = mm(bank(4 + n // 2)[:, (n % 2) * SEQ:(n % 2 + 1) * SEQ], C_("ones"), y_sq[:, 2 * n + t, :], t == 0, t == 1)
                    last.then_inc(S["yb_sum"], 1)

            v_ = proj[:, GV:GV + 4, :]
            pe.sem_inc(unit_used, RING)
            pe.wait_ge(in_loaded, 32)
            for layer in range(DEPTH):
                for q in range(PAIRS):
                    norm_part(2 * layer, q)
                u = 0
                for name, n in PLAN:
                    stage(name, layer)
                    for _ in range(n):
                        mixer_unit(layer, u)
                        u += 1
                for u in range(u, MIX_UNITS):
                    mixer_unit(layer, u)
                if layer == 0:
                    f0 = MIX_UNITS

                    def down(j, i=0):
                        for f in range(2):
                            for m in range(KT):
                                last = product(bank(m // 2)[:, (m % 2) * SEQ:(m % 2 + 1) * SEQ], (f0 + j) % RING, f * KT + m,
                                               hid_hi[:, f, :], hid_lo[:, f, :], False, False)
                        last.then_inc(unit_used, 1)

                    split_is(f0)
                    pe.wait_ge(S["std_done"], 2)
                    tile_pair(4, f0, 0, (S["h_lo_done"], PAIRS))
                    split_is(f0 + 1)
                    tile_pair(5, f0, 1)
                    pe.wait_ge(S["acc_zero"], 1)
                    with pe.Fori(0, FF_STEPS - 1) as i:
                        split_is(f0 + 2 + RING * i)
                        pe.wait_ge(S["silu_done"], i + 1)
                        tile_pair(4, f0, 2)
                        split_is(f0 + 3 + RING * i)
                        pe.wait_ge(S["hid_done"], 2 * i + 2)
                        down(3)
                        split_is(f0 + 4 + RING * i)
                        tile_pair(5, f0, 4)
                    split_is(f0 + FF_UNITS - 1)
                    pe.wait_ge(S["hid_done"], 2 * FF_STEPS)
                    down(FF_UNITS - 1)

            pe.wait_ge(S["h_done"], 2 * PAIRS * DEPTH)
            r_w = C_("router").rearrange("p (k n) -> p k n", k=KT)
            for t in range(TT):
                for k in range(KT):
                    last = mm(bank(6)[:, t * EXPERTS:(t + 1) * EXPERTS], h[:, k, t * P:(t + 1) * P], r_w[:, k, :], k == 0, k == KT - 1)
            last.then_inc(S["router_ps"], 1)
            for t in range(TT):
                for k in range(KT):
                    last = nc.tensor.transpose(bank(2 * t + k // 4)[:, (k % 4) * P:(k % 4 + 1) * P], h[:, k, t * P:(t + 1) * P], C_("ident"))
                last.then_inc(S["tok_ps"], 1)
            pe.wait_ge(S["sel_done"], 1)
            chosen = route[:, 3 * TT * EXPERTS:4 * TT * EXPERTS].rearrange("p (t n) -> p t n", t=TT)
            mm(bank(6)[:, 0:EXPERTS], C_("upto"), chosen[:, 0, :], True, True)
            mm(bank(6)[:, EXPERTS:2 * EXPERTS], C_("upto"), chosen[:, 1, :], True, False)
            mm(bank(6)[:, EXPERTS:2 * EXPERTS], C_("ones"), chosen[:, 0, :], False, True)
            mm(bank(6)[:, 2 * EXPERTS:3 * EXPERTS], C_("ones"), chosen[:, 0, :], True, False)
            mm(bank(6)[:, 2 * EXPERTS:3 * EXPERTS], C_("ones"), chosen[:, 1, :], False, True).then_inc(S["pos_ps"], 1)
            pe.wait_ge(S["tok_lo_done"], TT)
            pe.wait_ge(S["items_done"], 1)
            last_item = pe.value_load(ints[0:1, 31:32], min_val=MIN_ITEMS - 1, max_val=MAX_ITEMS - 1)

            def split_e_is(v, item):
                pe.wait_ge(lo_done, RING + MOE_U + v + item * ITEM_UNITS + 1)

            def up(o, v, half, item=0):
                split_e_is(v, item)
                for k in range(4):
                    w, kk = slice(k * CHUNK_F, (k + 1) * CHUNK_F), 4 * half + k
                    mm(o, xg_hi[:, kk, :], hi[:, v % RING, w], kk == 0, False)
                    mm(o, xg_hi[:, kk, :], lo[:, v % RING, w], False, False)
                    last = mm(o, xg_lo[:, kk, :], hi[:, v % RING, w], False, kk == KT - 1)
                last.then_inc(unit_used, 1)

            def down(v, half, item):
                split_e_is(v, item)
                for f in range(2):
                    for n in range(2):
                        w = slice(f * D + n * 512, f * D + (n + 1) * 512)
                        mm(bank(n), hT_hi[:, 2 * half + f, :], hi[:, v % RING, w], False, False)
                        mm(bank(n), hT_hi[:, 2 * half + f, :], lo[:, v % RING, w], False, False)
                        last = mm(bank(n), hT_lo[:, 2 * half + f, :], hi[:, v % RING, w], False, False)
                last.then_inc(unit_used, 1)

            def gather(item):
                pe.wait_ge(S["pick_done"], item + 1)
                for part, tok in enumerate((tok_hi, tok_lo)):
                    for k in range(KT):
                        o = bank(((2, 3), (7, 4))[part][k // 4])[:, (k % 4) * P:(k % 4 + 1) * P]
                        mm(o, tok[:, 0, k * P:(k + 1) * P], pick[:, 0, :], True, False)
                        last = mm(o, tok[:, 1, k * P:(k + 1) * P], pick[:, 1, :], False, True)
                    last.then_inc(S["gather_ps"], 1)

            def scatter(item, n):
                for m in range(4):
                    k = 4 * n + m
                    last = mm(bank(2 + m // 2)[:, (m % 2) * SEQ:(m % 2 + 1) * SEQ], y_sb[:, k * P:(k + 1) * P], pickT, True, True)
                last.then_inc(S["scatter_ps"], 1)

            def body(item, final):
                v = 4
                for c in range(CHUNKS):
                    ahead = not (final and c == CHUNKS - 1)
                    if ahead:
                        pe.wait_ge(S["esilu_done"], item * CHUNKS + c + 1)
                        if c == CHUNKS - 1:
                            pe.wait_ge(S["xg_hi_done"], item + 2)
                            pe.wait_ge(S["xg_lo_done"], item + 2)
                        up(bank(4), v, 0, item)
                    pe.wait_ge(S["eh_done"], item * CHUNKS + c + 1)
                    for f in range(4):
                        last = nc.tensor.transpose(bank(6)[:, f * P:(f + 1) * P], ff_h[:, f * P:(f + 1) * P], C_("ident"))
                    last.then_inc(S["hT_ps"], 1)
                    if ahead:
                        up(bank(4), v + 1, 1, item)
                        up(bank(5), v + 2, 0, item)
                        up(bank(5), v + 3, 1, item)
                        v += 4
                    if c == 1:
                        pe.wait_ge(S["y_copied"], item + 1)
                        scatter(item, 0)
                    if c == 2:
                        pe.wait_ge(S["item_added"], 2 * item + 2)
                        scatter(item, 1)
                    if c == 3:
                        pe.wait_ge(S["pick_g_done"], item + 1)
                        for t in range(TT):
                            last = nc.tensor.transpose(bank(7)[:, t * P:(t + 1) * P], pick_g[:, t, :], C_("ident"))
                        last.then_inc(S["pickT_ps"], 1)
                    if c == CHUNKS - 2 and not final:
                        pe.wait_ge(S["item_added"], 2 * item + 3)
                        pe.wait_ge(S["pickT_done"], item + 1)
                        pe.wait_ge(S["esilu_done"], item * CHUNKS + CHUNKS)
                        gather(item + 1)
                    if c == 0:
                        pe.wait_ge(S["y_zero"], item + 1)
                    pe.wait_ge(S["hT_lo_done"], item * CHUNKS + c + 1)
                    down(v, 0, item)
                    down(v + 1, 1, item)
                    v += 2

            gather(0)
            pe.wait_ge(S["xg_hi_done"], 1)
            pe.wait_ge(S["xg_lo_done"], 1)
            for v in range(4):
                up(bank(4 + v // 2), v, v % 2)
            with pe.Fori(0, last_item) as item:
                body(item, False)
            body(last_item, True)
            pe.wait_ge(S["y_copied"], last_item + 2)
            scatter(last_item + 1, 0)
            pe.wait_ge(S["item_added"], 2 * last_item + 4)
            scatter(last_item + 1, 1)
            for q in range(PAIRS):
                norm_part(2 * DEPTH, q)


def blocks_of(w):
    k, n = w.shape
    return w.reshape(k // P, P, n // P, P).transpose(0, 2, 1, 3)


def units_of(blocks):
    a = np.asarray(blocks).reshape(-1, BLOCKS, P, P)
    return a.transpose(0, 2, 1, 3).reshape(-1, P, UNIT)


def by_output(w):
    return blocks_of(w).transpose(1, 0, 2, 3).reshape(-1, P, P)


def per_channel(v):
    return v.reshape(-1, P).T


def mixer_units(q, layer):
    w = q["w_in"][layer]
    n_a, n_b, z = 3 * 512, 1024 + 2048 + HEADS, 1024
    b0 = n_a
    c0 = n_a + n_b
    d0 = c0 + 1024
    order = [w[:, b0 + z:b0 + z + 2048], w[:, c0:c0 + 1024], w[:, d0:d0 + 512], w[:, 0:n_a], w[:, b0:b0 + z]]
    parts = [by_output(np.concatenate(order, 1))]
    gate = q["w_gate"][layer].reshape(D, 4, D)
    early = [(blocks_of(gate[:, n]), blocks_of(q[name][layer])) for n, name in ((0, "w_br_a"), (2, "w_br_c"), (3, "w_br_d"))]
    parts.append(np.concatenate([g_or_br[n][:, j] for j in range(KT) for n in (0, 1) for g_or_br in early]))
    parts += [by_output(gate[:, 1]), by_output(q["w_br_b"][layer]), by_output(q["w_out"][layer])]
    return np.concatenate([units_of(p) for p in parts])


def dense_units(q):
    g, u = (by_output(q[n][0]).reshape(-1, BLOCKS, P, P) for n in ("ffn_wg", "ffn_wu"))
    d = blocks_of(q["ffn_wd"][0]).reshape(-1, BLOCKS, P, P)
    seq = [g[0], u[0]]
    for f in range(FF_STEPS - 1):
        seq += [g[f + 1], d[f], u[f + 1]]
    return units_of(np.concatenate(seq + [d[-1]]))


def expert_units(q):
    def up(w):
        return w.reshape(EXPERTS, 2, 4, P, CHUNKS, CHUNK_F).transpose(0, 4, 1, 3, 2, 5).reshape(EXPERTS, CHUNKS, 2, P, UNIT)

    g, u = up(q["moe_wg"][0]), up(q["moe_wu"][0])
    d = q["moe_wd"][0].reshape(EXPERTS, CHUNKS, 2, 2, P, D).transpose(0, 1, 2, 4, 3, 5).reshape(EXPERTS, CHUNKS, 2, P, UNIT)
    out = np.empty((EXPERTS, ITEM_UNITS, P, UNIT), np.float32)
    out[:, 0:2], out[:, 2:4] = g[:, 0], u[:, 0]
    for c in range(CHUNKS - 1):
        at = 4 + 6 * c
        out[:, at:at + 2], out[:, at + 2:at + 4], out[:, at + 4:at + 6] = g[:, c + 1], u[:, c + 1], d[:, c]
    out[:, ITEM_UNITS - 2:] = d[:, CHUNKS - 1]
    return out.reshape(-1, P, UNIT)


def params(q, layer):
    def rows(v):
        return np.broadcast_to(v.reshape(1, -1), (P, v.size))

    w_dt = q["w_in"][layer][:, 3 * 512 + 3072:3 * 512 + 3072 + HEADS].reshape(KT, P, HEADS).transpose(1, 0, 2).reshape(P, -1)
    parts = [per_channel(q["norm1_g"][layer]), per_channel(q["norm2_g"][layer]), per_channel(q["sc_conv_w"][layer]),
             per_channel(q["ssm_conv_w"][layer]), per_channel(q["ssm_conv_b"][layer]), rows(q["ssm_dt_bias"][layer]),
             rows(q["ssm_a_log"][layer]), per_channel(np.repeat(q["ssm_d"][layer], HEAD_DIM)), per_channel(q["ssm_norm_g"][layer]),
             per_channel(q["gm_ln_g"][layer]), per_channel(q["gm_ln_b"][layer]), per_channel(q["pool_scale"][layer]), w_dt,
             q["gm_ws"][layer].transpose(2, 0, 1).reshape(P, -1), rows(q["gm_bias"][layer]),
             q["pool_map"][layer].transpose(1, 0, 2).reshape(P, -1)]
    return np.concatenate(parts, 1)


def constants(q):
    r = np.arange(P)
    f = lambda a: np.asarray(a, np.float32)
    inv = np.stack([1.0 / np.minimum(np.arange(1, 17), w) for w in (2, 4, 8, 16)])
    wide = lambda a: np.broadcast_to(f(a).reshape(1, -1), (P, np.size(a)))
    parts = [f(np.eye(P)), f(r[:, None] <= r[None, :]), f(np.ones((P, P))), f(r[:, None] > r[None, :]), wide(r), wide(inv),
             wide(np.arange(EXPERTS)), wide(np.repeat(np.arange(MAX_ITEMS), EXPERTS)), wide([EPS]), per_channel(q["final_g"]),
             q["router_w"][0].reshape(KT, P, EXPERTS).transpose(1, 0, 2).reshape(P, -1)]
    return np.concatenate(parts, 1)


def kernel(**inputs):
    import concourse.bacc as bacc
    from concourse.bass_utils import run_bass_kernel_spmd

    q = {k: np.asarray(v) for k, v in inputs.items()}
    arrays = {
        "x_in": q["x"][0].T.reshape(KT, P, SEQ).transpose(1, 0, 2),
        "par_in": np.stack([params(q, layer) for layer in range(DEPTH)]),
        "con_in": constants(q),
        "mix_w": np.stack([mixer_units(q, layer) for layer in range(DEPTH)]),
        "ff_w": dense_units(q),
        "moe_w": expert_units(q),
    }
    arrays = {k: np.ascontiguousarray(v) for k, v in arrays.items()}
    nc = bacc.Bacc("TRN2", target_bir_lowering=False, num_devices=1)
    aps = [nc.dram_tensor(k, a.shape, mybir.dt.from_np(a.dtype), kind="ExternalInput").ap() for k, a in arrays.items()]
    out = nc.dram_tensor("out", (P, KT, SEQ), mybir.dt.float32, kind="ExternalOutput").ap()
    trunk(nc, *aps, out)
    r = run_bass_kernel_spmd(nc, [arrays], core_ids=[0])
    return r.results[0]["out"].transpose(1, 0, 2).reshape(D, SEQ).T.reshape(1, SEQ, D)
```

```python
from contextlib import ExitStack

import numpy as np
import concourse.bass as bass
from concourse import mybir

D = 1024
SEQ = 256
DEPTH = 2
P = 128
KT = D // P
TT = SEQ // P
UNIT = 2048
BLOCKS = UNIT // P
EPS = 1e-6
HEADS, HEAD_DIM, GROUPS = 16, 64, 4
SC_BLOCKS, XBC_BLOCKS, Z_BLOCKS = 4, 16, 8
D_FF, D_FFE, EXPERTS = 2816, 3584, 8
SC_K, SSM_K = 3, 4
FF_STEPS = D_FF // (2 * P)
CHUNK_F = 512
CHUNKS = D_FFE // CHUNK_F
ITEM_UNITS = 6 * CHUNKS
MAX_ITEMS = EXPERTS + (2 * SEQ) // (P + 1)
MIN_ITEMS = 2 * SEQ // P
RING = 3
AHEAD = 2

XBC, GU, GV, PD, A_H, A_B, A_C, ZB = 0, 16, 20, 24, 28, 32, 36, 40
N_PROJ = 48
IN_UNITS = N_PROJ // 2
EARLY = ("a", "c", "d")
EARLY_BLOCKS = len(EARLY) * (KT + 4)
EARLY_UNITS = KT * EARLY_BLOCKS // BLOCKS
B_UNITS = KT * KT // BLOCKS
OUT_UNITS = KT * KT // BLOCKS
U_EARLY = IN_UNITS
U_GB = U_EARLY + EARLY_UNITS
U_PB = U_GB + B_UNITS
U_OUT = U_PB + B_UNITS
MIX_UNITS = U_OUT + OUT_UNITS
FF_UNITS = 3 * FF_STEPS
RAW_E = 6
PLAN = (
    ("dt_row", 1), ("conv0", 1), ("dt_in", 1), ("conv1", 1), ("dt_log", 1), ("conv2", 1), ("dt_out", 1), ("conv3", 1),
    ("xs_T", 1), ("xdt", 1), ("conv4", 1), ("conv5", 1), ("gelu", 1), ("conv6", 1), ("mean", 1), ("conv7", 1), ("var", 1),
    ("ln", 1), ("v_T", 1), ("spatial", 2), ("pool_out", 3), ("short", 1), ("z", 1), ("cb0", 1), ("cb1", 3),
    ("seg0", 1), ("score0", 1), ("y0", 1), ("seg1", 1), ("score1", 1), ("y1", 1),
    ("seg2", 1), ("score2", 1), ("y2", 1), ("seg3", 1), ("score3", 1), ("y3", 0),
    ("y_sq", 1), ("y_sum", 1), ("y_spread", 0), ("y_norm", 0))


def early_event(layer, e):
    ends = [EARLY_BLOCKS * (n // 2) + (len(EARLY) * KT if n % 2 == 0 else EARLY_BLOCKS) for n in range(2 * KT)]
    own = [n for n in ends if n % BLOCKS]
    return ends[e], (own.index(ends[e]) + 1 + len(own) * layer if ends[e] % BLOCKS else None)


def columns(*parts):
    at, out = 0, {}
    for name, n in parts:
        out[name] = (at, at + n)
        at += n
    return out, at


PAR, N_PAR = columns(
    ("norm1", KT), ("norm2", KT), ("sc_w", SC_K * SC_BLOCKS), ("ssm_w", SSM_K * XBC_BLOCKS),
    ("ssm_b", XBC_BLOCKS), ("dt_bias", HEADS), ("a_log", HEADS), ("d_skip", 8), ("norm_g", 8),
    ("ln_g", 4), ("ln_b", 4), ("pool_scale", 4), ("w_dt", KT * HEADS), ("ws", 4 * P),
    ("gm_bias", 4 * P), ("pool_map", 4 * P))
PAR_FIRST = PAR["ws"][0]
CON, N_CON = columns(
    ("ident", P), ("upto", P), ("ones", P), ("after", P), ("iota", P), ("inv_count", 64),
    ("experts", EXPERTS), ("items", MAX_ITEMS * EXPERTS), ("eps", 1), ("final", KT), ("router", KT * EXPERTS))


def trunk(nc, x_in, par_in, con_in, mix_w, ff_w, moe_w, out):
    f32, f32r, i32, u32 = mybir.dt.float32, mybir.dt.float32r, mybir.dt.int32, mybir.dt.uint32
    ACT, ALU, AX = mybir.ActivationFunctionType, mybir.AluOpType, mybir.AxisListType
    ds = bass.ds
    ctx = ExitStack()
    with ctx:
        def sb(name, shape, dt=f32):
            return ctx.enter_context(nc.sbuf_tensor(name, shape, dt))

        def sem(name):
            return ctx.enter_context(nc.semaphore(name))

        raw = sb("weight_raw", [P, RING, UNIT])
        hi = sb("weight_hi", [P, RING, UNIT], f32r)
        lo = sb("weight_lo", [P, RING, UNIT], f32r)
        x = sb("x", [P, KT, SEQ])
        with nc.sbuf_tensor("first_raw", [P, 2, UNIT], f32) as first_raw:
            pass
        h_hi = sb("h_hi", [P, KT, SEQ], f32r)
        h_lo = sb("h_lo", [P, KT, SEQ], f32r)
        with nc.sbuf_tensor("proj_r", [P, N_PROJ, SEQ], f32r) as proj_r:
            pass
        proj = sb("proj", [P, N_PROJ, SEQ])
        with nc.sbuf_tensor("pool_tmp", [P, 24, SEQ], f32) as pool_tmp:
            pass
        y_hi = sb("y_hi", [P, 12, SEQ], f32r)
        y_lo = sb("y_lo", [P, 12, SEQ], f32r)
        with nc.sbuf_tensor("tmp", [P, 16, SEQ], f32) as tmp:
            pass
        yb_hi = sb("yb_hi", [P, 8, SEQ], f32r)
        yb_lo = sb("yb_lo", [P, 8, SEQ], f32r)
        par = sb("par", [P, N_PAR])
        con = sb("con", [P, N_CON])
        scr = sb("scr", [P, 1024])
        small = sb("small", [P, 12, 2, HEADS])
        da_hi, da_lo = (sb(n, [P, TT, HEADS], f32r) for n in ("da_hi", "da_lo"))
        after_r, ones_r = (sb(n, [P, P], f32r) for n in ("after_r", "ones_r"))
        stat = sb("stat", [P, 2 * GROUPS])
        row = sb("row", [HEADS, SEQ])
        ints = sb("ints", [P, 32], i32)
        PS = ctx.enter_context(nc.psum_tensor("psum", [P, 8, 512], f32))

        def bank(b, n=1):
            return PS[:, b:b + n, :].rearrange("p b n -> p (b n)")

        def tiles(ap, n=SEQ):
            return ap.rearrange("p (t n) -> p t n", n=n)

        def flat(ap):
            return ap.rearrange("p t n -> p (t n)")

        def P_(name, i=0, n=None):
            a, b = PAR[name]
            return par[:, a + i:(b if n is None else a + i + n)]

        def C_(name, i=0, n=None):
            a, b = CON[name]
            return con[:, a + i:(b if n is None else a + i + n)]

        sq, h = proj[:, 24:32, :], proj[:, 32:40, :]
        xdt = flat(tmp[:, 0:8, :]).rearrange("p (t c) -> p t c", t=TT)
        cb = flat(proj[:, 24:30, :]).rearrange("p (g l) -> p g l", g=GROUPS)
        seg_in0 = proj_r[:, 30:34, :], proj_r[:, 8:12, :]
        seg_in1 = tuple(tiles(flat(proj_r[:, n:n + 2, :]), P) for n in (34, 12))
        dec0 = tiles(flat(proj[:, 36:40, :]))
        dec1 = tiles(scr[:, 0:512], P)
        merged, gate_b, y_b = proj[:, 16:24, :], proj[:, 24:32, :], proj[:, ZB:ZB + 8, :]
        y_sq = proj[:, 8:16, :]
        vT = flat(tmp[:, 8:12, :]).rearrange("p (t c) -> p t c", t=TT)
        v_sq = tmp[:, 12:16, :]
        sums_a, sums_b, pooled = pool_tmp[:, 0:4, :], pool_tmp[:, 12:16, :], pool_tmp[:, 20:24, :]
        v_diag, v_mean = tmp[:, 8, :], tmp[:, 9, :]
        diag = scr[:, 0:SEQ]

        def gate_of(tile):
            at = 8 + 3 * (tile % 2)
            return tmp[:, at:at + 3, :]

        ff_g, ff_h = flat(proj[:, 40:42, :]), flat(proj[:, 42:44, :])
        pick_g, pickT = tiles(flat(proj[:, 44:45, :]), P), proj[:, 45, :]
        y_sb = scr[:, 0:D]
        hid_hi, hid_lo = y_hi[:, 0:2, :], y_lo[:, 0:2, :]
        tok_hi, tok_lo = (flat(t[:]).rearrange("p (t c) -> p t c", t=TT) for t in (yb_hi, yb_lo))
        xg_hi, xg_lo = (tiles(flat(t[:, 0:4, :]), P) for t in (y_hi, y_lo))
        hT_hi, hT_lo = (tiles(flat(t[:, 4:6, :]), P) for t in (y_hi, y_lo))
        pick = tiles(flat(y_hi[:, 6:7, :]), P)
        route = par[:, 0:1536]
        NT = EXPERTS
        at = [0]

        def table(*shape):
            n = int(np.prod(shape))
            ap = route[:, at[0]:at[0] + n]
            at[0] += n
            return ap.rearrange("p (a b) -> p a b", a=shape[0]) if len(shape) == 2 else ap

        logit, top, comb, chosen, slot = (table(TT, NT) for _ in range(5))
        place_f, g1, g2 = table(TT, NT), table(TT, 1), table(TT, 1)
        first_e, other_e = table(TT, NT), table(TT, NT)
        count, blocks_e, cum = table(NT), table(NT), table(NT)
        expert_f, second = table(MAX_ITEMS), table(MAX_ITEMS)
        grid, one_hot, pickv = table(MAX_ITEMS, NT), table(MAX_ITEMS, NT), table(MAX_ITEMS, NT)
        item_slot, item_gate = table(TT, MAX_ITEMS), table(TT, MAX_ITEMS)
        assert at[0] <= 1536
        outside = {0: flat(sq), 1: first_raw[:, 0, :], 4: first_raw[:, 1, :], 5: flat(h)}

        def raw_e(v):
            if v in outside:
                return outside[v]
            n = v % RAW_E
            return raw[:, n, :] if n < RING else flat(proj[:, 8 * (n - RING):8 * (n - RING) + 8, :])

        raw_landed = [sem(f"raw_landed{i}") for i in range(RING)]
        raw_e_landed = [sem(f"raw_e_landed{i}") for i in range(RAW_E)]
        hi_done, lo_done, unit_used = sem("hi_done"), sem("lo_done"), sem("unit_used")
        x_loaded = [sem(f"x_loaded{i}") for i in range(2)]
        con_loaded, par_loaded, par_rest_loaded, stored = (sem(n) for n in ("con_loaded", "par_loaded", "par_rest_loaded", "stored"))
        outside_landed = {v: sem(f"outside_landed{v}") for v in outside}
        dve_order, gp_order = sem("dve_order"), sem("gp_order")
        S = {n: sem(n) for n in (
            "sq_done", "sq_added", "norm_sum", "std_done", "diag_done", "rstd_ps", "h_done", "h_hi_done", "h_lo_done", "dt_sum", "dt_row", "dt_raw",
            "win_done", "gelu_done", "mean_sum", "dev_sq", "var_sum", "v_std", "v_diag", "v_rstd", "v_norm", "v_T", "v_T_sb",
            "ws_masked", "s_done", "pooled", "pool_out", "a_sc", "a_exp", "da_done", "masks_done", "dt_w", "dt_ln", "conv_acc", "conv_done",
            "z_done", "xs_T", "xdt_done", "cb_ps", "cb_done", "seg_in", "seg_done", "dec_exp", "score_done", "y_ps",
            "y_done", "yb_sq", "yb_sq_added", "yb_sum", "yb_std", "yb_diag", "yb_rstd", "ya_f", "ya_hi", "ya_lo", "yc_f",
            "yc_hi", "yc_lo", "yd_f", "yd_hi", "yd_lo", "yb_f", "yb_hi", "yb_lo", "early_ps", "gate_done", "early_added", "gate_b_done", "merge_done",
            "m_hi", "m_lo", "silu_done", "mult_done", "hid_done",
            "acc_zero", "ff_bank", "y_bank", "router_sum", "router_row", "router_ps", "gap_exp", "gap_in", "sel_done",
            "pos_ps", "items_done", "tables_done", "zeros_done",
            "tok_ps", "tok_hi_done", "tok_lo_done", "pick_done", "pick_g_done", "first_gather", "gather_ps", "pickT_ps", "pickT_done",
            "xg_hi_done", "xg_lo_done", "hT_ps", "hT_hi_done", "hT_lo_done", "esilu_done", "eh_done",
            "y_zero", "y_copied", "scatter_ps", "item_added", "final_done")}
        PAIRS = KT // 2

        MOE_U = MIX_UNITS + FF_UNITS + MIX_UNITS

        def base_of(layer):
            return layer * (MIX_UNITS + FF_UNITS)

        def last_split(layer, u):
            return layer == DEPTH - 1 and u + AHEAD >= MIX_UNITS

        block = ctx.enter_context(nc.Block())

        @block.sync
        def _(sp):
            def load(src, first, j, i=0):
                u = first + j + RING * i
                sp.wait_ge(lo_done, u + 1)
                sp.dma_start(raw[:, (first + j) % RING, :], src).then_inc(raw_landed[(first + j) % RING], 16)

            for half in range(2):
                sp.dma_start(x[:, 4 * half:4 * half + 4, :], x_in[:, 4 * half:4 * half + 4, :]).then_inc(x_loaded[half], 16)
            sp.dma_start(con[:], con_in).then_inc(con_loaded, 16)
            for layer in range(DEPTH):
                if layer:
                    sp.wait_ge(S["yb_lo"], 2 * layer)
                    sp.wait_ge(S["h_done"], 2 * PAIRS * layer)
                sp.dma_start(par[:, :PAR_FIRST], par_in[layer, :, :PAR_FIRST]).then_inc(par_loaded, 16)
                for j in range(RING):
                    load(mix_w[layer, j, :, :], base_of(layer), j)
                sp.dma_start(par[:, PAR_FIRST:], par_in[layer, :, PAR_FIRST:]).then_inc(par_rest_loaded, 16)
                with sp.Fori(1, MIX_UNITS // RING) as i:
                    for j in range(RING):
                        load(mix_w[layer, ds(i * RING + j, 1), :, :].rearrange("a p n -> (a p) n"), base_of(layer), j, i)
                if layer == 0:
                    with sp.Fori(0, FF_UNITS // RING) as i:
                        for j in range(RING):
                            load(ff_w[ds(i * RING + j, 1), :, :].rearrange("a p n -> (a p) n"), MIX_UNITS, j, i)

            def load_first(v):
                landed = outside_landed[v] if v in outside else raw_e_landed[v % RAW_E]
                sp.dma_start(raw_e(v), moe_w[v, :, :]).then_inc(landed, 16)

            sp.wait_ge(S["yb_sum"], DEPTH)
            load_first(3)
            load_first(10)
            sp.wait_ge(S["m_lo"], PAIRS * DEPTH)
            load_first(11)
            assert MOE_U % RING == 0
            for v in (6, 7, 2):
                sp.wait_ge(lo_done, MOE_U + v % RAW_E + 1)
                load_first(v)
            sp.wait_ge(S["norm_sum"], 2 * DEPTH)
            load_first(0)
            sp.wait_ge(unit_used, RING + MOE_U)
            load_first(1)
            load_first(4)
            sp.wait_ge(S["tok_ps"], TT)
            load_first(5)

            def load_e(unit, v, after):
                sp.wait_ge(lo_done, RING + MOE_U + after + 1)
                sp.dma_start(raw_e(v), moe_w[ds(unit, 1), :, :].rearrange("a p n -> (a p) n")).then_inc(raw_e_landed[v % RAW_E], 16)

            for v in (8, 9):
                load_e(v, v, v - RAW_E)
            sp.wait_ge(S["items_done"], 1)
            last_item = sp.value_load(ints[0:1, 31:32], min_val=MIN_ITEMS - 1, max_val=MAX_ITEMS - 1)
            with sp.Fori(0, last_item) as item:
                expert = sp.value_load(ints[0:1, ds(item, 1)], min_val=0, max_val=EXPERTS - 1)
                following = sp.value_load(ints[0:1, ds(item + 1, 1)], min_val=0, max_val=EXPERTS - 1)
                with sp.Fori(0, 4) as i:
                    for j in range(6):
                        load_e(expert * ITEM_UNITS + 12 + 6 * i + j, 12 + j, item * ITEM_UNITS + 6 + 6 * i + j)
                for j in range(4):
                    load_e(expert * ITEM_UNITS + 36 + j, 36 + j, item * ITEM_UNITS + 30 + j)
                for j in range(4):
                    load_e(following * ITEM_UNITS + j, 40 + j, item * ITEM_UNITS + 34 + j)
                for j in range(2):
                    load_e(expert * ITEM_UNITS + 40 + j, 44 + j, item * ITEM_UNITS + 38 + j)
                for j in range(8):
                    load_e(following * ITEM_UNITS + 4 + j, 46 + j, item * ITEM_UNITS + 40 + j)
            expert = sp.value_load(ints[0:1, ds(last_item, 1)], min_val=0, max_val=EXPERTS - 1)
            for v in range(12, ITEM_UNITS):
                load_e(expert * ITEM_UNITS + v, v, last_item * ITEM_UNITS + v - RAW_E)
            for q in range(PAIRS):
                sp.wait_ge(S["final_done"], q + 1)
                sp.dma_start(out[:, 2 * q:2 * q + 2, :], h[:, 2 * q:2 * q + 2, :]).then_inc(stored, 16)
            sp.wait_ge(stored, 16 * PAIRS)

        @block.scalar
        def _(act):
            A = nc.scalar.activation
            def split(first, j, i=0):
                slot = (first + j) % RING
                u = first + j + RING * i
                act.wait_ge(raw_landed[slot], 16 * ((first + j) // RING + i + 1))
                act.wait_ge(unit_used, u + 1)
                A(hi[:, slot, :], raw[:, slot, :], ACT.Copy).then_inc(hi_done, 1)

            def used(u):
                act.wait_ge(unit_used, RING + u + 1)

            def norm(n, parts=True):
                act.wait_ge(S["norm_sum"], n + 1)
                A(tiles(stat[:, 0:TT], 1), PS[:, 4:4 + TT, 0:1], ACT.Sqrt, bias=C_("eps"), scale=1.0 / D).then_inc(S["std_done"], 1)
                if parts:
                    for q in range(PAIRS):
                        act.wait_ge(S["h_done"], PAIRS * n + q + 1)
                        A(flat(h_hi[:, 2 * q:2 * q + 2, :]), flat(h[:, 2 * q:2 * q + 2, :]), ACT.Copy).then_inc(S["h_hi_done"], 1)

            def mixer_unit(layer, u):
                b = base_of(layer)
                if not last_split(layer, u):
                    split(b, u + AHEAD)
                if u < IN_UNITS:
                    used(b + u)
                    A(flat(proj[:, 2 * u:2 * u + 2, :]), bank(u % 4), ACT.Copy).then_inc(S["win_done"], 1)
                elif u < U_GB:
                    for tile in range(KT):
                        end, count = early_event(layer, 2 * tile)
                        if (end - 1) // BLOCKS == u - U_EARLY:
                            if count:
                                act.wait_ge(S["early_ps"], count)
                            else:
                                used(b + u)
                            if tile >= 2:
                                act.wait_ge(S["early_added"], KT * layer + tile - 1)
                            A(flat(gate_of(tile)), bank(0, 2)[:, 0:3 * SEQ], ACT.Sigmoid).then_inc(S["gate_done"], 1)
                elif u < U_PB:
                    q = u - U_GB
                    used(b + u)
                    if q == 0:
                        act.wait_ge(S["y_ps"], GROUPS * (layer + 1))
                    A(flat(gate_b[:, 2 * q:2 * q + 2, :]), bank(q), ACT.Sigmoid).then_inc(S["gate_b_done"], 1)
                elif u < U_OUT:
                    q = u - U_PB
                    act.wait_ge(S["merge_done"], PAIRS * layer + q + 1)
                    A(flat(h_hi[:, 2 * q:2 * q + 2, :]), flat(merged[:, 2 * q:2 * q + 2, :]), ACT.Copy).then_inc(S["m_hi"], 1)

            def stage(name, layer):
                kind, g = name.rstrip("01234567"), int(name[-1]) if name[-1].isdigit() else 0
                if kind == "dt_row":
                    act.wait_ge(S["dt_sum"], layer + 1)
                    A(row[:], bank(6)[0:HEADS, 0:SEQ], ACT.Copy).then_inc(S["dt_row"], 1)
                elif kind == "dt_in":
                    act.wait_ge(par_loaded, 16 * (layer + 1))
                    act.wait_ge(S["a_sc"], layer + 1)
                    A(small[:, 0, 0, :], P_("a_log"), ACT.Exp).then_inc(S["a_exp"], 1)
                    A(small[:, 3, :, :], small[:, 2, :, :], ACT.Exp).then_inc(S["a_exp"], 1)
                elif kind == "dt_log":
                    act.wait_ge(S["dt_w"], layer + 1)
                    A(small[:, 5, :, :], small[:, 4, :, :], ACT.Ln).then_inc(S["dt_ln"], 1)
                elif kind == "conv":
                    for t in (2 * g, 2 * g + 1):
                        act.wait_ge(S["conv_acc"], XBC_BLOCKS * layer + t + 1)
                        A(proj[:, XBC + t, :], scr[:, (t % 4) * SEQ:(t % 4 + 1) * SEQ], ACT.Silu, bias=P_("ssm_b", t, 1)).then_inc(S["conv_done"], 1)
                elif kind == "gelu":
                    act.wait_ge(S["win_done"], IN_UNITS * layer + 12)
                    A(flat(proj[:, GV:GV + 4, :]), flat(proj[:, GV:GV + 4, :]), ACT.Gelu_apprx_tanh).then_inc(S["gelu_done"], 1)
                    A(flat(proj[:, GU:GU + 4, :]), flat(proj[:, GU:GU + 4, :]), ACT.Gelu_apprx_tanh).then_inc(S["gelu_done"], 1)
                elif kind == "var":
                    act.wait_ge(S["var_sum"], layer + 1)
                    A(stat[:, 0:TT], bank(7)[:, 0:TT], ACT.Sqrt, bias=C_("eps"), scale=1.0 / 512).then_inc(S["v_std"], 1)
                elif kind == "v_T":
                    act.wait_ge(S["v_T"], layer + 1)
                    A(flat(tmp[:, 8:12, :]), bank(4, 2), ACT.Copy).then_inc(S["v_T_sb"], 1)
                elif kind == "spatial":
                    act.wait_ge(S["yc_f"], layer + 1)
                    A(flat(y_hi[:, 4:8, :]), flat(proj[:, GU:GU + 4, :]), ACT.Copy).then_inc(S["yc_hi"], 1)
                elif kind == "pool_out":
                    act.wait_ge(S["yd_f"], layer + 1)
                    A(flat(y_hi[:, 8:12, :]), flat(proj[:, PD:PD + 4, :]), ACT.Copy).then_inc(S["yd_hi"], 1)
                elif kind == "short":
                    act.wait_ge(S["ya_f"], layer + 1)
                    A(flat(y_hi[:, 0:4, :]), flat(proj[:, A_B:A_B + 4, :]), ACT.Copy).then_inc(S["ya_hi"], 1)
                elif kind == "z":
                    act.wait_ge(S["win_done"], IN_UNITS * (layer + 1))
                    A(flat(y_b), flat(y_b), ACT.Silu).then_inc(S["z_done"], 1)
                elif kind == "seg":
                    act.wait_ge(S["seg_done"], GROUPS * layer + g + 1)
                    if layer or g:
                        act.wait_ge(S["y_ps"], GROUPS * layer + g)
                    A(flat(dec0), bank(4, 2), ACT.Exp)
                    A(flat(dec1), bank(6), ACT.Exp).then_inc(S["dec_exp"], 1)
                elif kind == "y_sum":
                    act.wait_ge(S["yb_sum"], layer + 1)
                    A(stat[:], bank(4)[:, 0:2 * GROUPS], ACT.Sqrt, bias=C_("eps"), scale=1.0 / 256).then_inc(S["yb_std"], 1)
                elif kind == "y_norm":
                    for half in range(2):
                        act.wait_ge(S["yb_f"], 2 * layer + half + 1)
                        if half == 0:
                            act.wait_ge(S["early_added"], KT * (layer + 1))
                        A(flat(yb_hi[:, 4 * half:4 * half + 4, :]), flat(y_b[:, 4 * half:4 * half + 4, :]), ACT.Copy).then_inc(S["yb_hi"], 1)

            act.wait_ge(con_loaded, 16)
            A(after_r[:], C_("after"), ACT.Copy)
            A(ones_r[:], C_("ones"), ACT.Copy).then_inc(S["masks_done"], 1)
            for layer in range(DEPTH):
                if layer == 0:
                    split(0, 0)
                norm(2 * layer)
                if layer == 0:
                    split(0, 1)
                u = 0
                for name, n in PLAN:
                    stage(name, layer)
                    for _ in range(n):
                        mixer_unit(layer, u)
                        u += 1
                for u in range(u, MIX_UNITS):
                    mixer_unit(layer, u)
                norm(2 * layer + 1, layer < DEPTH - 1)
                if layer == 0:
                    f0 = MIX_UNITS
                    split(f0, AHEAD)
                    used(f0)
                    A(ff_g, bank(4), ACT.Silu).then_inc(S["silu_done"], 1)
                    split(f0, 1 + AHEAD)
                    with act.Fori(0, FF_STEPS - 1) as i:
                        split(f0, 2 + AHEAD, i)
                        act.wait_ge(unit_used, RING + f0 + 2 + RING * i + 1)
                        act.wait_ge(S["mult_done"], i + 1)
                        A(ff_g, bank(4), ACT.Silu).then_inc(S["silu_done"], 1)
                        split(f0, 3 + AHEAD, i)
                        split(f0, 4 + AHEAD, i)
                    split(f0, FF_UNITS - 1 + AHEAD)

            def split_e(v, item=0):
                if v in outside:
                    act.wait_ge(outside_landed[v], 16)
                else:
                    slot = v % RAW_E
                    first = next(u for u in range(slot, v + 1, RAW_E) if u not in outside)
                    act.wait_ge(raw_e_landed[slot], 16 * ((v - first) // RAW_E + item * (ITEM_UNITS // RAW_E) + 1))
                act.wait_ge(unit_used, MOE_U + v + item * ITEM_UNITS + 1)
                A(hi[:, v % RING, :], raw_e(v), ACT.Copy).then_inc(hi_done, 1)

            def gathered(item):
                act.wait_ge(S["gather_ps"], 2 * item + 1)
                A(flat(xg_hi), bank(2, 2), ACT.Copy).then_inc(S["xg_hi_done"], 1)

            def body(item, final):
                v = 4
                for c in range(CHUNKS):
                    ahead = not (final and c == CHUNKS - 1)
                    if ahead:
                        split_e(v + AHEAD, item)
                        v += 1
                    act.wait_ge(S["hT_ps"], item * CHUNKS + c + 1)
                    A(flat(hT_hi), bank(6), ACT.Copy).then_inc(S["hT_hi_done"], 1)
                    if ahead:
                        split_e(v + AHEAD, item)
                        act.wait_ge(unit_used, RING + MOE_U + v + item * ITEM_UNITS + 1)
                        A(ff_g, bank(4), ACT.Silu).then_inc(S["esilu_done"], 1)
                        v += 1
                        for _ in range(2):
                            split_e(v + AHEAD, item)
                            v += 1
                        if c == CHUNKS - 2 and not final:
                            gathered(item)
                    if c == 3:
                        act.wait_ge(S["pickT_ps"], item + 1)
                        A(pickT, bank(7)[:, 0:SEQ], ACT.Copy).then_inc(S["pickT_done"], 1)
                    for _ in range(2):
                        if final and v + AHEAD == ITEM_UNITS - 1:
                            pass
                        elif final and c == CHUNKS - 1:
                            if v == ITEM_UNITS - 2:
                                split_e(ITEM_UNITS - 1, item)
                        else:
                            split_e(v + AHEAD, item)
                        v += 1
                if not final:
                    act.wait_ge(unit_used, RING + MOE_U + v + item * ITEM_UNITS)
                act.wait_ge(S["item_added"], 2 * item + 3)
                if final:
                    for n in range(2):
                        if n == 0:
                            act.wait_ge(S["y_bank"], 1)
                        else:
                            act.wait_ge(unit_used, RING + MOE_U + v + item * ITEM_UNITS)
                        A(y_sb[:, 512 * n:512 * n + 512], bank(n), ACT.Copy).then_inc(S["y_copied"], 1)
                else:
                    A(y_sb, bank(0, 2), ACT.Copy).then_inc(S["y_copied"], 1)

            act.sem_inc(S["y_copied"], 1)
            split_e(0)
            act.wait_ge(S["router_sum"], 1)
            A(row[0:EXPERTS, :], bank(6)[0:EXPERTS, 0:SEQ], ACT.Copy).then_inc(S["router_row"], 1)
            for t in range(TT):
                act.wait_ge(S["tok_ps"], t + 1)
                A(tok_hi[:, t, :], bank(4 * t, 2), ACT.Copy).then_inc(S["tok_hi_done"], 1)
            act.wait_ge(S["gap_in"], 1)
            A(small[:, 6, :, 0:1], small[:, 5, :, 0:1], ACT.Exp).then_inc(S["gap_exp"], 1)
            split_e(1)
            for half in range(2):
                act.wait_ge(S["first_gather"], 2 * half + 1)
                A(flat(xg_hi[:, 4 * half:4 * half + 4, :]), bank(2 + half), ACT.Copy).then_inc(S["xg_hi_done"], 1)
            split_e(2)
            split_e(3)
            act.wait_ge(unit_used, RING + MOE_U + 2)
            A(ff_g, bank(4), ACT.Silu).then_inc(S["esilu_done"], 1)
            split_e(2 + AHEAD)
            split_e(3 + AHEAD)
            act.wait_ge(S["items_done"], 1)
            last_item = act.value_load(ints[0:1, 31:32], min_val=MIN_ITEMS - 1, max_val=MAX_ITEMS - 1)
            with act.Fori(0, last_item) as item:
                body(item, False)
            body(last_item, True)
            norm(2 * DEPTH, False)

        @block.vector
        def _(dve):
            V = nc.vector
            dve_n = [0]

            def link(ins):
                dve_n[0] += 1
                ins.then_inc(dve_order, 1)
                dve.wait_ge(dve_order, dve_n[0])

            def split(first, j, i=0):
                slot = (first + j) % RING
                dve.wait_ge(hi_done, first + j + RING * i + 1)
                V.tensor_tensor(lo[:, slot, :], raw[:, slot, :], hi[:, slot, :].bitcast(f32), ALU.subtract).then_inc(lo_done, 1)

            def rest(out_, whole, hi_part, signal):
                V.tensor_tensor(out_, whole, hi_part.bitcast(f32), ALU.subtract).then_inc(signal, 1)

            def squares(q):
                V.tensor_tensor(flat(sq[:, 2 * q:2 * q + 2, :]), flat(x[:, 2 * q:2 * q + 2, :]), flat(x[:, 2 * q:2 * q + 2, :]), ALU.mult)\
                    .then_inc(S["sq_done"], 1)

            def norm(n, gain):
                dve.wait_ge(S["std_done"], n + 1)
                link(V.reciprocal(stat[:, 0:TT], stat[:, 0:TT]))
                for t in range(TT):
                    last = V.tensor_scalar(diag[:, t * P:(t + 1) * P], C_("ident"), stat[:, t:t + 1], None, ALU.mult)
                last.then_inc(S["diag_done"], 1)
                dve.wait_ge(S["rstd_ps"], n + 1)

                def lows(q):
                    dve.wait_ge(S["h_hi_done"], PAIRS * n + q + 1)
                    rest(flat(h_lo[:, 2 * q:2 * q + 2, :]), flat(h[:, 2 * q:2 * q + 2, :]), flat(h_hi[:, 2 * q:2 * q + 2, :]), S["h_lo_done"])

                for q in range(PAIRS):
                    for k in (2 * q, 2 * q + 1):
                        last = V.scalar_tensor_tensor(h[:, k, :], x[:, k, :], gain[:, k:k + 1], bank(7)[:, 0:SEQ], ALU.mult, ALU.mult)
                    last.then_inc(S["final_done" if n == 2 * DEPTH else "h_done"], 1)
                    if q and n < 2 * DEPTH - 1:
                        lows(q - 1)
                if n < 2 * DEPTH - 1:
                    lows(PAIRS - 1)

            def merged_low(layer, q):
                dve.wait_ge(S["m_hi"], PAIRS * layer + q + 1)
                rest(flat(h_lo[:, 2 * q:2 * q + 2, :]), flat(merged[:, 2 * q:2 * q + 2, :]), flat(h_hi[:, 2 * q:2 * q + 2, :]), S["m_lo"])

            def mixer_unit(layer, u):
                b = base_of(layer)
                if not last_split(layer, u):
                    split(b, u + AHEAD)
                if U_EARLY <= u < U_GB:
                    for tile in range(KT):
                        end, count = early_event(layer, 2 * tile + 1)
                        if (end - 1) // BLOCKS == u - U_EARLY:
                            if count:
                                dve.wait_ge(S["early_ps"], count)
                            else:
                                dve.wait_ge(unit_used, RING + b + u + 1)
                            dve.wait_ge(S["gate_done"], KT * layer + tile + 1)
                            g = gate_of(tile)
                            link(V.tensor_tensor(flat(g), flat(g), bank(2, 2)[:, 0:3 * SEQ], ALU.mult))
                            link(V.tensor_tensor(g[:, 0, :], g[:, 0, :], g[:, 1, :], ALU.add))
                            V.tensor_tensor(merged[:, tile, :], g[:, 0, :], g[:, 2, :], ALU.add).then_inc(S["early_added"], 1)
                elif U_PB <= u < U_OUT:
                    q = u - U_PB
                    two = slice(2 * q, 2 * q + 2)
                    dve.wait_ge(unit_used, RING + b + u + 1)
                    dve.wait_ge(S["gate_b_done"], PAIRS * layer + q + 1)
                    dve.wait_ge(S["early_added"], KT * (layer + 1))
                    link(V.tensor_tensor(flat(gate_b[:, two, :]), flat(gate_b[:, two, :]), bank(4 + q), ALU.mult))
                    V.tensor_tensor(flat(merged[:, two, :]), flat(merged[:, two, :]), flat(gate_b[:, two, :]), ALU.add).then_inc(S["merge_done"], 1)
                    if q:
                        merged_low(layer, q - 1)
                    if q == PAIRS - 1:
                        merged_low(layer, q)
                elif u >= U_OUT:
                    q = u - U_OUT
                    dve.wait_ge(unit_used, RING + b + u + 1)
                    added(q)

            def added(q):
                link(V.tensor_tensor(flat(x[:, 2 * q:2 * q + 2, :]), flat(x[:, 2 * q:2 * q + 2, :]), bank(q), ALU.add))
                squares(q)

            def stage(name, layer):
                kind, g = name.rstrip("01234567"), int(name[-1]) if name[-1].isdigit() else 0
                if kind == "dt_in":
                    dve.wait_ge(S["dt_raw"], layer + 1)
                    raw_dt = bank(6)[:, SEQ:SEQ + TT * HEADS].rearrange("p (t n) -> p t n", t=TT)
                    for t in range(TT):
                        last = V.tensor_tensor(small[:, 1, t, :], raw_dt[:, t, :], P_("dt_bias"), ALU.add)
                    link(last)
                    link(V.tensor_scalar(small[:, 2], small[:, 1], -1.0, None, ALU.mult))
                    V.tensor_tensor(small[:, 2], small[:, 2], small[:, 1], ALU.min).then_inc(S["a_sc"], 1)
                elif kind == "dt_log":
                    dve.wait_ge(S["a_exp"], 2 * layer + 2)
                    V.tensor_scalar(small[:, 4], small[:, 3], 1.0, None, ALU.add).then_inc(S["dt_w"], 1)
                    dve.wait_ge(S["dt_w"], layer + 1)
                    link(V.scalar_tensor_tensor(small[:, 8], small[:, 4], -1.0, small[:, 3], ALU.add, ALU.subtract))
                    link(V.reciprocal(small[:, 9], small[:, 4]))
                    link(V.tensor_tensor(small[:, 8], small[:, 8], small[:, 9], ALU.mult))
                elif kind == "dt_out":
                    dve.wait_ge(S["dt_ln"], layer + 1)
                    link(V.tensor_tensor(small[:, 5], small[:, 5], small[:, 8], ALU.subtract))
                    link(V.scalar_tensor_tensor(small[:, 6], small[:, 1], 0.0, small[:, 5], ALU.max, ALU.add))
                    for t in range(TT):
                        last = V.scalar_tensor_tensor(small[:, 7, t, :], small[:, 6, t, :], -1.0, small[:, 0, 0, :], ALU.mult, ALU.mult)
                    link(last)
                    link(V.tensor_copy(da_hi[:], small[:, 7]))
                    rest(da_lo[:], small[:, 7], da_hi[:], S["da_done"])
                elif kind == "conv":
                    dve.wait_ge(S["win_done"], IN_UNITS * layer + g + 1)
                    if g > 1:
                        dve.wait_ge(S["conv_done"], XBC_BLOCKS * layer + 2 * (g - 1))
                    accs, raws = tiles(scr[:, 512 * (g % 2):512 * (g % 2) + 512]), proj[:, XBC + 2 * g:XBC + 2 * g + 2, :]
                    for t in range(2):
                        last = V.tensor_scalar(accs[:, t, :], raws[:, t, :], P_("ssm_w", 3 * XBC_BLOCKS + 2 * g + t, 1), None, ALU.mult)
                    link(last)
                    for tap in (2, 1, 0):
                        s = SSM_K - 1 - tap
                        for t in range(2):
                            last = V.scalar_tensor_tensor(accs[:, t, s:], raws[:, t, :SEQ - s], P_("ssm_w", tap * XBC_BLOCKS + 2 * g + t, 1),
                                                          accs[:, t, s:], ALU.mult, ALU.add)
                            if tap == 0:
                                last.then_inc(S["conv_acc"], 1)
                        if tap:
                            link(last)
                elif kind == "xdt":
                    for t in range(TT):
                        dve.wait_ge(S["xs_T"], TT * layer + t + 1)
                        V.tensor_tensor(xdt[:, t, :].rearrange("p (h n) -> p h n", h=HEADS),
                                        bank(6 - 2 * t, 2).rearrange("p (h n) -> p h n", h=HEADS),
                                        small[:, 6, t, :].rearrange("p (h n) -> p h n", n=1).broadcast_to([P, HEADS, HEAD_DIM]),
                                        ALU.mult).then_inc(S["xdt_done"], 1)
                elif kind == "mean":
                    dve.wait_ge(S["mean_sum"], layer + 1)
                    link(V.tensor_scalar(v_mean, bank(7)[:, 0:SEQ], 1.0 / 512, None, ALU.mult))
                    for t in range(4):
                        last = V.tensor_tensor(v_[:, t, :], v_[:, t, :], v_mean, ALU.subtract)
                    link(last)
                    V.tensor_tensor(flat(v_sq), flat(v_), flat(v_), ALU.mult).then_inc(S["dev_sq"], 1)
                elif kind == "var":
                    dve.wait_ge(S["v_std"], layer + 1)
                    link(V.reciprocal(stat[:, 0:TT], stat[:, 0:TT]))
                    for t in range(TT):
                        last = V.tensor_scalar(v_diag[:, t * P:(t + 1) * P], C_("ident"), stat[:, t:t + 1], None, ALU.mult)
                    last.then_inc(S["v_diag"], 1)
                elif kind == "ln":
                    dve.wait_ge(S["v_rstd"], layer + 1)
                    for t in range(4):
                        last = V.scalar_tensor_tensor(v_[:, t, :], v_[:, t, :], P_("ln_g", t, 1), bank(7)[:, 0:SEQ], ALU.mult, ALU.mult)
                    link(last)
                    for t in range(4):
                        last = V.tensor_scalar(v_[:, t, :], v_[:, t, :], P_("ln_b", t, 1), None, ALU.add)
                    last.then_inc(S["v_norm"], 1)
                elif kind == "spatial":
                    dve.wait_ge(S["s_done"], layer + 1)
                    for t in range(TT):
                        last = V.tensor_tensor(v_[:, :, t * P:(t + 1) * P], tiles(bank(6, 2))[:, :, t * P:(t + 1) * P],
                                               tiles(P_("gm_bias"), P), ALU.add)
                    link(last)
                    dve.wait_ge(S["gelu_done"], 2 * layer + 2)
                    V.tensor_tensor(flat(u_), flat(u_), flat(v_), ALU.mult).then_inc(S["yc_f"], 1)
                    dve.wait_ge(S["yc_hi"], layer + 1)
                    rest(flat(y_lo[:, 4:8, :]), flat(u_), flat(y_hi[:, 4:8, :]), S["yc_lo"])
                elif kind == "pool_out":
                    dve.wait_ge(S["pool_out"], layer + 1)
                    for t in range(4):
                        last = V.tensor_scalar(pd[:, t, :], tiles(bank(4, 2))[:, t, :], P_("pool_scale", t, 1), None, ALU.mult)
                    last.then_inc(S["yd_f"], 1)
                    dve.wait_ge(S["yd_hi"], layer + 1)
                    rest(flat(y_lo[:, 8:12, :]), flat(pd), flat(y_hi[:, 8:12, :]), S["yd_lo"])
                elif kind == "short":
                    a_b = proj[:, A_B:A_B + 4, :]
                    dve.wait_ge(S["ya_hi"], layer + 1)
                    rest(flat(y_lo[:, 0:4, :]), flat(a_b), flat(y_hi[:, 0:4, :]), S["ya_lo"])
                elif kind == "cb":
                    dve.wait_ge(S["yd_lo"], layer + 1)
                    for n in (2 * g, 2 * g + 1):
                        dve.wait_ge(S["cb_ps"], GROUPS * layer + n + 1)
                        ps = bank(6 + n % 2)
                        V.tensor_tensor(cb[:, n, 0:P], ps[:, 0:P], C_("upto"), ALU.mult)
                        V.tensor_copy(cb[:, n, P:2 * P], ps[:, P:2 * P])
                        V.tensor_tensor(cb[:, n, 2 * P:], ps[:, 2 * P:3 * P], C_("upto"), ALU.mult).then_inc(S["cb_done"], 1)
                elif kind == "score":
                    dve.wait_ge(S["dec_exp"], GROUPS * layer + g + 1)
                    dve.wait_ge(S["cb_done"], GROUPS * (layer + 1))
                    for n in range(4):
                        V.tensor_tensor(dec0[:, n, :], dec0[:, n, :], cb[:, g, 0:SEQ], ALU.mult)
                        last = V.tensor_tensor(dec1[:, n, :], dec1[:, n, :], cb[:, g, SEQ:], ALU.mult)
                    last.then_inc(S["score_done"], 1)
                elif kind == "y":
                    dve.wait_ge(S["y_ps"], GROUPS * layer + g + 1)
                    for t in range(2):
                        c = 2 * g + t
                        last = V.scalar_tensor_tensor(proj[:, XBC + c, :], proj[:, XBC + c, :], P_("d_skip", c, 1),
                                                      tiles(bank(7))[:, t, :], ALU.mult, ALU.add)
                    last.then_inc(S["y_done"], 1)
                elif kind == "y_sq":
                    dve.wait_ge(S["z_done"], layer + 1)
                    dve.wait_ge(S["y_done"], GROUPS * (layer + 1))
                    link(V.tensor_tensor(flat(y_b), flat(y_b), flat(proj[:, XBC:XBC + 8, :]), ALU.mult))
                    V.tensor_tensor(flat(y_sq), flat(y_b), flat(y_b), ALU.mult).then_inc(S["yb_sq"], 1)
                elif kind == "y_sum":
                    dve.wait_ge(S["yb_std"], layer + 1)
                    link(V.reciprocal(stat[:], stat[:]))
                    n = 2 * GROUPS
                    V.tensor_tensor(tiles(scr[:], P), C_("ident").rearrange("p (a n) -> p a n", a=1).broadcast_to([P, n, P]),
                                    tiles(stat[:], 1).broadcast_to([P, n, P]), ALU.mult).then_inc(S["yb_diag"], 1)
                elif kind == "y_norm":
                    dve.wait_ge(S["yb_rstd"], layer + 1)
                    for c in range(8):
                        last = V.scalar_tensor_tensor(y_b[:, c, :], y_b[:, c, :], P_("norm_g", c, 1),
                                                      bank(4, 2)[:, (c // 2) * SEQ:(c // 2 + 1) * SEQ], ALU.mult, ALU.mult)
                        if c % 4 == 3:
                            last.then_inc(S["yb_f"], 1)
                    for half in range(2):
                        four = slice(4 * half, 4 * half + 4)
                        dve.wait_ge(S["yb_hi"], 2 * layer + half + 1)
                        rest(flat(yb_lo[:, four, :]), flat(y_b[:, four, :]), flat(yb_hi[:, four, :]), S["yb_lo"])

            u_, v_, pd = (proj[:, n:n + 4, :] for n in (GU, GV, PD))
            dve.sem_inc(lo_done, RING)
            for layer in range(DEPTH):
                if layer == 0:
                    for q in range(PAIRS):
                        dve.wait_ge(x_loaded[q // 2], 16)
                        squares(q)
                    split(0, 0)
                dve.wait_ge(con_loaded, 16)
                dve.wait_ge(par_loaded, 16 * (layer + 1))
                norm(2 * layer, P_("norm1"))
                if layer == 0:
                    split(0, 1)
                u = 0
                for name, n in PLAN:
                    stage(name, layer)
                    for _ in range(n):
                        mixer_unit(layer, u)
                        u += 1
                for u in range(u, MIX_UNITS):
                    mixer_unit(layer, u)
                norm(2 * layer + 1, P_("norm2"))
                if layer == 0:
                    f0 = MIX_UNITS
                    V.memset(bank(0, 4), 0.0).then_inc(S["acc_zero"], 1)

                    def hidden(i):
                        V.tensor_tensor(ff_h, ff_g, bank(5), ALU.mult).then_inc(S["mult_done"], 1)
                        dve.wait_ge(S["mult_done"], i + 1)
                        V.tensor_copy(flat(hid_hi), ff_h).then_inc(S["hid_done"], 1)
                        dve.wait_ge(S["hid_done"], 2 * i + 1)
                        rest(flat(hid_lo), ff_h, flat(hid_hi), S["hid_done"])

                    split(f0, AHEAD)
                    split(f0, 1 + AHEAD)
                    dve.wait_ge(S["silu_done"], 1)
                    dve.wait_ge(unit_used, RING + f0 + 2)
                    hidden(0)
                    with dve.Fori(0, FF_STEPS - 1) as i:
                        for j in range(RING):
                            split(f0, 2 + j + AHEAD, i)
                        dve.wait_ge(S["silu_done"], i + 2)
                        dve.wait_ge(unit_used, RING + f0 + 2 + RING * i + 3)
                        hidden(i + 1)
                    split(f0, FF_UNITS - 1 + AHEAD)
                    for q in range(PAIRS):
                        if q < PAIRS - 1:
                            dve.wait_ge(S["ff_bank"], q + 1)
                        else:
                            dve.wait_ge(unit_used, RING + f0 + FF_UNITS)
                        added(q)

            place = ints[:, 0:16].bitcast(u32).rearrange("p (t n) -> p t n", t=TT)
            def split_e(v, item=0):
                dve.wait_ge(hi_done, MOE_U + v + item * ITEM_UNITS + 1)
                V.tensor_tensor(lo[:, v % RING, :], raw_e(v), hi[:, v % RING, :].bitcast(f32), ALU.subtract).then_inc(lo_done, 1)

            split_e(0)
            dve.wait_ge(S["router_ps"], 1)
            link(V.tensor_copy(logit, bank(6)[:, SEQ:SEQ + TT * NT].rearrange("p (t n) -> p t n", t=TT)))
            for t in range(TT):
                last = V.max(top[:, t, :], logit[:, t, :])
            link(last)
            V.tensor_tensor(small[:, 5, :, 0:1], top[:, :, 1:2], top[:, :, 0:1], ALU.subtract).then_inc(S["gap_in"], 1)
            for t in range(TT):
                last = V.max_index(place[:, t, :], top[:, t, :], logit[:, t, :])
            link(last)
            link(V.tensor_copy(place_f, place))
            for t in range(TT):
                V.tensor_scalar(first_e[:, t, :], C_("experts"), place_f[:, t, 0:1], None, ALU.is_equal)
                last = V.tensor_scalar(other_e[:, t, :], C_("experts"), place_f[:, t, 1:2], None, ALU.is_equal)
            link(last)
            V.tensor_tensor(chosen, first_e, other_e, ALU.add).then_inc(S["sel_done"], 1)
            dve.wait_ge(S["sel_done"], 1)
            dve.wait_ge(S["pos_ps"], 1)
            ranks, counts = (bank(6)[:, n:n + TT * NT].rearrange("p (t n) -> p t n", t=TT) for n in (0, TT * NT))
            link(V.tensor_copy(slot, ranks))
            link(V.tensor_tensor(slot[:, 1, :], slot[:, 1, :], counts[:, 0, :], ALU.add))
            link(V.tensor_tensor(slot, slot, chosen, ALU.mult))
            link(V.tensor_scalar(slot, slot, -1.0, None, ALU.add))
            for t in range(TT):
                last = V.tensor_scalar(pick[:, t, :], C_("iota"), slot[:, t, 0:1], None, ALU.is_equal)
            last.then_inc(S["pick_done"], 1)
            for t in range(TT):
                dve.wait_ge(S["tok_hi_done"], t + 1)
                rest(tok_lo[:, t, :], bank(4 * t, 2), tok_hi[:, t, :], S["tok_lo_done"])

            def picks(item):
                for t in range(TT):
                    last = V.tensor_scalar(pick[:, t, :], C_("iota"), item_slot[:, t, ds(item, 1)], None, ALU.is_equal)
                last.then_inc(S["pick_done"], 1)

            def gathered(item):
                dve.wait_ge(S["gather_ps"], 2 * item + 2)
                V.tensor_copy(flat(xg_lo[:, 4:8, :]), bank(4))
                V.tensor_copy(flat(xg_lo[:, 0:4, :]), bank(7)).then_inc(S["xg_lo_done"], 1)

            def add_half(item, n, b=2):
                dve.wait_ge(S["scatter_ps"], 2 * item + n + 1)
                four = slice(4 * n, 4 * n + 4)
                V.tensor_tensor(flat(x[:, four, :]), flat(x[:, four, :]), bank(b, 2), ALU.add).then_inc(S["item_added"], 1)

            def gated(item, c):
                dve.wait_ge(S["esilu_done"], item * CHUNKS + c + 1)
                V.tensor_tensor(ff_h, ff_g, bank(5), ALU.mult).then_inc(S["eh_done"], 1)

            def body(item, final):
                v = 4
                for c in range(CHUNKS):
                    ahead = not (final and c == CHUNKS - 1)
                    if ahead:
                        split_e(v + AHEAD, item)
                        v += 1
                    if c == 0:
                        dve.wait_ge(S["y_copied"], item + 1)
                        V.memset(bank(0, 2), 0.0).then_inc(S["y_zero"], 1)
                    dve.wait_ge(S["hT_hi_done"], item * CHUNKS + c + 1)
                    rest(flat(hT_lo), bank(6), flat(hT_hi), S["hT_lo_done"])
                    if ahead:
                        for _ in range(3):
                            split_e(v + AHEAD, item)
                            v += 1
                        dve.wait_ge(unit_used, RING + MOE_U + v + item * ITEM_UNITS)
                        gated(item, c + 1)
                        if c == CHUNKS - 2 and not final:
                            gathered(item)
                    if c in (1, 2):
                        add_half(item, c - 1)
                    if c == 2:
                        for t in range(TT):
                            last = V.tensor_scalar(pick_g[:, t, :], C_("iota"), item_slot[:, t, ds(item, 1)],
                                                   item_gate[:, t, ds(item, 1)], ALU.is_equal, ALU.mult)
                        last.then_inc(S["pick_g_done"], 1)
                    if c == 4 and not final:
                        picks(item + 1)
                    for _ in range(2):
                        if final and v + AHEAD == ITEM_UNITS - 1:
                            pass
                        elif final and c == CHUNKS - 1:
                            if v == ITEM_UNITS - 2:
                                split_e(ITEM_UNITS - 1, item)
                        else:
                            split_e(v + AHEAD, item)
                        v += 1

            split_e(1)
            for half, b in ((0, 7), (1, 0)):
                dve.wait_ge(S["first_gather"], 2 * half + 2)
                V.tensor_copy(flat(xg_lo[:, 4 * half:4 * half + 4, :]), bank(b)).then_inc(S["xg_lo_done"], 1)
            split_e(2)
            dve.wait_ge(S["gap_exp"], 1)
            link(V.tensor_scalar(g2, small[:, 6, :, 0:1], 1.0, None, ALU.add))
            link(V.reciprocal(g1, g2))
            link(V.tensor_tensor(g2, g1, small[:, 6, :, 0:1], ALU.mult))
            link(V.tensor_copy(count, counts[:, 0, :]))
            link(V.tensor_tensor(count, count, counts[:, 1, :], ALU.add))
            link(V.tensor_scalar(count[:, 0:1], count[:, 0:1], 1.0, None, ALU.max))
            link(V.tensor_scalar(cum, count, float(P) + 0.5, None, ALU.is_gt))
            link(V.scalar_tensor_tensor(blocks_e, count, 0.5, cum, ALU.is_gt, ALU.add))
            link(V.tensor_tensor_scan(cum, C_("ones", 0, NT), blocks_e, 0.0, ALU.mult, ALU.add))
            items = C_("items").rearrange("p (a b) -> p a b", a=MAX_ITEMS)
            link(V.tensor_tensor(grid, cum.rearrange("p (a b) -> p a b", a=1).broadcast_to([P, MAX_ITEMS, NT]), items, ALU.is_le))
            link(V.tensor_reduce(expert_f, grid, AX.X, ALU.add))
            V.tensor_copy(ints[:, 0:MAX_ITEMS], expert_f)
            link(V.memset(second, 0.0))
            link(V.tensor_tensor(second[:, 1:], expert_f[:, 1:], expert_f[:, :MAX_ITEMS - 1], ALU.is_equal))
            V.tensor_scalar(ints[:, 31:32], cum[:, NT - 1:NT], -1.0, None, ALU.add).then_inc(S["items_done"], 1)
            split_e(3)
            dve.sem_inc(S["item_added"], 1)
            split_e(4)
            split_e(5)
            dve.wait_ge(unit_used, RING + MOE_U + 4)
            gated(0, 0)
            dve.wait_ge(S["items_done"], 1)
            dve.wait_ge(S["tables_done"], 1)
            last_item = dve.value_load(ints[0:1, 31:32], min_val=MIN_ITEMS - 1, max_val=MAX_ITEMS - 1)

            with dve.Fori(0, last_item) as item:
                body(item, False)
            body(last_item, True)
            for n in range(2):
                dve.wait_ge(S["item_added"], 2 * last_item + 3 + n)
                add_half(last_item + 1, n, 2 + 4 * n)
                dve.wait_ge(S["item_added"], 2 * last_item + 4 + n)
                squares(2 * n)
                squares(2 * n + 1)
            norm(2 * DEPTH, C_("final"))

        @block.gpsimd
        def _(gp):
            G = nc.gpsimd
            gp_n = [0]

            def link(ins):
                gp_n[0] += 1
                ins.then_inc(gp_order, 1)
                gp.wait_ge(gp_order, gp_n[0])

            def squares_added(n):
                for q in (1, 2):
                    gp.wait_ge(S["sq_done"], PAIRS * n + q + 1)
                    last = G.tensor_tensor(flat(sq[:, 0:2, :]), flat(sq[:, 0:2, :]), flat(sq[:, 2 * q:2 * q + 2, :]), ALU.add)
                    if q == 1:
                        link(last)
                last.then_inc(S["sq_added"], 1)

            pd = proj[:, PD:PD + 4, :]
            for layer in range(DEPTH):
                squares_added(2 * layer)
                gp.wait_ge(con_loaded, 16)
                gp.wait_ge(par_rest_loaded, 16 * (layer + 1))
                for n in range(4):
                    last = G.tensor_tensor(P_("ws", n * P, P), P_("ws", n * P, P), C_("upto"), ALU.mult)
                last.then_inc(S["ws_masked"], 1)
                gp.wait_ge(S["win_done"], IN_UNITS * layer + PD // 2 + 2)
                src, dst = pd, sums_a
                for step in range(4):
                    w = 1 << step
                    G.tensor_tensor(dst[:, step:, w:], src[:, step:, w:], src[:, step:, :SEQ - w], ALU.add)
                    link(G.tensor_copy(dst[:, step:, 0:w], src[:, step:, 0:w]))
                    G.tensor_scalar(pooled[:, step, 16:], dst[:, step, 16:], 1.0 / (2 * w), None, ALU.mult)
                    link(G.tensor_tensor(pooled[:, step, 0:16], dst[:, step, 0:16], C_("inv_count", 16 * step, 16), ALU.mult))
                    G.tensor_tensor(pooled[:, step, :], pooled[:, step, :], pd[:, step, :], ALU.subtract).then_inc(S["pooled"], 1)
                    src, dst = (sums_a, sums_b) if step % 2 == 0 else (sums_b, sums_a)
                gp.wait_ge(par_loaded, 16 * (layer + 1))
                gp.wait_ge(S["win_done"], IN_UNITS * layer + A_C // 2 + 2)
                a_h, a_b, a_c = (proj[:, n:n + 4, :] for n in (A_H, A_B, A_C))
                link(G.tensor_tensor(flat(a_h), flat(a_h), flat(a_c), ALU.mult))
                for t in range(SC_BLOCKS):
                    last = G.tensor_scalar(a_c[:, t, :], a_h[:, t, :], P_("sc_w", 2 * SC_BLOCKS + t, 1), None, ALU.mult)
                link(last)
                for tap in (1, 0):
                    s = SC_K - 1 - tap
                    for t in range(SC_BLOCKS):
                        last = G.tensor_scalar(sums_a[:, t, s:], a_h[:, t, :SEQ - s], P_("sc_w", tap * SC_BLOCKS + t, 1), None, ALU.mult)
                    link(last)
                    link(G.tensor_tensor(a_c[:, :, s:], a_c[:, :, s:], sums_a[:, :, s:], ALU.add))
                G.tensor_tensor(flat(a_b), flat(a_b), flat(a_c), ALU.mult).then_inc(S["ya_f"], 1)
                gp.wait_ge(S["da_done"], layer + 1)
                gp.wait_ge(S["ya_lo"], layer + 1)
                up_and_ones = C_("upto", 0, 2 * P)
                for g in range(GROUPS):
                    if g:
                        gp.wait_ge(S["seg_done"], GROUPS * layer + g)
                    for part, da in enumerate((da_hi, da_lo)):
                        if g == 0 and part == 1:
                            gp.wait_ge(S["cb_ps"], GROUPS * (layer + 1))
                        for n in range(4):
                            head = slice(4 * g + n, 4 * g + n + 1)
                            G.tensor_scalar(seg_in0[part][:, n, :], up_and_ones, da[:, 0, head].bitcast(f32), None, ALU.mult)
                            last = G.tensor_scalar(seg_in1[part][:, n, :], C_("upto"), da[:, 1, head].bitcast(f32), None, ALU.mult)
                    last.then_inc(S["seg_in"], 1)
                gp.wait_ge(S["yb_sq"], layer + 1)
                pairs = y_sq.rearrange("p (g t) n -> p g t n", t=2)
                G.tensor_tensor(pairs[:, :, 0, :], pairs[:, :, 0, :], pairs[:, :, 1, :], ALU.add).then_inc(S["yb_sq_added"], 1)
                squares_added(2 * layer + 1)

            gp.wait_ge(S["rstd_ps"], 2 * DEPTH)
            G.memset(y_sb, 0.0)
            G.memset(pickT, 0.0).then_inc(S["zeros_done"], 1)
            gp.wait_ge(S["items_done"], 1)
            for t in range(TT):
                last = G.tensor_scalar(comb[:, t, :], first_e[:, t, :], g1[:, t, :], None, ALU.mult)
            link(last)
            for t in range(TT):
                last = G.tensor_scalar(other_e[:, t, :], other_e[:, t, :], g2[:, t, :], None, ALU.mult)
            link(last)
            link(G.tensor_tensor(comb, comb, other_e, ALU.add))
            experts = C_("experts")
            for i in range(MAX_ITEMS):
                last = G.tensor_scalar(one_hot[:, i, :], experts, expert_f[:, i:i + 1], None, ALU.is_equal)
            link(last)
            link(G.tensor_scalar(second, second, -float(P), None, ALU.mult))
            for t in range(TT):
                for dst, of in ((item_slot, slot), (item_gate, comb)):
                    link(G.tensor_tensor(pickv, one_hot, of[:, t:t + 1, :].broadcast_to([P, MAX_ITEMS, NT]), ALU.mult))
                    for w in (4, 2):
                        link(G.tensor_tensor(pickv[:, :, 0:w], pickv[:, :, 0:w], pickv[:, :, w:2 * w], ALU.add))
                    link(G.tensor_tensor(tiles(dst[:, t, :], 1), pickv[:, :, 0:1], pickv[:, :, 1:2], ALU.add))
                link(G.tensor_tensor(item_slot[:, t, :], item_slot[:, t, :], second, ALU.add))
            gp.sem_inc(S["tables_done"], 1)
            squares_added(2 * DEPTH)

        @block.tensor
        def _(pe):
            def mm(o, a, b_, start, stop, **k):
                return nc.tensor.matmul(o, a, b_, start=start, stop=stop, skip_group_check=True, **k)

            def product(o, slot, blk, a_hi, a_lo, start, stop):
                w = slice(blk * P, (blk + 1) * P)
                mm(o, hi[:, slot, w], a_hi, start, False)
                mm(o, hi[:, slot, w], a_lo, False, False)
                return mm(o, lo[:, slot, w], a_hi, False, stop)

            def tile_pair(b_out, first, j, ready=None):
                for t in range(2):
                    for k in range(KT):
                        if ready and t == 0 and k % 2 == 0:
                            pe.wait_ge(ready[0], ready[1] + k // 2 + 1)
                        last = product(bank(b_out)[:, t * SEQ:(t + 1) * SEQ], (first + j) % RING, KT * t + k,
                                       h_hi[:, k, :], h_lo[:, k, :], k == 0, k == KT - 1)
                last.then_inc(unit_used, 1)

            def split_is(u):
                pe.wait_ge(lo_done, RING + u + 1)

            def norm_sums(n):
                for k in (0, 1, KT - 2, KT - 1):
                    if k == 0:
                        pe.wait_ge(S["sq_added"], n + 1)
                    elif k == KT - 2:
                        pe.wait_ge(S["sq_done"], PAIRS * (n + 1))
                    for t in range(TT):
                        last = mm(bank(4 + t)[:, 0:1], sq[:, k, t * P:(t + 1) * P], C_("ones", 0, 1), k == 0, k == KT - 1)
                last.then_inc(S["norm_sum"], 1)
                pe.wait_ge(S["diag_done"], n + 1)
                mm(bank(7)[:, 0:SEQ], C_("ones"), diag, True, True).then_inc(S["rstd_ps"], 1)

            def early_unit(layer, u):
                b = base_of(layer)
                ends = {}
                for e in range(2 * KT):
                    end, count = early_event(layer, e)
                    ends[end] = count
                for blk in range(BLOCKS * (u - U_EARLY), BLOCKS * (u - U_EARLY + 1)):
                    tile, n = blk // EARLY_BLOCKS, blk % EARLY_BLOCKS
                    if n < len(EARLY) * KT:
                        if n == 0 and tile == 0:
                            pe.wait_ge(S["win_done"], IN_UNITS * (layer + 1))
                        elif n == 0:
                            pe.wait_ge(S["gate_done"], KT * layer + tile)
                        br, k, depth = n // KT, n % KT, KT
                        out_bank, a_hi, a_lo = br // 2, h_hi[:, k, :], h_lo[:, k, :]
                    else:
                        n -= len(EARLY) * KT
                        if n == 0 and tile == 0:
                            for ready in ("ya_lo", "yc_lo", "yd_lo"):
                                pe.wait_ge(S[ready], layer + 1)
                        elif n == 0:
                            pe.wait_ge(S["early_added"], KT * layer + tile)
                        br, k, depth = n // 4, n % 4, 4
                        out_bank, a_hi, a_lo = 2 + br // 2, y_hi[:, n, :], y_lo[:, n, :]
                    last = product(bank(out_bank)[:, (br % 2) * SEQ:(br % 2 + 1) * SEQ], (b + u) % RING, blk % BLOCKS,
                                   a_hi, a_lo, k == 0, k == depth - 1)
                    if (blk + 1) % BLOCKS == 0:
                        last.then_inc(unit_used, 1)
                    elif blk + 1 in ends:
                        last.then_inc(S["early_ps"], 1)

            def mixer_unit(layer, u):
                b = base_of(layer)
                split_is(b + u)
                if u < IN_UNITS:
                    n = IN_UNITS * layer + u
                    if n >= 4:
                        pe.wait_ge(S["win_done"], n - 3)
                    tile_pair(u % 4, b, u, (S["h_lo_done"], 2 * PAIRS * layer) if u == 0 else None)
                elif u < U_GB:
                    early_unit(layer, u)
                elif u < U_PB:
                    if u == U_GB:
                        pe.wait_ge(S["gate_done"], KT * (layer + 1))
                        pe.wait_ge(S["early_added"], KT * (layer + 1))
                    tile_pair(u - U_GB, b, u)
                elif u < U_OUT:
                    q = u - U_PB
                    if q == 0:
                        pe.wait_ge(S["yb_lo"], 2 * (layer + 1))
                    for t in range(2):
                        for k in range(KT):
                            last = product(bank(4 + q)[:, t * SEQ:(t + 1) * SEQ], (b + u) % RING, KT * t + k,
                                           yb_hi[:, k, :], yb_lo[:, k, :], k == 0, k == KT - 1)
                    last.then_inc(unit_used, 1)
                else:
                    q = u - U_OUT
                    tile_pair(q, b, u, (S["m_lo"], PAIRS * layer) if q == 0 else None)
                    if q == OUT_UNITS - 1:
                        norm_sums(2 * layer + 1)

            def stage(name, layer):
                kind, g = name.rstrip("01234567"), int(name[-1]) if name[-1].isdigit() else 0
                if kind == "dt_row":
                    w_dt = P_("w_dt").rearrange("p (k n) -> p k n", k=KT)
                    for k in range(KT):
                        if k % 2 == 0:
                            pe.wait_ge(S["h_done"], 2 * PAIRS * layer + k // 2 + 1)
                        last = mm(bank(6)[0:HEADS, 0:SEQ], w_dt[:, k, :], h[:, k, :], k == 0, k == KT - 1)
                    last.then_inc(S["dt_sum"], 1)
                elif kind == "dt_in":
                    pe.wait_ge(S["dt_row"], layer + 1)
                    for t in range(TT):
                        last = nc.tensor.transpose(bank(6)[:, SEQ + t * HEADS:SEQ + (t + 1) * HEADS], row[:, t * P:(t + 1) * P],
                                                   C_("ident")[0:HEADS, 0:HEADS])
                    last.then_inc(S["dt_raw"], 1)
                elif kind == "xs_T":
                    pe.wait_ge(S["conv_done"], XBC_BLOCKS * layer + 8)
                    pe.wait_ge(S["a_sc"], layer + 1)
                    for t in range(TT):
                        for c in range(8):
                            last = nc.tensor.transpose(bank(6 - 2 * t + c // 4)[:, (c % 4) * P:(c % 4 + 1) * P],
                                                       proj[:, XBC + c, t * P:(t + 1) * P], C_("ident"))
                        last.then_inc(S["xs_T"], 1)
                elif kind == "mean":
                    pe.wait_ge(S["gelu_done"], 2 * layer + 1)
                    pe.wait_ge(S["xdt_done"], TT * (layer + 1))
                    for k in range(4):
                        last = mm(bank(7)[:, 0:SEQ], C_("ones"), v_[:, k, :], k == 0, k == 3)
                    last.then_inc(S["mean_sum"], 1)
                elif kind == "var":
                    pe.wait_ge(S["dev_sq"], layer + 1)
                    for t in range(TT):
                        for k in range(4):
                            last = mm(bank(7)[:, t:t + 1], v_sq[:, k, t * P:(t + 1) * P], C_("ones", 0, 1), k == 0, k == 3)
                    last.then_inc(S["var_sum"], 1)
                elif kind == "ln":
                    pe.wait_ge(S["v_diag"], layer + 1)
                    mm(bank(7)[:, 0:SEQ], C_("ones"), v_diag, True, True).then_inc(S["v_rstd"], 1)
                elif kind == "v_T":
                    pe.wait_ge(S["v_norm"], layer + 1)
                    for t in range(TT):
                        for n in range(4):
                            last = nc.tensor.transpose(bank(4 + t)[:, n * P:(n + 1) * P], v_[:, n, t * P:(t + 1) * P], C_("ident"))
                    last.then_inc(S["v_T"], 1)
                elif kind == "spatial":
                    pe.wait_ge(S["v_T_sb"], layer + 1)
                    pe.wait_ge(S["ws_masked"], layer + 1)
                    for n in range(4):
                        for t in range(TT):
                            at = (n % 2) * SEQ + t * P
                            last = mm(bank(6 + n // 2)[:, at:at + P], vT[:, t, n * P:(n + 1) * P], P_("ws", n * P, P), True, True)
                    last.then_inc(S["s_done"], 1)
                elif kind == "pool_out":
                    pe.wait_ge(S["pooled"], 4 * (layer + 1))
                    for n in range(4):
                        last = mm(bank(4 + n // 2)[:, (n % 2) * SEQ:(n % 2 + 1) * SEQ], P_("pool_map", n * P, P), pooled[:, n, :], True, True)
                    last.then_inc(S["pool_out"], 1)
                elif kind == "cb":
                    pe.wait_ge(S["conv_done"], XBC_BLOCKS * (layer + 1))
                    if g == 0:
                        pe.wait_ge(S["yc_f"], layer + 1)
                    else:
                        pe.wait_ge(S["cb_done"], GROUPS * layer + 2)
                    for n in (2 * g, 2 * g + 1):
                        b_t, c_t = proj[:, XBC + 8 + n, :], proj[:, XBC + 12 + n, :]
                        mm(bank(6 + n % 2)[:, 0:SEQ], b_t[:, 0:P], c_t, True, True)
                        mm(bank(6 + n % 2)[:, SEQ:SEQ + P], b_t[:, P:], c_t[:, P:], True, True).then_inc(S["cb_ps"], 1)
                elif kind == "seg":
                    pe.wait_ge(S["seg_in"], GROUPS * layer + g + 1)
                    pe.wait_ge(S["yd_f"], layer + 1)
                    pe.wait_ge(S["cb_done"], GROUPS * (layer + 1))
                    for n in range(2):
                        for part in range(2):
                            mm(bank(4 + n), after_r[:], flat(seg_in0[part][:, 2 * n:2 * n + 2, :]), part == 0, False)
                        for part in range(2):
                            mm(tiles(bank(4 + n))[:, :, P:], ones_r[:], seg_in1[part][:, 2 * n:2 * n + 2, :], False, part == 1)
                    for part in range(2):
                        last = mm(bank(6), after_r[:], flat(seg_in1[part]), part == 0, part == 1)
                    last.then_inc(S["seg_done"], 1)
                elif kind == "y":
                    pe.wait_ge(S["score_done"], GROUPS * layer + g + 1)
                    if layer or g:
                        pe.wait_ge(S["y_done"], GROUPS * layer + g)
                    for n in range(4):
                        head = 4 * g + n
                        o = bank(7)[HEAD_DIM * (n % 2):HEAD_DIM * (n % 2 + 1), (n // 2) * SEQ:(n // 2 + 1) * SEQ]
                        heads = slice(head * HEAD_DIM, (head + 1) * HEAD_DIM)
                        mm(o, xdt[:, 0, heads], dec0[:, n, :], True, False)
                        last = mm(o[:, P:], xdt[:, 1, heads], dec1[:, n, :], False, True)
                    last.then_inc(S["y_ps"], 1)
                elif kind == "y_sum":
                    pe.wait_ge(S["yb_sq_added"], layer + 1)
                    for n in range(GROUPS):
                        for t in range(TT):
                            last = mm(bank(4)[:, TT * n + t:TT * n + t + 1], y_sq[:, 2 * n, t * P:(t + 1) * P], C_("ones", 0, 1), True, True)
                    last.then_inc(S["yb_sum"], 1)
                elif kind == "y_spread":
                    pe.wait_ge(S["yb_diag"], layer + 1)
                    for n in range(2):
                        last = mm(bank(4 + n), C_("ones"), scr[:, 512 * n:512 * n + 512], True, True)
                    last.then_inc(S["yb_rstd"], 1)

            v_ = proj[:, GV:GV + 4, :]
            pe.sem_inc(unit_used, RING)
            pe.wait_ge(con_loaded, 16)
            pe.wait_ge(S["masks_done"], 1)
            for layer in range(DEPTH):
                norm_sums(2 * layer)
                u = 0
                for name, n in PLAN:
                    stage(name, layer)
                    for _ in range(n):
                        mixer_unit(layer, u)
                        u += 1
                for u in range(u, MIX_UNITS):
                    mixer_unit(layer, u)
                if layer == 0:
                    f0 = MIX_UNITS

                    def down(j, final=False):
                        order = [(f, m) for f in range(2) for m in range(KT)]
                        if final:
                            order.sort(key=lambda fm: fm[1] // 2)
                        for n, (f, m) in enumerate(order):
                            last = product(bank(m // 2)[:, (m % 2) * SEQ:(m % 2 + 1) * SEQ], (f0 + j) % RING, f * KT + m,
                                           hid_hi[:, f, :], hid_lo[:, f, :], False, False)
                            if final and n in (3, 7, 11):
                                last.then_inc(S["ff_bank"], 1)
                        last.then_inc(unit_used, 1)

                    split_is(f0)
                    tile_pair(4, f0, 0, (S["h_lo_done"], PAIRS))
                    split_is(f0 + 1)
                    tile_pair(5, f0, 1)
                    pe.wait_ge(S["acc_zero"], 1)
                    with pe.Fori(0, FF_STEPS - 1) as i:
                        split_is(f0 + 2 + RING * i)
                        pe.wait_ge(S["silu_done"], i + 1)
                        tile_pair(4, f0, 2)
                        split_is(f0 + 3 + RING * i)
                        pe.wait_ge(S["hid_done"], 2 * i + 2)
                        down(3)
                        split_is(f0 + 4 + RING * i)
                        tile_pair(5, f0, 4)
                    split_is(f0 + FF_UNITS - 1)
                    pe.wait_ge(S["hid_done"], 2 * FF_STEPS)
                    down(FF_UNITS - 1, True)

            r_w = C_("router").rearrange("p (k n) -> p k n", k=KT)
            for k in range(KT):
                if k % 2 == 0:
                    pe.wait_ge(S["h_done"], PAIRS * (2 * DEPTH - 1) + k // 2 + 1)
                last = mm(bank(6)[0:EXPERTS, 0:SEQ], r_w[:, k, :], h[:, k, :], k == 0, k == KT - 1)
            last.then_inc(S["router_sum"], 1)

            def tokens(t):
                for k in range(KT):
                    last = nc.tensor.transpose(bank(4 * t + k // 4)[:, (k % 4) * P:(k % 4 + 1) * P], h[:, k, t * P:(t + 1) * P], C_("ident"))
                last.then_inc(S["tok_ps"], 1)

            tokens(0)
            pe.wait_ge(S["router_row"], 1)
            for t in range(TT):
                last = nc.tensor.transpose(bank(6)[:, SEQ + t * EXPERTS:SEQ + (t + 1) * EXPERTS], row[0:EXPERTS, t * P:(t + 1) * P],
                                           C_("ident")[0:EXPERTS, 0:EXPERTS])
            last.then_inc(S["router_ps"], 1)
            tokens(1)
            pe.wait_ge(S["sel_done"], 1)
            chosen = route[:, 3 * TT * EXPERTS:4 * TT * EXPERTS]
            mm(bank(6)[:, 0:TT * EXPERTS], C_("upto"), chosen, True, True)
            mm(bank(6)[:, TT * EXPERTS:2 * TT * EXPERTS], C_("ones"), chosen, True, True).then_inc(S["pos_ps"], 1)

            def split_e_is(v, item):
                pe.wait_ge(lo_done, RING + MOE_U + v + item * ITEM_UNITS + 1)

            def up(o, v, half, item=0):
                split_e_is(v, item)
                for k in range(4):
                    w, kk = slice(k * CHUNK_F, (k + 1) * CHUNK_F), 4 * half + k
                    mm(o, xg_hi[:, kk, :], hi[:, v % RING, w], kk == 0, False)
                    mm(o, xg_hi[:, kk, :], lo[:, v % RING, w], False, False)
                    last = mm(o, xg_lo[:, kk, :], hi[:, v % RING, w], False, kk == KT - 1)
                last.then_inc(unit_used, 1)

            def down(v, half, item, final=False):
                split_e_is(v, item)
                for f, n in ((0, 0), (1, 0), (0, 1), (1, 1)) if final else ((0, 0), (0, 1), (1, 0), (1, 1)):
                    w = slice(f * D + n * 512, f * D + (n + 1) * 512)
                    mm(bank(n), hT_hi[:, 2 * half + f, :], hi[:, v % RING, w], False, False)
                    mm(bank(n), hT_hi[:, 2 * half + f, :], lo[:, v % RING, w], False, False)
                    last = mm(bank(n), hT_lo[:, 2 * half + f, :], hi[:, v % RING, w], False, False)
                    if final and (f, n) == (1, 0):
                        last.then_inc(S["y_bank"], 1)
                last.then_inc(unit_used, 1)

            def gather_tiles(part, half, b):
                tok = (tok_hi, tok_lo)[part]
                for k in range(4 * half, 4 * half + 4):
                    o = bank(b)[:, (k % 4) * P:(k % 4 + 1) * P]
                    mm(o, tok[:, 0, k * P:(k + 1) * P], pick[:, 0, :], True, False)
                    last = mm(o, tok[:, 1, k * P:(k + 1) * P], pick[:, 1, :], False, True)
                return last

            def gather(item):
                pe.wait_ge(S["pick_done"], item + 1)
                for part in range(2):
                    for half in range(2):
                        last = gather_tiles(part, half, ((2, 3), (7, 4))[part][half])
                    last.then_inc(S["gather_ps"], 1)

            def scatter(item, n, b=2):
                for m in range(4):
                    k = 4 * n + m
                    last = mm(bank(b + m // 2)[:, (m % 2) * SEQ:(m % 2 + 1) * SEQ], y_sb[:, k * P:(k + 1) * P], pickT, True, True)
                last.then_inc(S["scatter_ps"], 1)

            def body(item, final):
                v = 4
                for c in range(CHUNKS):
                    ahead = not (final and c == CHUNKS - 1)
                    if ahead:
                        pe.wait_ge(S["esilu_done"], item * CHUNKS + c + 1)
                        if c == CHUNKS - 1:
                            pe.wait_ge(S["xg_hi_done"], item + 3)
                            pe.wait_ge(S["xg_lo_done"], item + 3)
                        up(bank(4), v, 0, item)
                    pe.wait_ge(S["eh_done"], item * CHUNKS + c + 1)
                    for f in range(4):
                        last = nc.tensor.transpose(bank(6)[:, f * P:(f + 1) * P], ff_h[:, f * P:(f + 1) * P], C_("ident"))
                    last.then_inc(S["hT_ps"], 1)
                    if ahead:
                        up(bank(4), v + 1, 1, item)
                        up(bank(5), v + 2, 0, item)
                        up(bank(5), v + 3, 1, item)
                        v += 4
                    if c == 1:
                        pe.wait_ge(S["y_copied"], item + 1)
                        scatter(item, 0)
                    if c == 2:
                        pe.wait_ge(S["item_added"], 2 * item + 2)
                        scatter(item, 1)
                    if c == 3:
                        pe.wait_ge(S["pick_g_done"], item + 1)
                        for t in range(TT):
                            last = nc.tensor.transpose(bank(7)[:, t * P:(t + 1) * P], pick_g[:, t, :], C_("ident"))
                        last.then_inc(S["pickT_ps"], 1)
                    if c == CHUNKS - 2 and not final:
                        pe.wait_ge(S["item_added"], 2 * item + 3)
                        pe.wait_ge(S["pickT_done"], item + 1)
                        pe.wait_ge(S["esilu_done"], item * CHUNKS + CHUNKS)
                        gather(item + 1)
                    if c == 0:
                        pe.wait_ge(S["y_zero"], item + 1)
                    pe.wait_ge(S["hT_lo_done"], item * CHUNKS + c + 1)
                    down(v, 0, item)
                    down(v + 1, 1, item, final and c == CHUNKS - 1)
                    v += 2

            pe.wait_ge(S["pick_done"], 1)
            pe.wait_ge(S["tok_hi_done"], TT)
            for half in range(2):
                gather_tiles(0, half, 2 + half).then_inc(S["first_gather"], 1)
                if half == 0:
                    pe.wait_ge(S["tok_lo_done"], TT)
                gather_tiles(1, half, (7, 0)[half]).then_inc(S["first_gather"], 1)
            pe.wait_ge(S["zeros_done"], 1)
            for v in range(4):
                if v < 2:
                    pe.wait_ge(S["xg_hi_done"], v + 1)
                    pe.wait_ge(S["xg_lo_done"], v + 1)
                up(bank(4 + v // 2), v, v % 2)
            pe.wait_ge(S["items_done"], 1)
            last_item = pe.value_load(ints[0:1, 31:32], min_val=MIN_ITEMS - 1, max_val=MAX_ITEMS - 1)
            with pe.Fori(0, last_item) as item:
                body(item, False)
            body(last_item, True)
            pe.wait_ge(S["y_copied"], last_item + 2)
            scatter(last_item + 1, 0)
            pe.wait_ge(S["y_copied"], last_item + 3)
            scatter(last_item + 1, 1, 6)
            norm_sums(2 * DEPTH)


def blocks_of(w):
    k, n = w.shape
    return w.reshape(k // P, P, n // P, P).transpose(0, 2, 1, 3)


def units_of(blocks):
    a = np.asarray(blocks).reshape(-1, BLOCKS, P, P)
    return a.transpose(0, 2, 1, 3).reshape(-1, P, UNIT)


def by_output(w):
    return blocks_of(w).transpose(1, 0, 2, 3).reshape(-1, P, P)


def per_channel(v):
    return v.reshape(-1, P).T


def mixer_units(q, layer):
    w = q["w_in"][layer]
    n_a, n_b, z = 3 * 512, 1024 + 2048 + HEADS, 1024
    b0 = n_a
    c0 = n_a + n_b
    d0 = c0 + 1024
    order = [w[:, b0 + z:b0 + z + 2048], w[:, c0:c0 + 1024], w[:, d0:d0 + 512], w[:, 0:n_a], w[:, b0:b0 + z]]
    parts = [by_output(np.concatenate(order, 1))]
    gate = q["w_gate"][layer].reshape(D, 4, D)
    early = [(blocks_of(gate[:, n]), blocks_of(q[name][layer])) for n, name in ((0, "w_br_a"), (2, "w_br_c"), (3, "w_br_d"))]
    parts.append(np.concatenate([g_or_br[n][:, j] for j in range(KT) for n in (0, 1) for g_or_br in early]))
    parts += [by_output(gate[:, 1]), by_output(q["w_br_b"][layer]), by_output(q["w_out"][layer])]
    return np.concatenate([units_of(p) for p in parts])


def dense_units(q):
    g, u = (by_output(q[n][0]).reshape(-1, BLOCKS, P, P) for n in ("ffn_wg", "ffn_wu"))
    d = blocks_of(q["ffn_wd"][0]).reshape(-1, BLOCKS, P, P)
    seq = [g[0], u[0]]
    for f in range(FF_STEPS - 1):
        seq += [g[f + 1], d[f], u[f + 1]]
    return units_of(np.concatenate(seq + [d[-1]]))


def expert_units(q):
    def up(w):
        return w.reshape(EXPERTS, 2, 4, P, CHUNKS, CHUNK_F).transpose(0, 4, 1, 3, 2, 5).reshape(EXPERTS, CHUNKS, 2, P, UNIT)

    g, u = up(q["moe_wg"][0]), up(q["moe_wu"][0])
    d = q["moe_wd"][0].reshape(EXPERTS, CHUNKS, 2, 2, P, D).transpose(0, 1, 2, 4, 3, 5).reshape(EXPERTS, CHUNKS, 2, P, UNIT)
    out = np.empty((EXPERTS, ITEM_UNITS, P, UNIT), np.float32)
    out[:, 0:2], out[:, 2:4] = g[:, 0], u[:, 0]
    for c in range(CHUNKS - 1):
        at = 4 + 6 * c
        out[:, at:at + 2], out[:, at + 2:at + 4], out[:, at + 4:at + 6] = g[:, c + 1], u[:, c + 1], d[:, c]
    out[:, ITEM_UNITS - 2:] = d[:, CHUNKS - 1]
    return out.reshape(-1, P, UNIT)


def params(q, layer):
    def rows(v):
        return np.broadcast_to(v.reshape(1, -1), (P, v.size))

    w_dt = q["w_in"][layer][:, 3 * 512 + 3072:3 * 512 + 3072 + HEADS].reshape(KT, P, HEADS).transpose(1, 0, 2).reshape(P, -1)
    parts = [per_channel(q["norm1_g"][layer]), per_channel(q["norm2_g"][layer]), per_channel(q["sc_conv_w"][layer]),
             per_channel(q["ssm_conv_w"][layer]), per_channel(q["ssm_conv_b"][layer]), rows(q["ssm_dt_bias"][layer]),
             rows(q["ssm_a_log"][layer]), per_channel(np.repeat(q["ssm_d"][layer], HEAD_DIM)), per_channel(q["ssm_norm_g"][layer]),
             per_channel(q["gm_ln_g"][layer]), per_channel(q["gm_ln_b"][layer]), per_channel(q["pool_scale"][layer]), w_dt,
             q["gm_ws"][layer].transpose(2, 0, 1).reshape(P, -1), rows(q["gm_bias"][layer]),
             q["pool_map"][layer].transpose(1, 0, 2).reshape(P, -1)]
    return np.concatenate(parts, 1)


def constants(q):
    r = np.arange(P)
    f = lambda a: np.asarray(a, np.float32)
    inv = np.stack([1.0 / np.minimum(np.arange(1, 17), w) for w in (2, 4, 8, 16)])
    wide = lambda a: np.broadcast_to(f(a).reshape(1, -1), (P, np.size(a)))
    parts = [f(np.eye(P)), f(r[:, None] <= r[None, :]), f(np.ones((P, P))), f(r[:, None] > r[None, :]), wide(r), wide(inv),
             wide(np.arange(EXPERTS)), wide(np.repeat(np.arange(MAX_ITEMS), EXPERTS)), wide([EPS]), per_channel(q["final_g"]),
             q["router_w"][0].reshape(KT, P, EXPERTS).transpose(1, 0, 2).reshape(P, -1)]
    return np.concatenate(parts, 1)


def kernel(**inputs):
    import concourse.bacc as bacc
    from concourse.bass_utils import run_bass_kernel_spmd

    q = {k: np.asarray(v) for k, v in inputs.items()}
    arrays = {
        "x_in": q["x"][0].T.reshape(KT, P, SEQ).transpose(1, 0, 2),
        "par_in": np.stack([params(q, layer) for layer in range(DEPTH)]),
        "con_in": constants(q),
        "mix_w": np.stack([mixer_units(q, layer) for layer in range(DEPTH)]),
        "ff_w": dense_units(q),
        "moe_w": expert_units(q),
    }
    arrays = {k: np.ascontiguousarray(v) for k, v in arrays.items()}
    nc = bacc.Bacc("TRN2", target_bir_lowering=False, num_devices=1)
    aps = [nc.dram_tensor(k, a.shape, mybir.dt.from_np(a.dtype), kind="ExternalInput").ap() for k, a in arrays.items()]
    out = nc.dram_tensor("out", (P, KT, SEQ), mybir.dt.float32, kind="ExternalOutput").ap()
    trunk(nc, *aps, out)
    r = run_bass_kernel_spmd(nc, [arrays], core_ids=[0])
    return r.results[0]["out"].transpose(1, 0, 2).reshape(D, SEQ).T.reshape(1, SEQ, D)
```
